# Optimizing a Trainium2 kernel written in Bass

```python
import math
import jax
import jax.numpy as jnp
from jax import lax
import numpy as np
import jax, jax.numpy as jnp

D_MODEL = 2048
BATCH = 1
SEQ = 256
DEPTH = 1

NSA_HEADS = 8
NSA_KV_GROUPS = 2
NSA_HPG = NSA_HEADS // NSA_KV_GROUPS
NSA_HEAD_DIM = 128
NSA_WIDTH = NSA_HEADS * NSA_HEAD_DIM
NSA_KV_WIDTH = NSA_KV_GROUPS * NSA_HEAD_DIM
CMP_BLOCK = 32
CMP_STRIDE = 16
CMP_HIDDEN = 256
SEL_BLOCK = 64
SEL_TOP_N = 16
SEL_FORCE = 1000.0
WINDOW = 512
NSA_QBLOCK = 32

GDN_HEADS = 8
GDN_HEAD_DIM = 128
GDN_WIDTH = GDN_HEADS * GDN_HEAD_DIM
CONV_WIDTH = 4
GDN_CHUNK = 64

REL_BUCKETS = 32
REL_MAX_DIST = 128

D_FF = 4 * D_MODEL
NORM_EPS = 1e-6

IN_SPLIT_SIZES = (NSA_WIDTH, 6 * NSA_KV_WIDTH, 3 * NSA_HEADS, 3 * GDN_WIDTH, GDN_WIDTH, GDN_HEADS, GDN_HEADS, 2 * D_MODEL)
IN_COLS = NSA_WIDTH + 6 * NSA_KV_WIDTH + 3 * NSA_HEADS + 3 * GDN_WIDTH + GDN_WIDTH + GDN_HEADS + GDN_HEADS + 2 * D_MODEL


def rms_norm(x, w):
    xf = x.astype(jnp.float32)
    y = xf * lax.rsqrt(jnp.mean(xf * xf, axis=-1, keepdims=True) + NORM_EPS)
    return (y * w.astype(jnp.float32)).astype(x.dtype)

def masked_softmax(s, valid):
    s = jnp.where(valid, s.astype(jnp.float32), -jnp.inf)
    m = jnp.max(s, axis=-1, keepdims=True)
    m = jnp.where(jnp.isfinite(m), m, 0.0)
    e = jnp.exp(s - m)
    return e / jnp.maximum(jnp.sum(e, axis=-1, keepdims=True), 1e-30)

def t5_bucket(dist):
    n = jnp.maximum(dist, 0)
    exact = REL_BUCKETS // 2
    nf = jnp.maximum(n, 1).astype(jnp.float32)
    large = exact + (jnp.log(nf / exact) / math.log(REL_MAX_DIST / exact) * (REL_BUCKETS - exact)).astype(jnp.int32)
    large = jnp.minimum(large, REL_BUCKETS - 1)
    return jnp.where(n < exact, n, large)

def rel_bias_grid(rel_table, dist):
    tq, tk = dist.shape
    b = rel_table[t5_bucket(dist)]
    return b.reshape(tq, tk, NSA_KV_GROUPS, NSA_HPG).transpose(2, 3, 0, 1)

def compress_tokens(kv, pe, w1, w2):
    b, s, g, dh = kv.shape
    n_sub = CMP_BLOCK // CMP_STRIDE
    n_cmp = s // CMP_STRIDE - n_sub + 1
    r = kv.reshape(b, s // CMP_STRIDE, CMP_STRIDE, g, dh)
    blocks = jnp.concatenate([r[:, j:j + n_cmp] for j in range(n_sub)], axis=2)
    blocks = blocks + pe[None, None, :, None, :]
    flat = blocks.transpose(0, 1, 3, 2, 4).reshape(b, n_cmp, g, CMP_BLOCK * dh)
    return jax.nn.gelu(flat @ w1) @ w2

def nsa_attention(q, kv, gate_logits, rel_table, pe_k, pe_v, w1_k, w2_k, w1_v, w2_v):
    b, s, _ = q.shape
    g_, j_, dh = NSA_KV_GROUPS, NSA_HPG, NSA_HEAD_DIM
    scale = dh ** -0.5
    q = q.reshape(b, s, g_, j_, dh)
    k_c, v_c, k_s, v_s, k_w, v_w = [t.reshape(b, s, g_, dh) for t in jnp.split(kv, 6, axis=-1)]
    kc = compress_tokens(k_c, pe_k, w1_k, w2_k)
    vc = compress_tokens(v_c, pe_v, w1_v, w2_v)
    n_cmp = kc.shape[1]
    n_sel = s // SEL_BLOCK
    top_n = min(SEL_TOP_N, n_sel)
    ks = k_s.reshape(b, n_sel, SEL_BLOCK, g_, dh).transpose(0, 3, 1, 2, 4)
    vs = v_s.reshape(b, n_sel, SEL_BLOCK, g_, dh).transpose(0, 3, 1, 2, 4)
    pad = ((0, 0), (WINDOW, 0), (0, 0), (0, 0))
    kw = jnp.pad(k_w, pad)
    vw = jnp.pad(v_w, pad)
    gates = jax.nn.sigmoid(gate_logits).reshape(b, s, g_, j_, 3)

    cmp_end = jnp.arange(n_cmp) * CMP_STRIDE + (CMP_BLOCK - 1)
    c_start = np.arange(n_cmp) * CMP_STRIDE
    s_start = np.arange(n_sel) * SEL_BLOCK
    cover = jnp.asarray(((c_start[:, None] <= s_start[None, :] + SEL_BLOCK - 1)
                         & (c_start[:, None] + CMP_BLOCK - 1 >= s_start[None, :])).astype(np.float32))
    sel_ids = jnp.arange(n_sel)
    rel_flat = rel_table.reshape(REL_BUCKETS, g_, j_).transpose(1, 0, 2).reshape(g_ * REL_BUCKETS, j_)
    group_off = jnp.arange(g_)[None, :, None, None, None] * REL_BUCKETS
    gather_blocks = jax.vmap(jax.vmap(lambda blk, ix: blk[ix]))

    def query_block(i):
        q0 = i * NSA_QBLOCK
        t = q0 + jnp.arange(NSA_QBLOCK)
        qb = lax.dynamic_slice_in_dim(q, q0, NSA_QBLOCK, axis=1)
        gb = lax.dynamic_slice_in_dim(gates, q0, NSA_QBLOCK, axis=1)

        dist_c = t[:, None] - cmp_end[None, :]
        s_c = jnp.einsum('btgjd,bngd->bgjtn', qb, kc) * scale + rel_bias_grid(rel_table, dist_c)
        p_c = masked_softmax(s_c, dist_c >= 0)
        o_c = jnp.einsum('bgjtn,bngd->btgjd', p_c.astype(vc.dtype), vc)

        imp = jnp.einsum('bgjtn,nm->btgm', p_c, cover)
        cur = t // SEL_BLOCK
        forced = (sel_ids[None, :] == 0) | (sel_ids[None, :] == cur[:, None]) | (sel_ids[None, :] == cur[:, None] - 1)
        causal_blk = sel_ids[None, :] <= cur[:, None]
        score = jnp.where(causal_blk[:, None, :], imp + jnp.where(forced, SEL_FORCE, 0.0)[:, None, :], -jnp.inf)
        top_val, top_idx = lax.top_k(score, top_n)
        top_idx = top_idx.transpose(0, 2, 1, 3)
        k_sel = gather_blocks(ks, top_idx)
        v_sel = gather_blocks(vs, top_idx)
        key_pos = top_idx[..., None] * SEL_BLOCK + jnp.arange(SEL_BLOCK)
        dist_s = t[None, None, :, None, None] - key_pos
        valid_s = jnp.isfinite(top_val).transpose(0, 2, 1, 3)[..., None] & (dist_s >= 0)
        bias_s = rel_flat[group_off + t5_bucket(dist_s)]
        s_s = jnp.einsum('btgjd,bgtnrd->bgjtnr', qb, k_sel) * scale + jnp.moveaxis(bias_s, -1, 2)
        n_keys = top_n * SEL_BLOCK
        p_s = masked_softmax(s_s.reshape(b, g_, j_, NSA_QBLOCK, n_keys),
                             valid_s.reshape(b, g_, 1, NSA_QBLOCK, n_keys))
        o_s = jnp.einsum('bgjtnr,bgtnrd->btgjd', p_s.reshape(s_s.shape).astype(v_sel.dtype), v_sel)

        kwb = lax.dynamic_slice_in_dim(kw, q0, WINDOW + NSA_QBLOCK, axis=1)
        vwb = lax.dynamic_slice_in_dim(vw, q0, WINDOW + NSA_QBLOCK, axis=1)
        kpos = q0 - WINDOW + jnp.arange(WINDOW + NSA_QBLOCK)
        dist_w = t[:, None] - kpos[None, :]
        valid_w = (dist_w >= 0) & (dist_w < WINDOW) & (kpos[None, :] >= 0)
        s_w = jnp.einsum('btgjd,bsgd->bgjts', qb, kwb) * scale + rel_bias_grid(rel_table, dist_w)
        p_w = masked_softmax(s_w, valid_w)
        o_w = jnp.einsum('bgjts,bsgd->btgjd', p_w.astype(vwb.dtype), vwb)

        return gb[..., 0:1] * o_c + gb[..., 1:2] * o_s + gb[..., 2:3] * o_w

    out = lax.map(query_block, jnp.arange(s // NSA_QBLOCK))
    return out.transpose(1, 0, 2, 3, 4, 5).reshape(b, s, NSA_WIDTH)

def causal_depthwise_conv(x, w):
    return lax.conv_general_dilated(x, w[:, None, :], window_strides=(1,), padding=[(CONV_WIDTH - 1, 0)],
                                    dimension_numbers=('NWC', 'WIO', 'NWC'), feature_group_count=x.shape[-1])

def l2_normalize(x):
    return x * lax.rsqrt(jnp.sum(x * x, axis=-1, keepdims=True) + NORM_EPS)

def gated_delta_rule(q, k, v, g, beta):
    b, s, h, dk = q.shape
    dv = v.shape[-1]
    c = GDN_CHUNK
    n = s // c
    q = l2_normalize(q) * dk ** -0.5
    k = l2_normalize(k)

    def chunks(t):
        return jnp.moveaxis(t.reshape(b, n, c, h, *t.shape[3:]), 3, 1)

    q, k, v, g, beta = (chunks(t) for t in (q, k, v, g, beta))
    g = jnp.cumsum(g, axis=-1)
    kb = k * beta[..., None]
    vb = v * beta[..., None]
    tri = jnp.tril(jnp.ones((c, c), dtype=bool))
    strict = jnp.tril(jnp.ones((c, c), dtype=bool), -1)
    diff = g[..., :, None] - g[..., None, :]
    decay = jnp.where(tri, jnp.exp(jnp.where(tri, diff, 0.0)), 0.0)
    lower = jnp.where(strict, jnp.einsum('bhncd,bhnsd->bhncs', kb, k) * decay, 0.0)
    eye = jnp.eye(c, dtype=q.dtype)
    tinv = lax.linalg.triangular_solve(eye + lower, jnp.broadcast_to(eye, lower.shape),
                                       left_side=True, lower=True, unit_diagonal=True)
    u = tinv @ vb
    w = tinv @ (kb * jnp.exp(g)[..., None])
    qk = jnp.einsum('bhncd,bhnsd->bhncs', q, k) * decay

    def step(state, inp):
        qn, kn, un, wn, gn, qkn = inp
        v_new = un - wn @ state
        o = (qn * jnp.exp(gn)[..., None]) @ state + qkn @ v_new
        g_last = gn[..., -1:]
        state = state * jnp.exp(g_last)[..., None] + jnp.einsum('bhck,bhcv->bhkv', kn * jnp.exp(g_last - gn)[..., None], v_new)
        return state, o

    xs = tuple(jnp.moveaxis(t, 2, 0) for t in (q, k, u, w, g, qk))
    state0 = jnp.zeros((b, h, dk, dv), q.dtype)
    _, o = lax.scan(step, state0, xs)
    return o.transpose(1, 0, 3, 2, 4).reshape(b, s, h, dv)

def gated_deltanet(qkv, z, a, bl, conv_w, a_log, dt_bias, norm_w):
    b, s, _ = qkv.shape
    dtype = qkv.dtype
    qkv = jax.nn.silu(causal_depthwise_conv(qkv, conv_w)).astype(jnp.float32)
    q, k, v = jnp.split(qkv, 3, axis=-1)
    shape = (b, s, GDN_HEADS, GDN_HEAD_DIM)
    beta = jax.nn.sigmoid(bl.astype(jnp.float32))
    g = -jnp.exp(a_log.astype(jnp.float32)) * jax.nn.softplus(a.astype(jnp.float32) + dt_bias.astype(jnp.float32))
    o = gated_delta_rule(q.reshape(shape), k.reshape(shape), v.reshape(shape), g, beta)
    o = o * lax.rsqrt(jnp.mean(o * o, axis=-1, keepdims=True) + NORM_EPS) * norm_w.astype(jnp.float32)
    o = o * jax.nn.silu(z.astype(jnp.float32)).reshape(shape)
    return o.reshape(b, s, GDN_WIDTH).astype(dtype)

def hybrid_layer(x, rel_table, ln1_w, w_in, pe_k, pe_v, w1_k, w2_k, w1_v, w2_v, conv_w, a_log, dt_bias,
                 gdn_norm_w, w_pa, w_pb, w_o, ln2_w, w_up, w_down):
    h = rms_norm(x, ln1_w)
    proj = h @ w_in
    offs = [int(o) for o in np.cumsum(IN_SPLIT_SIZES)[:-1]]
    nsa_q, nsa_kv, nsa_gate, gdn_qkv, gdn_z, gdn_a, gdn_b, merge = jnp.split(proj, offs, axis=-1)
    o_a = nsa_attention(nsa_q, nsa_kv, nsa_gate, rel_table, pe_k, pe_v, w1_k, w2_k, w1_v, w2_v)
    o_b = gated_deltanet(gdn_qkv, gdn_z, gdn_a, gdn_b, conv_w, a_log, dt_bias, gdn_norm_w)
    g_a, g_b = jnp.split(jax.nn.sigmoid(merge), 2, axis=-1)
    x = x + (g_a * (o_a @ w_pa) + g_b * (o_b @ w_pb)) @ w_o
    h = rms_norm(x, ln2_w)
    return x + jnp.square(jax.nn.relu(h @ w_up)) @ w_down

def first_inputs(seed: int = 0) -> dict:
    key = jax.random.key(seed)
    k = jax.random.split(key, 21)
    f32 = jnp.float32
    L = DEPTH

    def normal(kk, shape, scale):
        return jax.random.normal(kk, shape, f32) * scale

    cmp_in = CMP_BLOCK * NSA_HEAD_DIM
    dt = jnp.exp(jax.random.uniform(k[12], (L, GDN_HEADS), f32, math.log(1e-3), math.log(1e-1)))
    return {
        'x': normal(k[0], (BATCH, SEQ, D_MODEL), 1.0),
        'rel_table': normal(k[1], (REL_BUCKETS, NSA_HEADS), 0.5),
        'ln1_w': 1.0 + normal(k[2], (L, D_MODEL), 0.02),
        'w_in': normal(k[3], (L, D_MODEL, IN_COLS), D_MODEL ** -0.5),
        'cmp_pe_k': normal(k[4], (L, CMP_BLOCK, NSA_HEAD_DIM), 0.1),
        'cmp_pe_v': normal(k[5], (L, CMP_BLOCK, NSA_HEAD_DIM), 0.1),
        'cmp_w1_k': normal(k[6], (L, cmp_in, CMP_HIDDEN), cmp_in ** -0.5),
        'cmp_w2_k': normal(k[7], (L, CMP_HIDDEN, NSA_HEAD_DIM), CMP_HIDDEN ** -0.5),
        'cmp_w1_v': normal(k[8], (L, cmp_in, CMP_HIDDEN), cmp_in ** -0.5),
        'cmp_w2_v': normal(k[9], (L, CMP_HIDDEN, NSA_HEAD_DIM), CMP_HIDDEN ** -0.5),
        'conv_w': normal(k[10], (L, CONV_WIDTH, 3 * GDN_WIDTH), CONV_WIDTH ** -0.5),
        'a_log': jnp.log(jax.random.uniform(k[11], (L, GDN_HEADS), f32, 1.0, 16.0)),
        'dt_bias': dt + jnp.log(-jnp.expm1(-dt)),
        'gdn_norm_w': 1.0 + normal(k[13], (L, GDN_HEAD_DIM), 0.02),
        'w_pa': normal(k[14], (L, NSA_WIDTH, D_MODEL), NSA_WIDTH ** -0.5),
        'w_pb': normal(k[15], (L, GDN_WIDTH, D_MODEL), GDN_WIDTH ** -0.5),
        'w_o': normal(k[16], (L, D_MODEL, D_MODEL), D_MODEL ** -0.5),
        'ln2_w': 1.0 + normal(k[17], (L, D_MODEL), 0.02),
        'w_up': normal(k[18], (L, D_MODEL, D_FF), D_MODEL ** -0.5),
        'w_down': normal(k[19], (L, D_FF, D_MODEL), D_FF ** -0.5),
        'ln_f_w': 1.0 + normal(k[20], (D_MODEL,), 0.02),
    }

def first_block(x, rel_table, ln1_w, w_in, cmp_pe_k, cmp_pe_v, cmp_w1_k, cmp_w2_k, cmp_w1_v, cmp_w2_v, conv_w,
              a_log, dt_bias, gdn_norm_w, w_pa, w_pb, w_o, ln2_w, w_up, w_down, ln_f_w):
    for l in range(DEPTH):
        x = hybrid_layer(x, rel_table, ln1_w[l], w_in[l], cmp_pe_k[l], cmp_pe_v[l], cmp_w1_k[l], cmp_w2_k[l],
                         cmp_w1_v[l], cmp_w2_v[l], conv_w[l], a_log[l], dt_bias[l], gdn_norm_w[l],
                         w_pa[l], w_pb[l], w_o[l], ln2_w[l], w_up[l], w_down[l])
    return rms_norm(x, ln_f_w)


DEPTH_2 = 2

N_MIXERS = 2
N_FOX_LAYERS = (DEPTH_2 + 1) // 2
N_RET_LAYERS = DEPTH_2 // 2

FOX_HEAD_DIM = 128
FOX_HEADS = D_MODEL // FOX_HEAD_DIM
FOX_WIDTH = FOX_HEADS * FOX_HEAD_DIM
FOX_BLOCK = 128
FOX_IN_COLS = 4 * FOX_WIDTH + FOX_HEADS

RET_QK_DIM = 256
RET_HEADS = D_MODEL // RET_QK_DIM
RET_V_DIM = 2 * RET_QK_DIM
RET_QK_WIDTH = RET_HEADS * RET_QK_DIM
RET_V_WIDTH = RET_HEADS * RET_V_DIM
RET_CHUNK = 128
RET_IN_COLS = 2 * RET_QK_WIDTH + 2 * RET_V_WIDTH
ROPE_BASE = 10000.0

LN_EPS = 1e-5
GN_EPS = 1e-6
QK_EPS = 1e-6
DEEPNORM_ALPHA = (2.0 * DEPTH_2) ** 0.25
DEEPNORM_BETA = (8.0 * DEPTH_2) ** -0.25


def layer_norm(x, g, b):
    xf = x.astype(jnp.float32)
    mu = jnp.mean(xf, axis=-1, keepdims=True)
    var = jnp.mean(jnp.square(xf - mu), axis=-1, keepdims=True)
    y = (xf - mu) * lax.rsqrt(var + LN_EPS) * g.astype(jnp.float32) + b.astype(jnp.float32)
    return y.astype(x.dtype)

def rms_norm_2(x, g):
    xf = x.astype(jnp.float32)
    y = xf * lax.rsqrt(jnp.mean(jnp.square(xf), axis=-1, keepdims=True) + QK_EPS) * g.astype(jnp.float32)
    return y.astype(x.dtype)

def group_norm_heads(x):
    mu = jnp.mean(x, axis=-1, keepdims=True)
    var = jnp.mean(jnp.square(x - mu), axis=-1, keepdims=True)
    return (x - mu) * lax.rsqrt(var + GN_EPS)

def rotary(t):
    S, d = t.shape[1], t.shape[-1]
    inv_freq = ROPE_BASE ** (-jnp.arange(0, d, 2, dtype=jnp.float32) / d)
    ang = jnp.arange(S, dtype=jnp.float32)[:, None] * inv_freq[None, :]
    cos = jnp.cos(ang)[None, :, None, :]
    sin = jnp.sin(ang)[None, :, None, :]
    t1, t2 = t[..., : d // 2], t[..., d // 2:]
    return jnp.concatenate([t1 * cos - t2 * sin, t1 * sin + t2 * cos], axis=-1)

def fox_branch(x, w_in, b_f, q_gain, k_gain, w_out):
    B, S, _ = x.shape
    proj = jnp.einsum('bsd,de->bse', x, w_in)
    q, k, v, gate, f_logit = jnp.split(
        proj, [FOX_WIDTH, 2 * FOX_WIDTH, 3 * FOX_WIDTH, 4 * FOX_WIDTH], axis=-1)

    def heads(t):
        return t.reshape(B, S, FOX_HEADS, FOX_HEAD_DIM).transpose(0, 2, 1, 3)

    q = rms_norm_2(heads(q), q_gain)
    k = rms_norm_2(heads(k), k_gain)
    v = heads(v)
    log_f = jax.nn.log_sigmoid((f_logit + b_f).astype(jnp.float32))
    c = jnp.cumsum(log_f, axis=1).transpose(0, 2, 1)

    n_blocks = S // FOX_BLOCK
    q_blocks = q.reshape(B, FOX_HEADS, n_blocks, FOX_BLOCK, FOX_HEAD_DIM).transpose(2, 0, 1, 3, 4)
    c_blocks = c.reshape(B, FOX_HEADS, n_blocks, FOX_BLOCK).transpose(2, 0, 1, 3)
    key_pos = jnp.arange(S)
    scale = FOX_HEAD_DIM ** -0.5

    def attend_block(args):
        qb, cb, blk = args
        s = jnp.einsum('bhqd,bhkd->bhqk', qb, k).astype(jnp.float32) * scale
        s = s + cb[..., :, None] - c[..., None, :]
        q_pos = blk * FOX_BLOCK + jnp.arange(FOX_BLOCK)
        s = jnp.where(key_pos[None, :] <= q_pos[:, None], s, -jnp.inf)
        p = jax.nn.softmax(s, axis=-1).astype(v.dtype)
        return jnp.einsum('bhqk,bhkd->bhqd', p, v)

    o = lax.map(attend_block, (q_blocks, c_blocks, jnp.arange(n_blocks)))
    o = o.transpose(1, 0, 3, 2, 4).reshape(B, S, FOX_WIDTH)
    y = o * jax.nn.silu(gate)
    return jnp.einsum('bse,ed->bsd', y, w_out)

def retention_branch(x, w_in, w_out):
    B, S, _ = x.shape
    proj = jnp.einsum('bsd,de->bse', x, w_in)
    q, k, v, gate = jnp.split(
        proj, [RET_QK_WIDTH, 2 * RET_QK_WIDTH, 2 * RET_QK_WIDTH + RET_V_WIDTH], axis=-1)
    q = rotary(q.reshape(B, S, RET_HEADS, RET_QK_DIM).astype(jnp.float32))
    k = rotary(k.reshape(B, S, RET_HEADS, RET_QK_DIM).astype(jnp.float32)) * (RET_QK_DIM ** -0.5)
    v = v.reshape(B, S, RET_HEADS, RET_V_DIM).astype(jnp.float32)

    log_gamma = jnp.log1p(-jnp.exp2(-5.0 - jnp.arange(RET_HEADS, dtype=jnp.float32)))
    pos = jnp.arange(RET_CHUNK, dtype=jnp.float32)
    diff = pos[:, None] - pos[None, :]
    intra_decay = jnp.where(diff >= 0,
                            jnp.exp(jnp.maximum(diff, 0.0)[None] * log_gamma[:, None, None]),
                            0.0)
    query_decay = jnp.exp((pos[None, :] + 1.0) * log_gamma[:, None])
    key_decay = jnp.exp((RET_CHUNK - 1.0 - pos[None, :]) * log_gamma[:, None])
    chunk_decay = jnp.exp(RET_CHUNK * log_gamma)

    n_chunks = S // RET_CHUNK

    def chunks(t):
        return t.reshape(B, n_chunks, RET_CHUNK, RET_HEADS, t.shape[-1]).transpose(1, 0, 3, 2, 4)

    def step(R, inp):
        qc, kc, vc = inp
        inner = jnp.einsum('bhqd,bhkd->bhqk', qc, kc) * intra_decay[None]
        o = (jnp.einsum('bhqk,bhkv->bhqv', inner, vc)
             + jnp.einsum('bhqd,bhdv->bhqv', qc, R) * query_decay[None, :, :, None])
        R = (R * chunk_decay[None, :, None, None]
             + jnp.einsum('bhkd,bhkv->bhdv', kc * key_decay[None, :, :, None], vc))
        return R, o

    R0 = jnp.zeros((B, RET_HEADS, RET_QK_DIM, RET_V_DIM), jnp.float32)
    _, o = lax.scan(step, R0, (chunks(q), chunks(k), chunks(v)))
    o = o.transpose(1, 0, 3, 2, 4)
    o = group_norm_heads(o).reshape(B, S, RET_V_WIDTH).astype(gate.dtype)
    y = o * jax.nn.silu(gate)
    return jnp.einsum('bse,ed->bsd', y, w_out)

def second_inputs(seed: int = 0) -> dict:
    key = jax.random.key(seed)
    ks = jax.random.split(key, 10)
    std_in = D_MODEL ** -0.5
    fox_col_scale = jnp.ones((FOX_IN_COLS,), jnp.float32).at[2 * FOX_WIDTH:3 * FOX_WIDTH].set(DEEPNORM_BETA)
    ret_col_scale = jnp.ones((RET_IN_COLS,), jnp.float32).at[
        2 * RET_QK_WIDTH:2 * RET_QK_WIDTH + RET_V_WIDTH].set(DEEPNORM_BETA)
    x = jax.random.normal(ks[0], (BATCH, SEQ, D_MODEL), jnp.float32)
    fox_w_in = jax.random.normal(ks[1], (N_FOX_LAYERS, D_MODEL, FOX_IN_COLS), jnp.float32) * std_in * fox_col_scale
    fox_b_f = 3.0 + 0.5 * jax.random.normal(ks[2], (N_FOX_LAYERS, FOX_HEADS), jnp.float32)
    fox_q_gain = 1.0 + 0.02 * jax.random.normal(ks[3], (N_FOX_LAYERS, FOX_HEAD_DIM), jnp.float32)
    fox_k_gain = 1.0 + 0.02 * jax.random.normal(ks[4], (N_FOX_LAYERS, FOX_HEAD_DIM), jnp.float32)
    fox_w_out = (jax.random.normal(ks[5], (N_FOX_LAYERS, FOX_WIDTH, D_MODEL), jnp.float32)
                 * (FOX_WIDTH ** -0.5) * DEEPNORM_BETA)
    ret_w_in = jax.random.normal(ks[6], (N_RET_LAYERS, D_MODEL, RET_IN_COLS), jnp.float32) * std_in * ret_col_scale
    ret_w_out = (jax.random.normal(ks[7], (N_RET_LAYERS, RET_V_WIDTH, D_MODEL), jnp.float32)
                 * (RET_V_WIDTH ** -0.5) * DEEPNORM_BETA)
    ln_gain = 1.0 + 0.02 * jax.random.normal(ks[8], (DEPTH_2, D_MODEL), jnp.float32)
    ln_bias = 0.02 * jax.random.normal(ks[9], (DEPTH_2, D_MODEL), jnp.float32)
    return {"x": x, "fox_w_in": fox_w_in, "fox_b_f": fox_b_f, "fox_q_gain": fox_q_gain,
            "fox_k_gain": fox_k_gain, "fox_w_out": fox_w_out, "ret_w_in": ret_w_in,
            "ret_w_out": ret_w_out, "ln_gain": ln_gain, "ln_bias": ln_bias}

def second_block(x, fox_w_in, fox_b_f, fox_q_gain, fox_k_gain, fox_w_out, ret_w_in, ret_w_out,
              ln_gain, ln_bias):
    h = x
    for i in range(DEPTH_2):
        j = i // N_MIXERS
        if i % N_MIXERS == 0:
            y = fox_branch(h, fox_w_in[j], fox_b_f[j], fox_q_gain[j], fox_k_gain[j], fox_w_out[j])
        else:
            y = retention_branch(h, ret_w_in[j], ret_w_out[j])
        h = layer_norm(DEEPNORM_ALPHA * h + y, ln_gain[i], ln_bias[i])
    return h


def setup_inputs(seed=0):
    out = dict(first_inputs(seed))
    for name, value in second_inputs(seed + 1).items():
        if name != "x":
            out[name + "_2"] = value
    return out


def reference(
    x, rel_table, ln1_w, w_in, cmp_pe_k, cmp_pe_v, cmp_w1_k, cmp_w2_k, cmp_w1_v, cmp_w2_v,
    conv_w, a_log, dt_bias, gdn_norm_w, w_pa, w_pb, w_o, ln2_w, w_up, w_down, ln_f_w,
    fox_w_in_2, fox_b_f_2, fox_q_gain_2, fox_k_gain_2, fox_w_out_2, ret_w_in_2, ret_w_out_2,
    ln_gain_2, ln_bias_2,
):
    x = first_block(
        x, rel_table, ln1_w, w_in, cmp_pe_k, cmp_pe_v, cmp_w1_k, cmp_w2_k, cmp_w1_v, cmp_w2_v,
        conv_w, a_log, dt_bias, gdn_norm_w, w_pa, w_pb, w_o, ln2_w, w_up, w_down, ln_f_w,
    )
    return second_block(
        x, fox_w_in_2, fox_b_f_2, fox_q_gain_2, fox_k_gain_2, fox_w_out_2, ret_w_in_2,
        ret_w_out_2, ln_gain_2, ln_bias_2,
    )


_drawn_inputs = setup_inputs


def setup_inputs(seed=0):
    import zlib

    import numpy as np

    out = dict(_drawn_inputs(seed))
    spreads = {}
    factors = {'ln1_w': 4.356,
     'cmp_pe_k': 8.0,
     'cmp_pe_v': 10.996,
     'gdn_norm_w': 7.69,
     'ln2_w': 3.058,
     'ln_f_w': 2.679,
     'fox_b_f_2': 49.728,
     'fox_q_gain_2': 8.0,
     'fox_k_gain_2': 8.0}
    for name, (base, spread) in spreads.items():
        noise = np.random.default_rng([zlib.crc32(name.encode()), seed]).standard_normal(out[name].shape)
        drawn = base * np.exp(spread * noise) if base else spread * noise
        out[name] = jnp.asarray(drawn.astype(out[name].dtype))
    for name, factor in factors.items():
        out[name] = (out[name] * factor).astype(out[name].dtype)
    return out
```

```python
import math
from contextlib import ExitStack

import numpy as np

import concourse.bass as bass
from concourse import mybir

F32 = mybir.dt.float32
F32R = mybir.dt.float32r
ALU = mybir.AluOpType
ACT = mybir.ActivationFunctionType
AX = mybir.AxisListType

P = 128
S = 256
NT = S // P
D = 2048
KT = D // P
NB = 512
GPJ = 8
CPJ = 4
HD = 128
NH = 8
HG = 4
CMP_BLOCK, CMP_STRIDE = 32, 16
NCMP = S // CMP_STRIDE - 1
NC0 = (P - CMP_BLOCK) // CMP_STRIDE + 1
NKV = 2
CMP_HIDDEN = 256
BUCKETS, MAX_DIST = 32, 128
CHUNK = 64
LEVELS = 6
FOX_HEADS = 16
RET_HEADS, RET_QK, RET_V = 8, 256, 512
NEG = -1e30
NORM_EPS, LN_EPS = 1e-6, 1e-5
ALPHA = (2.0 * 2) ** 0.25
SEG = P + S
SEGC = SEG + NC0 + NCMP
ATT_SCALE = HD ** -0.5

C_NSA = 0
C_GATE = NH * HD + 6 * NKV * HD
C_GDN = C_GATE + 3 * NH
C_AB = C_GDN + 4 * NH * HD
C_MERGE = C_AB + 2 * NH

J_NSA = 0
J_CMP = J_NSA + (NH * HD + 6 * NKV * HD) // NB
J_GDN = J_CMP + 2
J_MERGE = J_GDN + 8
J_PAB = J_MERGE + 8
J_WO = J_PAB + 4
J_MLP = J_WO + 4
J_FOX = J_MLP + 32
J_FOXO = J_FOX + 16
J_RET = J_FOXO + 4
J_END = J_RET + 32


class Lin:

    def __init__(self, c, terms=()):
        self.c, self.terms = c, tuple(terms)

    def __add__(self, k):
        if isinstance(k, Lin):
            return Lin(self.c + k.c, self.terms + k.terms)
        return Lin(self.c + k, self.terms)

    def __sub__(self, k):
        return Lin(self.c - k, self.terms)

    def __mul__(self, k):
        return Lin(self.c * k, [(a * k, v) for a, v in self.terms])

    def half(self):
        assert all(a % 2 == 0 for a, _ in self.terms)
        return Lin(self.c // 2, [(a // 2, v) for a, v in self.terms])

    def value(self):
        v = self.c
        for a, r in self.terms:
            v = r * a + v
        return v


def lin(i):
    return i if isinstance(i, Lin) else Lin(0, [(1, i)]) if not isinstance(i, int) else Lin(i)


def wait(eng, sem, n):
    n = lin(n)
    assert n.c > 0 or not n.terms, "a wait against a register that is 0 in the first round"
    if n.c > 0:
        eng.wait_ge(sem, n.value())


class Chain:

    def __init__(self, eng, sem, start=0):
        self.eng, self.sem, self.start, self.k = eng, sem, lin(start), 0

    def link(self, ins):
        ins.then_inc(self.sem, 1)
        self.k += 1
        wait(self.eng, self.sem, self.start + self.k)

    def end(self, k):
        assert self.k == k, f"the chain has {self.k} steps, not {k}"


K_GDN_DVE, K_FOX_DVE, K_RET_DVE = 16, 6, 10


def build(nc, x, rel_table, ln1_w, w_in, pe_k, pe_v, w1_k, w2_k, w1_v, w2_v, conv_w, a_log, dt_bias,
          gdn_norm_w, w_pa, w_pb, w_o, ln2_w, w_up, w_down, ln_f_w, fox_w_in, fox_b_f, fox_q_gain,
          fox_k_gain, fox_w_out, ret_w_in, ret_w_out, ln_gain, ln_bias,
          c_onehot, c_masks, c_causal, c_rope, c_intra, c_decay, out):
    ctx = ExitStack()
    with ctx:
        def sb(name, shape, dt=F32):
            return ctx.enter_context(nc.sbuf_tensor(name, shape, dt))

        def sem(name):
            return ctx.enter_context(nc.semaphore(name))

        raw = sb("raw", [P, CPJ, 4, NB])
        w_hi = sb("w_hi", [P, 4, 2, NB], F32R)
        w_lo = sb("w_lo", [P, 4, 2, NB], F32R)
        lt_a = [sb("lt_a_hi", [P, KT, S], F32R), sb("lt_a_lo", [P, KT, S], F32R)]
        lt_b = [sb("lt_b_hi", [P, KT, S], F32R), sb("lt_b_lo", [P, KT, S], F32R)]
        res = sb("res", [P, NT, D])
        ARENA = 14592
        arena = sb("arena", [P, ARENA])
        ident = sb("ident", [P, P])
        w2 = sb("w2", [P, 2, 2, HD])
        cwt = sb("cwt", [P, 4 * 24])
        pet = sb("pet", [P, 2, CMP_BLOCK])
        gnorm = sb("gnorm", [P, HD])
        fgain = sb("fgain", [P, 2, HD])
        gates = sb("gates", [P, NT, 3 * NH])
        sm = sb("sm", [P, 320])

        def at(off, *shape):
            n = math.prod(shape)
            assert off + n <= ARENA, (off, shape)
            v = arena[:, off:off + n]
            if len(shape) == 2:
                v = v.rearrange("p (a b) -> p a b", b=shape[1])
            if len(shape) == 3:
                v = v.rearrange("p (a b c) -> p a b c", b=shape[1], c=shape[2])
            if len(shape) == 4:
                v = v.rearrange("p (a b c d) -> p a b c d", b=shape[1], c=shape[2], d=shape[3])
            return v

        used = [0]

        def small(*shape):
            n = math.prod(shape)
            v = sm[:, used[0]:used[0] + n]
            used[0] += n
            assert used[0] <= 320
            if len(shape) == 2:
                v = v.rearrange("p (a b) -> p a b", b=shape[1])
            if len(shape) == 3:
                v = v.rearrange("p (a b c) -> p a b c", b=shape[1], c=shape[2])
            return v

        mhalf = small(32)
        ssum = small(NT)
        rstd = small(NT)
        a_row = small(NH)
        dt_row = small(NH)
        bf_row = small(FOX_HEADS)
        lnst = small(NT, 4, 6)
        lnmv = small(NT, 2)
        lnr = small(NT)

        acc = [[ctx.enter_context(nc.psum_tensor(f"acc{a}{t}", [P, NB], F32)) for t in range(NT)]
               for a in range(2)]
        mx = ctx.enter_context(nc.psum_tensor("mx", [P, 4, NB], F32))

        raw_loaded = [sem(f"raw_loaded{i}") for i in range(CPJ)]
        hi_ready = sem("hi_ready")
        lo_ready = sem("lo_ready")
        granules_done = sem("granules_done")
        acc_taken = [sem("acc_taken0"), sem("acc_taken1")]
        lt_turned = sem("lt_turned")
        lt_hi_ready = sem("lt_hi_ready")
        lt_lo_ready = sem("lt_lo_ready")
        S_ = {}

        def sg(name):
            if name not in S_:
                S_[name] = sem(name)
            return S_[name]

        names = ("const_loaded x_loaded w_loaded ident_ready row_loaded toep_loaded toep_stored store_done "
                 "sq_done ms_ready rstd_ready h_ready").split()
        for n in names:
            sg(n)

        block = ctx.enter_context(nc.Block())

        def load_job(sp, J, src, rows=512, chunks=CPJ):
            J = lin(J)
            for q in range(chunks):
                wait(sp, lo_ready, J * GPJ + 2 * q + 2 - GPJ)
                w = src(q)
                sp.dma_start(raw[:, q, :, :].rearrange("p a b -> p (a b)").rearrange(
                    "p (j n) -> p j n", j=rows // P), w.rearrange("(j p) n -> p j n", p=P)) \
                    .then_inc(raw_loaded[q], 16)

        def block_of(w, row0, col):
            def src(q):
                r = row0 + q * 512 if isinstance(row0, int) else row0 + q * 512
                rs = slice(r, r + 512) if isinstance(r, int) else bass.ds(r, 512)
                cs = slice(col, col + NB) if isinstance(col, int) else bass.ds(col, NB)
                return w[rs, cs]
            return src

        def split_hi(act, J, r0, r1):
            J = lin(J)
            for r in range(r0, r1):
                slot, half = (r % GPJ) // 2, r % 2
                if half == 0:
                    wait(act, raw_loaded[slot], (J + (1 + r // GPJ)) * 16)
                wait(act, granules_done, J * GPJ + r - 3)
                nc.scalar.activation(w_hi[:, r % 4], raw[:, slot, 2 * half:2 * half + 2, :],
                                     ACT.Copy).then_inc(hi_ready, 1)

        def split_lo(dve, J, r0, r1):
            J = lin(J)
            for r in range(r0, r1):
                slot, half = (r % GPJ) // 2, r % 2
                wait(dve, hi_ready, J * GPJ + r + 1)
                nc.vector.tensor_tensor(w_lo[:, r % 4], raw[:, slot, 2 * half:2 * half + 2, :],
                                        w_hi[:, r % 4].bitcast(F32), ALU.subtract) \
                    .then_inc(lo_ready, 1)

        def ahead(J):
            return GPJ + 4

        def multiply(pe, J, lt, par, hook=None, free=None):
            J = lin(J)
            assert J.c % 2 == par
            if free is None:
                wait(pe, acc_taken[par], J.half())
            else:
                wait(pe, *free)
            for r in range(GPJ):
                if hook:
                    hook(r)
                wait(pe, lo_ready, J * GPJ + r + 1)
                for k in range(2):
                    kt = 2 * r + k
                    hi, lo = w_hi[:, r % 4, k, :], w_lo[:, r % 4, k, :]
                    for t in range(NT):
                        a_hi = lt[0][:, kt, t * P:(t + 1) * P]
                        a_lo = lt[1][:, kt, t * P:(t + 1) * P]
                        o = acc[par][t][:, :]
                        nc.tensor.matmul(o, a_hi, hi, start=(kt == 0), stop=False)
                        nc.tensor.matmul(o, a_hi, lo, start=False, stop=False)
                        last = nc.tensor.matmul(o, a_lo, hi, start=False, stop=(kt == KT - 1))
                last.then_inc(granules_done, 1)

        def take(eng, J, par, ops):
            wait(eng, granules_done, lin(J) * GPJ + GPJ)
            for t in range(NT):
                last = ops(t)
            last.then_inc(acc_taken[par], 1)

        def turn(pe, B, src, n):
            B = lin(B)
            wait(pe, lt_lo_ready, B)
            for b in range(n):
                if b >= 4:
                    wait(pe, lt_lo_ready, B + b - 3)
                for c in range(2):
                    for t in range(NT):
                        last = nc.tensor.transpose(mx[:, b % 4, (2 * c + t) * P:(2 * c + t + 1) * P],
                                                   src(2 * b + c, t), ident[:, :])
                last.then_inc(lt_turned, 1)

        def turn_hi(act, B, dst, n):
            B = lin(B)
            for b in range(n):
                wait(act, lt_turned, B + b + 1)
                nc.scalar.activation(dst(b)[0], mx[:, b % 4, :].rearrange("p (c s) -> p c s", s=S),
                                     ACT.Copy).then_inc(lt_hi_ready, 1)

        def turn_lo(dve, B, dst, n):
            B = lin(B)
            for b in range(n):
                wait(dve, lt_hi_ready, B + b + 1)
                hi, lo = dst(b)
                nc.vector.tensor_tensor(lo, mx[:, b % 4, :].rearrange("p (c s) -> p c s", s=S),
                                        hi.bitcast(F32), ALU.subtract).then_inc(lt_lo_ready, 1)

        def whole(lt):
            return lambda b: (lt[0][:, 2 * b:2 * b + 2, :], lt[1][:, 2 * b:2 * b + 2, :])

        def part(lt, kt):
            return lambda b: (lt[0][:, bass.ds(kt + 2 * b, 2), :], lt[1][:, bass.ds(kt + 2 * b, 2), :])

        B_LN1, B_OA = 0, 8
        B_OB = B_OA + 4
        B_Y = B_OB + 4
        B_LN2 = B_Y + 8
        B_U = B_LN2 + 8
        B_LNF = B_U + 32
        B_FO = B_LNF + 8
        B_LNG = B_FO + 8
        B_RO = B_LNG + 8

        h_nat = at(0, NT, D)
        w_row = at(NT * D, 2, D)

        def rms_act(act, k):
            for t in range(NT):
                last = nc.scalar.activation(h_nat[:, t, :], res[:, t, :], ACT.Square,
                                            accum_out=ssum[:, t:t + 1])
            last.then_inc(sg("sq_done"), 1)

        def rms_dve(dve, k, dst):
            dve.wait_ge(sg("sq_done"), k + 1)
            nc.vector.tensor_scalar(ssum, ssum, 1.0 / D, NORM_EPS, ALU.mult, ALU.add) \
                .then_inc(sg("ms_ready"), 1)
            dve.wait_ge(sg("rstd_ready"), k + 1)
            dve.wait_ge(sg("row_loaded"), 16 * k) if k else dve.wait_ge(sg("first_row_loaded"), 16)
            for t in range(NT):
                last = nc.vector.scalar_tensor_tensor(dst[:, t, :], res[:, t, :], rstd[:, t:t + 1],
                                                      w_row[:, 0, :], ALU.mult, ALU.mult)
            last.then_inc(sg("h_ready"), 1)

        def root_pool(pool, src_ready, n, base, dst, w, done):
            wait(pool, src_ready, n)
            nc.gpsimd.tensor_tensor(dst, base, mhalf[:, 0:w], ALU.pow).then_inc(done, 1)

        nat = at(0, 5, NT, NB)
        T = at(5120, 16, S)
        bm = at(9216, NH, SEGC)
        sc = at(0, HG, SEG)
        scc = at(1536, HG, NC0 + NCMP)
        pt = at(12464, HG, SEG)
        o_nat = at(5120 + 8 * S, NT, HG, HD)
        blk = at(2 * 1024, 960)
        wsmall = at(12464, KT, 40)
        onehot = at(9216, 384)
        tabl = at(9216 + 384, NH)
        distb = at(9216 + 400, 384)
        pe_nat = at(14000, 2, HD)
        cw_nat = at(14000 + 256, HD)
        cmp_hid = at(2048 + 0, 2, CMP_HIDDEN)
        cmp_hT = at(2048 + 512, 4, NKV * NCMP)
        kcT = at(2048 + 632, NKV * NCMP)
        vc = at(2048 + 662, NKV, HD)
        cb = [lt.rearrange("p a b -> p (a b)")[:, 0:2 * 960].rearrange("p (v n) -> p v n", v=2)
              for lt in (lt_b[0][:, :, :], lt_b[1][:, :, :])]
        mask0 = small(NC0)
        rowmax = small(4, HG)
        esum = small(4, HG)
        coef = small(3, NT, HG)
        att = {n: sg(n) for n in ("scores_ready scores_taken rowmax_ready exp_done probs_turned probs_copied "
                                  "att_out_ready att_out_taken").split()}

        def unit_pe(pe, u, sc, pt, q, k, v):
            u = lin(u)
            wait(pe, att["att_out_taken"], u)
            for j in range(HG):
                nc.tensor.matmul(mx[:, j, 0:P], q(j)[:, 0:P], k(j)[:, 0:P], start=True, stop=True)
                last = nc.tensor.matmul(mx[:, j, P:SEG], q(j)[:, P:S], k(j), start=True, stop=True)
            last.then_inc(att["scores_ready"], 1)
            wait(pe, att["exp_done"], u + 1)
            for j in range(HG):
                for b in range(3):
                    last = nc.tensor.transpose(mx[:, j, b * P:(b + 1) * P], sc[:, j, b * P:(b + 1) * P],
                                               ident[:, :])
            last.then_inc(att["probs_turned"], 1)
            wait(pe, att["probs_copied"], u + 1)
            for j in range(HG):
                nc.tensor.matmul(mx[:, 0, j * HD:(j + 1) * HD], pt[:, j, 0:P], v(j, 0), start=True, stop=True)
                nc.tensor.matmul(mx[:, 1, j * HD:(j + 1) * HD], pt[:, j, P:S], v(j, 0), start=True, stop=False)
                last = nc.tensor.matmul(mx[:, 1, j * HD:(j + 1) * HD], pt[:, j, S:SEG], v(j, 1),
                                        start=False, stop=True)
            last.then_inc(att["att_out_ready"], 1)

        def unit_act(act, u, sc, pt):
            u = lin(u)
            wait(act, att["rowmax_ready"], u + 1)
            for j in range(HG):
                for t, (a, b) in enumerate(((0, P), (P, SEG))):
                    last = nc.scalar.activation(sc[:, j, a:b], sc[:, j, a:b], ACT.Exp,
                                                bias=rowmax[:, t, j:j + 1], accum_out=esum[:, t, j:j + 1])
            last.then_inc(att["exp_done"], 1)
            wait(act, att["probs_turned"], u + 1)
            nc.scalar.activation(pt[:, :, :], mx[:, :, 0:SEG], ACT.Copy).then_inc(att["probs_copied"], 1)

        def unit_dve(dve, u, ch, sc, o_nat, bias, gate, first):
            u = lin(u)
            wait(dve, att["scores_ready"], u + 1)
            ch.link(nc.vector.scalar_tensor_tensor(sc[:, :, :], mx[:, :, 0:SEG], ATT_SCALE, bias,
                                                   ALU.mult, ALU.add))
            nc.vector.tensor_reduce(rowmax[:, 0, :], sc[:, :, 0:P], AX.X, ALU.max, negate=True)
            nc.vector.tensor_reduce(rowmax[:, 1, :], sc[:, :, P:SEG], AX.X, ALU.max, negate=True) \
                .then_inc(att["rowmax_ready"], 1)
            wait(dve, att["exp_done"], u + 1)
            ch.link(nc.vector.tensor_scalar(coef[:, 0], esum[:, 0:2], 1e-30, None, ALU.max))
            ch.link(nc.vector.reciprocal(coef[:, 1], coef[:, 0]))
            if gate is None:
                gate = coef[:, 1]
            else:
                ch.link(nc.vector.tensor_tensor(coef[:, 2], coef[:, 1], gate, ALU.mult))
                gate = coef[:, 2]
            wait(dve, att["att_out_ready"], u + 1)
            for t in range(NT):
                for j in range(HG):
                    o = o_nat[:, t, j, :]
                    ps = mx[:, t, j * HD:(j + 1) * HD]
                    c = gate[:, t, j:j + 1]
                    if first:
                        last = nc.vector.tensor_scalar(o, ps, c, None, ALU.mult)
                    else:
                        last = nc.vector.scalar_tensor_tensor(o, ps, c, o, ALU.mult, ALU.add)
            last.then_inc(att["att_out_taken"], 1)

        g_nat = at(0, 4, NT, NB)
        g_ct = at(4096, 12, 260)
        g_cv = at(7216, 12, S)
        g_rn = at(10288, NT, 12, HD)
        g_mask = at(13360, LEVELS + 3, P)
        M_STRICT, M_TRI, M_ONES = LEVELS, LEVELS + 1, LEVELS + 2
        g_sq = at(4096, NT, 8, HD)
        g_vb, g_kbeg, g_kdec = (at(i * 1024, NT, HG, HD) for i in range(3))
        g_qg = at(4096 + 2048, NT, HG, HD)
        g_qT, g_kT, g_qgT = (at(7216 + i * 1024, HG, S) for i in range(3))
        g_dec, g_qkT, g_A = (at(10288 + i * 1024, HG * NT, P) for i in range(3))
        g_X, g_Y, g_P1 = (at(4096 + i * 1024, HG * NT, P) for i in range(3))
        g_U = g_dec
        g_wT = g_A
        g_o = at(4096, NT, HG, HD)
        g_S = at(4096 + 2048, HG, HD)
        g_V = at(4096 + 2048 + 512, HG, HD)
        G_G, G_BETA, G_CUM, G_E, G_KD, G_BEG = range(6)
        tok = sb("tok", [P, 6, NT, NH])
        tg = sb("tg", [P, 6, NT, HG])
        cwg = sb("cwg", [P, 12, HG])
        gss = small(NT, 8)
        grs = small(NT, 8)
        egl = small(HG * NT, 2)
        gt = [small(NT, NH) for _ in range(3)]

        f_nat = at(0, 4, NT, NB)
        f_T = at(4096, 8, S)
        f_sc = at(6144, HG, SEG)
        f_pt = at(7680, HG, SEG)
        f_o = at(9216, NT, HG, HD)
        f_bias = at(10240, HG, SEG)
        f_causal = at(11776, SEG)
        f_logf = at(12160, NT, FOX_HEADS)
        f_lg = at(12192, NT, HG)
        f_ones = at(12208, P)
        f_t = [at(12336 + 32 * i, NT, FOX_HEADS) for i in range(3)]
        f_w = at(12448, KT, FOX_HEADS)
        f_ss = at(12704, NT, 8)
        f_rs = at(12720, NT, 8)
        tri = at(12736, P)

        mg = at(0, 8, NT, NB)
        y_nat = at(8192, NT, D)
        y_tmp = at(12288, NT, NB)
        relu = at(0, NT, NB)
        u_nat = at(1024, 2, NT, NB)

        r_nat = at(0, 6, NT, NB)
        r_T = at(6144, 8, S)
        r_qdT = at(8192, HG, P)
        r_kd = at(8704, 2, RET_QK)
        r_in = at(9216, 4, P)
        r_R = at(9728, 4, RET_V)
        r_D = at(11776, 2, P)
        r_cs = at(12032, 2, NT, P)
        r_tmp = at(12544, 4, NT * 2 * P)
        r_dec = small(2, RET_HEADS)
        r_st = small(NT, 6)
        r_mv = small(NT, 2)
        r_rs = small(NT)

        bias_dram = nc.dram_tensor("bias_by_distance", [NH, P, 384], F32).ap()

        def bcast(ap, n):
            return bass.AP(tensor=ap.tensor, offset=ap.offset, ap=[*ap.ap, [0, n]])

        def heads_bcast(ap, n):
            return bass.AP(tensor=ap.tensor, offset=ap.offset, ap=[ap.ap[0], [0, n], *ap.ap[1:]])

        N_CONST = 15
        NSA_ORDER = [4, 5, 0, 1, 2, 3, 6, 7]
        NSA_TILES = [(i // 4, i % 4) for i in range(8)] + [(2, 0), (2, 1), (2, 2), (2, 3), (3, 0), (3, 1),
                                                          (4, 0), (4, 1)]
        small_ps = mx[:, 0, 0:128].rearrange("p (t n) -> p t n", t=NT)

        @block.sync
        def _(sp):
            def fori(n):
                return sp.Fori(0, n)
            sp.dma_start(res[:, :, :], x.rearrange("(t p) d -> p t d", p=P)).then_inc(sg("x_loaded"), 16)
            sp.dma_start(w_row[:, 0, :], ln1_w.partition_broadcast(P)).then_inc(sg("first_row_loaded"), 16)
            load_job(sp, 0, block_of(w_in, 0, C_NSA))
            with fori(2) as i:
                for c in range(2):
                    load_job(sp, Lin(1 + c, [(2, i)]), block_of(w_in, 0, i * (2 * NB) + (C_NSA + (1 + c) * NB)))
            for c, w in enumerate((w1_k, w1_v)):
                load_job(sp, J_CMP + c, lambda q, w=w: w[q * 1024:(q + 1) * 1024, :], rows=1024)
            with fori(2) as g:
                for kind in range(4):
                    load_job(sp, Lin(J_GDN + kind, [(4, g)]),
                             block_of(w_in, 0, g * NB + (C_GDN + kind * NH * HD)))
            with fori(4) as i:
                for c in range(2):
                    load_job(sp, Lin(J_MERGE + c, [(2, i)]), block_of(w_in, 0, i * (2 * NB) + (C_MERGE + c * NB)))
            with fori(2) as i:
                for c in range(2):
                    col = i * (2 * NB) + c * NB
                    load_job(sp, Lin(J_PAB + c, [(2, i)]),
                             lambda q, col=col: (w_pa, w_pb)[q // 2][(q % 2) * 512:(q % 2 + 1) * 512,
                                                                    bass.ds(col, NB)])
            with fori(2) as i:
                for c in range(2):
                    load_job(sp, Lin(J_WO + c, [(2, i)]), block_of(w_o, 0, i * (2 * NB) + c * NB))
            with fori(4) as g:
                for c in range(4):
                    load_job(sp, Lin(J_MLP + c, [(8, g)]), block_of(w_up, 0, g * D + c * NB))
                for c in range(4):
                    load_job(sp, Lin(J_MLP + 4 + c, [(8, g)]), block_of(w_down, g * D, c * NB))
            with fori(4) as g:
                for kind in range(4):
                    load_job(sp, Lin(J_FOX + kind, [(4, g)]), block_of(fox_w_in, 0, g * NB + kind * D))
            with fori(2) as i:
                for c in range(2):
                    load_job(sp, Lin(J_FOXO + c, [(2, i)]), block_of(fox_w_out, 0, i * (2 * NB) + c * NB))
            with fori(2) as h:
                with fori(2) as p:
                    J = Lin(J_RET, [(16, h), (6, p)])
                    load_job(sp, J, block_of(ret_w_in, 0, h * 1024 + p * NB))
                    load_job(sp, J + 1, block_of(ret_w_in, 0, h * 1024 + p * NB + D))
                    for c in range(4):
                        load_job(sp, J + 2 + c, block_of(ret_w_in, 0, h * 2048 + p * 1024
                                                         + (2 * D + (c // 2) * 2 * D + (c % 2) * NB)))
                for c in range(4):
                    load_job(sp, Lin(J_RET + 12 + c, [(16, h)]), block_of(ret_w_out, h * D, c * NB))
            load_job(sp, J_END, block_of(ret_w_out, 0, 0), chunks=2)
            sp.wait_ge(sg("ln_done"), 2)
            sp.dma_start(out.rearrange("(t p) d -> p t d", p=P), res[:, :, :]).then_inc(sg("store_done"), 16)
            sp.wait_ge(sg("store_done"), 16)

        @block.gpsimd
        def _(pool):
            def fori(n):
                return pool.Fori(0, n)
            ch = Chain(pool, sg("pool_step"))

            def load(dst, src, s, n=None):
                pool.dma_start(dst, src).then_inc(sg(s), 16)

            ch.link(nc.gpsimd.memset(ident[:, :], 0.0))
            nc.gpsimd.affine_select(out=ident[:, :], in_=ident[:, :], compare_op=ALU.not_equal, fill=1.0,
                                    base=0, pattern=[[-1, P]], channel_multiplier=1) \
                .then_inc(sg("ident_ready"), 1)
            ch.link(nc.gpsimd.memset(mhalf, -0.5))
            ch.link(nc.gpsimd.memset(mask0, 1.0))
            ch.link(nc.gpsimd.affine_select(out=mask0, in_=mask0, compare_op=ALU.is_ge, fill=0.0,
                                            base=-(CMP_BLOCK - 1), pattern=[[-CMP_STRIDE, NC0]],
                                            channel_multiplier=1))
            root_pool(pool, sg("ms_ready"), 1, ssum, rstd, NT, sg("rstd_ready"))

            pool.wait_ge(sg("prep_taken"), 1)
            src = distb[0:NH, :]
            pool.dma_start(bias_dram, bass.AP(tensor=src.tensor, offset=src.offset,
                                              ap=[src.ap[0], [0, P], src.ap[1]])).then_inc(sg("toep_stored"), 16)
            pool.wait_ge(sg("toep_stored"), 16)
            for a, b, off in ((0, P, 2 * P - 1), (P, SEG, P - 1)):
                src = bass.AP(tensor=bias_dram.tensor, offset=off, ap=[[384 - 1, P], [384 * P, NH], [1, b - a]])
                pool.dma_start(bm[:, :, a:b], src).then_inc(sg("toep_loaded"), 16)
            pool.wait_ge(sg("toep_loaded"), 32)
            nc.gpsimd.affine_select(out=bm[:, :, 0:P], in_=bm[:, :, 0:P], compare_op=ALU.is_ge, fill=NEG,
                                    base=0, pattern=[[0, NH], [-1, P]], channel_multiplier=1) \
                .then_inc(sg("bias_masked"), 1)
            nc.gpsimd.affine_select(out=bm[:, :, P:SEG], in_=bm[:, :, P:SEG], compare_op=ALU.is_ge, fill=NEG,
                                    base=P, pattern=[[0, NH], [-1, S]], channel_multiplier=1) \
                .then_inc(sg("bias_masked"), 1)
            pool.wait_ge(lt_lo_ready, B_OB)
            load(g_mask[:, :, :], c_masks[0:LEVELS + 3].rearrange("m p c -> p m c"), "mask_loaded")
            with fori(2) as g:
                root_pool(pool, sg("gss_ready"), Lin(1, [(2, g)]),
                          gss.rearrange("p a b -> p (a b)"), grs.rearrange("p a b -> p (a b)"), 16,
                          sg("grs_ready"))
                root_pool(pool, sg("gss_ready"), Lin(2, [(2, g)]),
                          gss.rearrange("p a b -> p (a b)")[:, 0:8],
                          grs.rearrange("p a b -> p (a b)")[:, 0:8], 8, sg("grs_ready"))
            pool.wait_ge(sg("y_ready"), 1)
            load(w_row[:, 0, :], ln2_w.partition_broadcast(P), "row_loaded")
            root_pool(pool, sg("ms_ready"), 2, ssum, rstd, NT, sg("rstd_ready"))
            pool.wait_ge(sg("h_ready"), 2)
            load(w_row[:, 0, :], ln_f_w.partition_broadcast(P), "row_loaded")
            root_pool(pool, sg("ms_ready"), 3, ssum, rstd, NT, sg("rstd_ready"))
            pool.wait_ge(sg("h_ready"), 3)
            load(f_causal, c_causal, "fox_loaded")
            load(tri, c_masks[LEVELS + 3], "fox_loaded")
            load(f_w, fox_w_in[:, 4 * D:4 * D + FOX_HEADS].rearrange("(k p) n -> p k n", p=P), "fox_loaded")
            nc.gpsimd.memset(f_ones[:, :], 1.0).then_inc(sg("f_ones_ready"), 1)
            with fori(4) as g:
                root_pool(pool, sg("f_ms_ready"), Lin(1, [(1, g)]), f_ss.rearrange("p a b -> p (a b)"),
                          f_rs.rearrange("p a b -> p (a b)"), 16, sg("f_rs_ready"))
            pool.wait_ge(sg("fo_ready"), 4)
            for i in range(2):
                load(w_row[:, i, :], (ln_gain, ln_bias)[i][0, :].partition_broadcast(P), "ln_row_loaded")
            root_pool(pool, sg("ln_ms_ready"), 1, lnr, rstd, NT, sg("ln_rs_ready"))
            pool.wait_ge(sg("ln_done"), 1)
            load(r_cs[:, :, :, :], c_rope.rearrange("a (t p) n -> p a t n", p=P), "ret_loaded")
            load(r_dec, c_decay.rearrange("a p n -> p a n"), "ret_loaded")
            with fori(2) as h:
                with fori(2) as p:
                    pr = Lin(0, [(2, h), (1, p)])
                    wait(pool, acc_taken[1], Lin(J_RET, [(16, h), (6, p)]).half() + 1)
                    pool.dma_start(r_D[:, :, :], c_intra[:, bass.ds(h * 4 + p * 2, 2), :]) \
                        .then_inc(sg("r_D_loaded"), 16)
                    for hh in range(2):
                        root_pool(pool, sg("r_ms_ready"), pr * 2 + (hh + 1), r_rs, r_rs, NT,
                                  sg("r_rs_ready"))
            for i in range(2):
                if i == 0:
                    pool.wait_ge(lt_lo_ready, B_RO + 16)
                load(w_row[:, i, :], (ln_gain, ln_bias)[i][1, :].partition_broadcast(P), "ln_row_loaded")
            root_pool(pool, sg("ln_ms_ready"), 2, lnr, rstd, NT, sg("ln_rs_ready"))

        @block.scalar
        def _(act):
            A = nc.scalar.activation

            def fori(n):
                return act.Fori(0, n)

            loads = [(onehot[0:BUCKETS, :], c_onehot), (tabl[0:BUCKETS, :], rel_table),
                     (cw_nat[0:96, :], conv_w.rearrange("w (c p) -> (w c) p", p=P)),
                     (pe_nat[0:CMP_BLOCK, 0, :], pe_k), (pe_nat[0:CMP_BLOCK, 1, :], pe_v),
                     (wsmall[:, :, 0:24], w_in[:, C_GATE:C_GDN].rearrange("(k p) n -> p k n", p=P)),
                     (wsmall[:, :, 24:40], w_in[:, C_AB:C_MERGE].rearrange("(k p) n -> p k n", p=P)),
                     (w2[:, 0, :, :], w2_k.rearrange("(c p) n -> p c n", p=P)),
                     (w2[:, 1, :, :], w2_v.rearrange("(c p) n -> p c n", p=P)),
                     (a_row, a_log.partition_broadcast(P)), (dt_row, dt_bias.partition_broadcast(P)),
                     (bf_row, fox_b_f.partition_broadcast(P)), (gnorm[:, :], gdn_norm_w.partition_broadcast(P)),
                     (fgain[:, 0, :], fox_q_gain.partition_broadcast(P)),
                     (fgain[:, 1, :], fox_k_gain.partition_broadcast(P))]
            for dst, src in loads:
                act.dma_start(dst, src).then_inc(sg("const_loaded"), 16)
            assert N_CONST == len(loads)

            act.wait_ge(sg("x_loaded"), 16)
            rms_act(act, 0)
            split_hi(act, 0, 0, 4)
            turn_hi(act, B_LN1, whole(lt_a), 8)
            act.wait_ge(sg("gates_ready"), 1)
            A(gates[:, :, :], small_ps[:, :, 0:24], ACT.Sigmoid)
            A(gt[1], small_ps[:, :, 24:32], ACT.Copy)
            A(tok[:, G_BETA], small_ps[:, :, 32:40], ACT.Sigmoid).then_inc(sg("gates_done"), 1)
            act.wait_ge(sg("softplus_arg"), 1)
            act.wait_ge(sg("const_loaded"), 16 * N_CONST)
            A(gt[0], gt[0], ACT.Exp).then_inc(sg("act_step"), 1)
            act.wait_ge(sg("act_step"), 1)
            A(gt[0], gt[0], ACT.Ln, bias=1.0)
            A(a_row, a_row, ACT.Exp).then_inc(sg("softplus_done"), 1)

            def copy_job(J, dst, func=ACT.Copy, scale=1.0):
                split_hi(act, J, 4, ahead(J))
                take(act, J, lin(J).c % 2, lambda t: A(dst(t), acc[lin(J).c % 2][t][:, :], func, scale=scale))

            copy_job(0, lambda t: nat[:, 0, t, :])
            with fori(2) as i:
                for c in range(2):
                    copy_job(Lin(1 + c, [(2, i)]),
                             lambda t: nat[:, bass.ds(i * 2 + (1 + c), 1), t, :].rearrange("p a n -> p (a n)"))
            for n, b in enumerate(NSA_ORDER):
                act.wait_ge(sg("nsa_turned"), n + 1)
                A(T[:, 2 * b:2 * b + 2, :], mx[:, n % 4, :].rearrange("p (c s) -> p c s", s=S),
                  ACT.Copy).then_inc(sg("nsa_copied"), 1)
            for kv in range(2):
                act.wait_ge(sg("blocks_ready"), kv + 1)
                A(cb[0][:, kv, :], blk, ACT.Copy).then_inc(sg("blocks_hi"), 1)
            split_hi(act, J_CMP, 4, 12)
            split_hi(act, J_CMP + 1, 4, 12)
            for kv in range(2):
                par = (J_CMP + kv) % 2
                wait(act, granules_done, (J_CMP + kv + 1) * GPJ)
                A(cmp_hid[0:NKV * NCMP, kv, :], acc[par][0][0:NKV * NCMP, 0:CMP_HIDDEN],
                  ACT.Gelu_apprx_tanh).then_inc(acc_taken[par], 1)
            act.wait_ge(sg("hid_turned"), 1)
            A(cmp_hT, mx[:, 0, 0:4 * NKV * NCMP].rearrange("p (a b) -> p a b", a=4), ACT.Copy) \
                .then_inc(sg("hid_copied"), 1)
            act.wait_ge(sg("cmp_ready"), 1)
            A(kcT, mx[:, 1, 0:NKV * NCMP], ACT.Copy)
            A(vc[0:NCMP, :, :], mx[0:NCMP, 2, 0:NKV * HD].rearrange("p (g d) -> p g d", g=NKV), ACT.Copy) \
                .then_inc(sg("cmp_copied"), 1)
            for g in range(NKV):
                act.wait_ge(sg("cmp_rowmax"), g + 1)
                for j in range(HG):
                    for t, (a, b) in enumerate(((0, NC0), (NC0, NC0 + NCMP))):
                        last = A(scc[:, j, a:b], scc[:, j, a:b], ACT.Exp, bias=rowmax[:, t, j:j + 1])
                last.then_inc(sg("cmp_exp"), 1)
                act.wait_ge(sg("cmp_turned"), g + 1)
                A(pt[0:NC0, :, 0:P], mx[0:NC0, :, 0:P], ACT.Copy)
                A(pt[0:NCMP, :, P:S], mx[0:NCMP, :, P:S], ACT.Copy).then_inc(sg("cmp_probs_copied"), 1)
                for b in range(2):
                    unit_act(act, 2 * g + b, sc, pt)
                turn_hi(act, B_OA + 2 * g, part(lt_b, 4 * g), 2)

            act.wait_ge(sg("gcum_ready"), 1)
            A(tok[:, G_E], tok[:, G_CUM], ACT.Exp)
            A(tok[:, G_KD], tok[:, G_KD], ACT.Exp).then_inc(sg("gexp_done"), 1)
            with fori(2) as g:
                for kind in range(4):
                    copy_job(Lin(J_GDN + kind, [(4, g)]), lambda t, kind=kind: g_nat[:, kind, t, :])
                six = Lin(0, [(6, g)])
                one = Lin(0, [(1, g)])
                for b in range(6):
                    wait(act, sg("gct_turned"), six + b + 1)
                    A(g_ct[:, 2 * b:2 * b + 2, 3:3 + S], mx[:, b % 4, :].rearrange("p (c s) -> p c s", s=S),
                      ACT.Copy).then_inc(sg("gct_copied"), 1)
                wait(act, sg("conv_done"), one + 1)
                A(g_cv[:, :, :], g_cv[:, :, :], ACT.Silu)
                A(g_nat[:, 3], g_nat[:, 3], ACT.Silu).then_inc(sg("silu_done"), 1)
                for b in range(6):
                    wait(act, sg("grn_turned"), six + b + 1)
                    A(g_rn[:, b // 3, 4 * (b % 3):4 * (b % 3) + 4, :],
                      mx[:, b % 4, :].rearrange("p (c s) -> p c s", s=HD), ACT.Copy) \
                        .then_inc(sg("grn_copied"), 1)
                for b in range(6):
                    wait(act, sg("gqk_turned"), six + b + 1)
                    A(g_cv[:, 2 * b:2 * b + 2, :], mx[:, b % 4, :].rearrange("p (c s) -> p c s", s=S),
                      ACT.Copy).then_inc(sg("gqk_copied"), 1)
                wait(act, sg("gdiff_ready"), one + 1)
                A(g_dec[:, :, :], g_dec[:, :, :], ACT.Exp, scale=-1.0)
                A(egl, egl, ACT.Exp)
                A(g_qkT[:, :, :], g_qkT[:, :, :], ACT.Exp).then_inc(sg("gdecay_ready"), 1)
                with fori(LEVELS) as l:
                    lv = Lin(0, [(LEVELS, g), (1, l)])
                    wait(act, sg("inv_p"), lv + 1)
                    A(g_P1[:, :, :], mx[:, 0:2, :].rearrange("p b (c s) -> p (b c) s", s=P), ACT.Copy) \
                        .then_inc(sg("inv_p_copied"), 1)
                wait(act, sg("uw_ready"), one + 1)
                A(g_U[:, :, :], mx[:, 0:2, :].rearrange("p b (c s) -> p (b c) s", s=P), ACT.Copy)
                A(g_wT[:, :, :], mx[:, 2:4, :].rearrange("p b (c s) -> p (b c) s", s=P), ACT.Copy) \
                    .then_inc(sg("uw_copied"), 1)
                for n in range(4):
                    t, r = n // 2, slice(CHUNK * (n % 2), CHUNK * (n % 2) + CHUNK)
                    wait(act, sg("ws_ready"), Lin(n + 1, [(4, g)]))
                    A(g_o[r, t, :, :], mx[r, 1, :].rearrange("p (h d) -> p h d", d=HD), ACT.Copy) \
                        .then_inc(sg("oq_copied"), 1)
                turn_hi(act, Lin(B_OB, [(2, g)]), part(lt_b, g * HG + NH), 2)

            with fori(4) as i:
                for c in range(2):
                    copy_job(Lin(J_MERGE + c, [(2, i)]),
                             lambda t: mg[:, bass.ds(i * 2 + c, 1), t, :].rearrange("p a n -> p (a n)"),
                             ACT.Sigmoid)
            with fori(2) as i:
                for c in range(2):
                    split_hi(act, Lin(J_PAB + c, [(2, i)]), 4, 12)
            turn_hi(act, B_Y, whole(lt_a), 8)
            with fori(2) as i:
                for c in range(2):
                    split_hi(act, Lin(J_WO + c, [(2, i)]), 4, 12)
            act.wait_ge(sg("wo_done"), 4)
            rms_act(act, 1)
            turn_hi(act, B_LN2, whole(lt_a), 8)
            with fori(4) as g:
                for c in range(5):
                    J = Lin(J_MLP + c, [(8, g)])
                    split_hi(act, J, 4, 6)
                    if c:
                        turn_hi(act, Lin(B_U + 2 * (c - 1), [(8, g)]), part(lt_b, 4 * (c - 1)), 2)
                    split_hi(act, J, 6, 12)
                    if c < 4:
                        wait(act, granules_done, J * GPJ + GPJ)
                        for t in range(NT):
                            last = A(relu[:, t, :], acc[J.c % 2][t][:, :], ACT.Relu)
                        last.then_inc(acc_taken[J.c % 2], 1)
                for c in range(5, 8):
                    split_hi(act, Lin(J_MLP + c, [(8, g)]), 4, 12)
            act.wait_ge(sg("down_done"), 16)
            rms_act(act, 2)
            turn_hi(act, B_LNF, whole(lt_a), 8)

            act.wait_ge(sg("f_arg_ready"), 1)
            A(f_t[1], f_t[1], ACT.Exp).then_inc(sg("act_step"), 1)
            act.wait_ge(sg("act_step"), 2)
            A(f_t[1], f_t[1], ACT.Ln, bias=1.0).then_inc(sg("f_ln_done"), 1)
            with fori(4) as g:
                for kind in range(4):
                    copy_job(Lin(J_FOX + kind, [(4, g)]), lambda t, kind=kind: f_nat[:, kind, t, :],
                             ACT.Silu if kind == 3 else ACT.Copy)
                for b in range(4):
                    wait(act, sg("fqk_turned"), Lin(b + 1, [(4, g)]))
                    A(f_T[:, 2 * b:2 * b + 2, :], mx[:, b % 4, :].rearrange("p (c s) -> p c s", s=S),
                      ACT.Copy).then_inc(sg("fqk_copied"), 1)
                unit_act(act, Lin(4, [(1, g)]), f_sc, f_pt)
                turn_hi(act, Lin(B_FO, [(2, g)]), part(lt_b, g * HG), 2)
            with fori(2) as i:
                for c in range(2):
                    split_hi(act, Lin(J_FOXO + c, [(2, i)]), 4, 12)
            turn_hi(act, B_LNG, whole(lt_a), 8)

            with fori(2) as h:
                with fori(2) as p:
                    pr = Lin(0, [(2, h), (1, p)])
                    J = Lin(J_RET, [(16, h), (6, p)])
                    for c in range(6):
                        copy_job(J + c, lambda t, c=c: r_nat[:, c, t, :],
                                 ACT.Silu if c > 3 else ACT.Copy, RET_QK ** -0.5 if c == 1 else 1.0)
                    for b in range(4):
                        wait(act, sg("rqk_turned"), pr * 5 + b + 1)
                        A(r_T[:, 2 * b:2 * b + 2, :], mx[:, b % 4, :].rearrange("p (c s) -> p c s", s=S),
                          ACT.Copy).then_inc(sg("rqk_copied"), 1)
                    wait(act, sg("rqk_turned"), pr * 5 + 5)
                    A(r_qdT[:, :, :], mx[:, 0, :].rearrange("p (c s) -> p c s", s=P), ACT.Copy) \
                        .then_inc(sg("rqk_copied"), 1)
                    for hh in range(2):
                        wait(act, sg("r_R_ready"), pr * 2 + hh + 1)
                        A(r_R[:, 2 * hh:2 * hh + 2, :], mx[:, 2:4, :], ACT.Copy) \
                            .then_inc(sg("r_R_copied"), 1)
                    turn_hi(act, Lin(B_RO, [(8, h), (4, p)]), part(lt_b, p * 8), 4)
                for c in range(4):
                    split_hi(act, Lin(J_RET + 12 + c, [(16, h)]), 4, 12)

        @block.tensor
        def _(pe):
            MM, TR = nc.tensor.matmul, nc.tensor.transpose

            def fori(n):
                return pe.Fori(0, n)

            def small_mm(dst, w, n):
                for t in range(NT):
                    for kt in range(KT):
                        for p in range(2):
                            last = MM(dst[:, t, 0:n], lt_a[p][:, kt, t * P:(t + 1) * P].bitcast(F32),
                                      w[:, kt, 0:n], start=(kt + p == 0), stop=(kt == KT - 1 and p == 1))
                return last

            pe.wait_ge(sg("const_loaded"), 16 * N_CONST)
            pe.wait_ge(sg("ident_ready"), 1)
            MM(mx[0:NH, 0, 0:384], tabl[0:BUCKETS, :], onehot[0:BUCKETS, :], start=True, stop=True)
            TR(mx[:, 1, 0:96], cw_nat[0:96, :], ident[0:96, 0:96])
            for kv in range(2):
                last = TR(mx[:, 2, 32 * kv:32 * kv + 32], pe_nat[0:CMP_BLOCK, kv, :],
                          ident[0:CMP_BLOCK, 0:CMP_BLOCK])
            last.then_inc(sg("prep_ready"), 1)
            pe.wait_ge(sg("prep_taken"), 1)
            pe.wait_ge(sg("h_ready"), 1)
            turn(pe, B_LN1, lambda c, t: h_nat[:, t, c * P:(c + 1) * P], 8)
            pe.wait_ge(lt_lo_ready, B_LN1 + 8)
            small_mm(small_ps, wsmall, 40).then_inc(sg("gates_ready"), 1)

            multiply(pe, 0, lt_a, 0)
            with fori(2) as i:
                for c in range(2):
                    multiply(pe, Lin(1 + c, [(2, i)]), lt_a, (1 + c) % 2,
                             free=(acc_taken[0], Lin(1, [(1, i)])) if c == 0 else None)
            pe.wait_ge(acc_taken[0], 3)
            pe.wait_ge(sg("gates_done"), 1)
            for n, b in enumerate(NSA_ORDER):
                if n >= 4:
                    pe.wait_ge(sg("nsa_copied"), n - 3)
                for c in range(2):
                    blkno, col = NSA_TILES[2 * b + c]
                    for t in range(NT):
                        last = TR(mx[:, n % 4, (2 * c + t) * P:(2 * c + t + 1) * P],
                                  nat[:, blkno, t, col * P:(col + 1) * P], ident[:, :])
                last.then_inc(sg("nsa_turned"), 1)
            for kv in range(2):
                J, par = J_CMP + kv, (J_CMP + kv) % 2
                pe.wait_ge(acc_taken[par], J // 2)
                pe.wait_ge(sg("blocks_lo"), kv + 1)
                for r in range(GPJ):
                    pe.wait_ge(lo_ready, J * GPJ + r + 1)
                    for k in range(4):
                        j = 4 * r + k
                        hi, lo = (w[:, r % 4].rearrange("p a b -> p (a b)")[:, k * 256:(k + 1) * 256]
                                  for w in (w_hi, w_lo))
                        b_hi, b_lo = (cb[p][:, kv, j * 30:(j + 1) * 30] for p in range(2))
                        o = acc[par][0][0:NKV * NCMP, 0:CMP_HIDDEN]
                        MM(o, b_hi, hi, start=(j == 0), stop=False)
                        MM(o, b_hi, lo, start=False, stop=False)
                        last = MM(o, b_lo, hi, start=False, stop=(j == CMP_BLOCK - 1))
                    last.then_inc(granules_done, 1)
            n = NKV * NCMP
            pe.wait_ge(acc_taken[J_CMP % 2], J_CMP // 2 + 1)
            pe.wait_ge(acc_taken[(J_CMP + 1) % 2], (J_CMP + 1) // 2 + 1)
            pe.wait_ge(sg("nsa_copied"), 8)
            for kv in range(2):
                for c in range(2):
                    last = TR(mx[:, 0, (2 * kv + c) * n:(2 * kv + c + 1) * n],
                              cmp_hid[0:n, kv, c * P:(c + 1) * P], ident[0:n, 0:n])
            last.then_inc(sg("hid_turned"), 1)
            pe.wait_ge(sg("hid_copied"), 1)
            for c in range(2):
                MM(mx[:, 1, 0:n], w2[:, 0, c, :], cmp_hT[:, c, :], start=(c == 0), stop=(c == 1))
            for g in range(NKV):
                for c in range(2):
                    last = MM(mx[0:NCMP, 2, g * HD:(g + 1) * HD], cmp_hT[:, 2 + c, g * NCMP:(g + 1) * NCMP],
                              w2[:, 1, c, :], start=(c == 0), stop=(c == 1))
            last.then_inc(sg("cmp_ready"), 1)
            pe.wait_ge(sg("cmp_copied"), 1)
            for g in range(NKV):
                kc = kcT[:, g * NCMP:(g + 1) * NCMP]
                for j in range(HG):
                    MM(mx[:, j, 0:NC0], T[:, HG * g + j, 0:P], kc[:, 0:NC0], start=True, stop=True)
                    last = MM(mx[:, j, NC0:NC0 + NCMP], T[:, HG * g + j, P:S], kc, start=True, stop=True)
                last.then_inc(sg("cmp_scores"), 1)
                pe.wait_ge(sg("cmp_probs"), g + 1)
                for j in range(HG):
                    TR(mx[0:NC0, j, 0:P], scc[:, j, 0:NC0], ident[:, :])
                    last = TR(mx[0:NCMP, j, P:S], scc[:, j, NC0:NC0 + NCMP], ident[:, :])
                last.then_inc(sg("cmp_turned"), 1)
                pe.wait_ge(sg("cmp_probs_copied"), g + 1)
                for j in range(HG):
                    MM(mx[:, 0, j * HD:(j + 1) * HD], pt[0:NC0, j, 0:P], vc[0:NC0, g, :], start=True, stop=True)
                    last = MM(mx[:, 1, j * HD:(j + 1) * HD], pt[0:NCMP, j, P:S], vc[0:NCMP, g, :],
                              start=True, stop=True)
                last.then_inc(sg("cmp_out_ready"), 1)
                pe.wait_ge(sg("cmp_out_taken"), g + 1)
                for b in range(2):
                    unit_pe(pe, 2 * g + b, sc, pt, lambda j: T[:, HG * g + j, :], lambda j: T[:, 12 + 2 * b + g, :],
                            lambda j, t: nat[:, 3 + b, t, (2 + g) * HD:(3 + g) * HD])
                pe.wait_ge(att["att_out_taken"], 2 * g + 2)
                turn(pe, B_OA + 2 * g, lambda c, t: o_nat[:, t, c, :], 2)
                pe.wait_ge(lt_lo_ready, B_OA + 2 * g + 2)

            pe.wait_ge(sg("mask_loaded"), 16)
            for t in range(NT):
                MM(mx[:, 0, t * NH:(t + 1) * NH], g_mask[:, M_TRI, :], tok[:, G_G, t, :], start=True, stop=True)
                last = MM(mx[:, 0, (2 + t) * NH:(3 + t) * NH], g_mask[:, M_ONES, :], tok[:, G_G, t, :],
                          start=True, stop=True)
            last.then_inc(sg("gsum_ready"), 1)
            with fori(2) as g:
                six = Lin(0, [(6, g)])
                one = Lin(0, [(1, g)])
                for kind in range(4):
                    J = Lin(J_GDN + kind, [(4, g)])
                    multiply(pe, J, lt_a, J.c % 2)
                wait(pe, acc_taken[1], Lin((J_GDN + 2) // 2 + 1, [(2, g)]))
                wait(pe, acc_taken[0], Lin((J_GDN + 3) // 2 + 1, [(2, g)]))
                pe.wait_ge(sg("gcum_ready"), 1)
                for b in range(6):
                    if b >= 4:
                        wait(pe, sg("gct_copied"), six + b - 3)
                    for c in range(2):
                        i = 2 * b + c
                        for t in range(NT):
                            last = TR(mx[:, b % 4, (2 * c + t) * P:(2 * c + t + 1) * P],
                                      g_nat[:, i // 4, t, (i % 4) * P:(i % 4 + 1) * P], ident[:, :])
                    last.then_inc(sg("gct_turned"), 1)
                wait(pe, sg("silu_done"), one + 1)
                for b in range(6):
                    if b >= 4:
                        wait(pe, sg("grn_copied"), six + b - 3)
                    for c in range(4):
                        last = TR(mx[:, b % 4, c * P:(c + 1) * P],
                                  g_cv[:, 4 * (b % 3) + c, (b // 3) * P:(b // 3 + 1) * P], ident[:, :])
                    last.then_inc(sg("grn_turned"), 1)
                wait(pe, sg("g_normed"), one + 1)
                for b in range(6):
                    if b >= 4:
                        wait(pe, sg("gqk_copied"), six + b - 3)
                    for c in range(2):
                        i = 2 * b + c
                        for t in range(NT):
                            src = g_rn[:, t, i, :] if i < 8 else g_qg[:, t, i - 8, :]
                            last = TR(mx[:, b % 4, (2 * c + t) * P:(2 * c + t + 1) * P], src, ident[:, :])
                    last.then_inc(sg("gqk_turned"), 1)
                wait(pe, sg("gqk_copied"), six + 6)
                for h in range(HG):
                    for t in range(NT):
                        i = h * NT + t
                        last = MM(mx[:, i // 4, (i % 4) * P:(i % 4 + 1) * P],
                                  tg[:, G_G, t, h:h + 1].to_broadcast([P, P]), g_mask[:, M_TRI, :],
                                  start=True, stop=True)
                last.then_inc(sg("gb_ready"), 1)
                for h in range(HG):
                    for t in range(NT):
                        i = h * NT + t
                        k = g_kT[:, h, t * P:(t + 1) * P]
                        last = MM(mx[:, 2 + i // 4, (i % 4) * P:(i % 4 + 1) * P], k, k, start=True, stop=True)
                last.then_inc(sg("kk_ready"), 1)
                wait(pe, sg("gdiff_ready"), one + 1)
                for h in range(HG):
                    for t in range(NT):
                        i = h * NT + t
                        last = MM(mx[:, i // 4, (i % 4) * P:(i % 4 + 1) * P], g_kT[:, h, t * P:(t + 1) * P],
                                  g_qT[:, h, t * P:(t + 1) * P], start=True, stop=True)
                last.then_inc(sg("qk_ready"), 1)
                with fori(LEVELS) as l:
                    lv = Lin(0, [(LEVELS, g), (1, l)])
                    wait(pe, sg("inv_c"), Lin(1, [(LEVELS + 1, g), (1, l)]))
                    for i in range(HG * NT):
                        last = MM(mx[:, i // 4, (i % 4) * P:(i % 4 + 1) * P], g_dec[:, i, :], g_Y[:, i, :],
                                  start=True, stop=True)
                    last.then_inc(sg("inv_p"), 1)
                    wait(pe, sg("inv_p_copied"), lv + 1)
                    for i in range(HG * NT):
                        MM(mx[:, 2 + i // 4, (i % 4) * P:(i % 4 + 1) * P], g_X[:, i, :], g_P1[:, i, :],
                           start=True, stop=True)
                    for i in range(HG * NT):
                        last = MM(mx[:, i // 4, (i % 4) * P:(i % 4 + 1) * P], g_P1[:, i, :], g_X[:, i, :],
                                  start=True, stop=True)
                    last.then_inc(sg("inv_q"), 1)
                wait(pe, sg("inv_c"), Lin(LEVELS + 1, [(LEVELS + 1, g)]))
                for h in range(HG):
                    for t in range(NT):
                        i = h * NT + t
                        MM(mx[:, i // 4, (i % 4) * P:(i % 4 + 1) * P], g_Y[:, i, :], g_vb[:, t, h, :],
                           start=True, stop=True)
                        last = MM(mx[:, 2 + i // 4, (i % 4) * P:(i % 4 + 1) * P], g_kbeg[:, t, h, :],
                                  g_Y[:, i, :], start=True, stop=True)
                last.then_inc(sg("uw_ready"), 1)
                wait(pe, sg("uw_copied"), one + 1)
                for n in range(4):
                    t, r = n // 2, slice(CHUNK * (n % 2), CHUNK * (n % 2) + CHUNK)
                    wait(pe, sg("s_ready"), Lin(n + 1, [(5, g)]))
                    if n:
                        wait(pe, sg("oq_copied"), Lin(n, [(4, g)]))
                    for h in range(HG):
                        MM(mx[:, 0, h * HD:(h + 1) * HD], g_wT[:, h * NT + t, :], g_S[:, h, :],
                           start=True, stop=True)
                    for h in range(HG):
                        last = MM(mx[r, 1, h * HD:(h + 1) * HD], g_qgT[:, h, t * P + r.start:t * P + r.stop],
                                  g_S[:, h, :], start=True, stop=True)
                    last.then_inc(sg("ws_ready"), 1)
                    wait(pe, sg("v_ready"), Lin(n + 1, [(4, g)]))
                    for h in range(HG):
                        last = MM(mx[:, 2, h * HD:(h + 1) * HD], g_kdec[r, t, h, :], g_V[r, h, :],
                                  start=True, stop=True)
                    last.then_inc(sg("su_ready"), 1)
                    if n % 2:
                        for h in range(HG):
                            last = MM(mx[:, 3, h * HD:(h + 1) * HD], g_qkT[:, h * NT + t, :], g_V[:, h, :],
                                      start=True, stop=True)
                        last.then_inc(sg("in_ready"), 1)
                wait(pe, sg("go_ready"), one + 1)
                turn(pe, Lin(B_OB, [(2, g)]), lambda c, t: g_o[:, t, c, :], 2)
                wait(pe, lt_lo_ready, Lin(B_OB + 2, [(2, g)]))

            with fori(4) as i:
                for c in range(2):
                    J = Lin(J_MERGE + c, [(2, i)])
                    multiply(pe, J, lt_a, J.c % 2)
            with fori(2) as i:
                for c in range(2):
                    J = Lin(J_PAB + c, [(2, i)])
                    wait(pe, acc_taken[0], (J + 1).half() if J.c % 2 else J.half())
                    wait(pe, acc_taken[1], J.half())
                    for r in range(GPJ):
                        wait(pe, lo_ready, J * GPJ + r + 1)
                        for k in range(2):
                            kt = 2 * r + k
                            for t in range(NT):
                                a_hi, a_lo = (lt_b[p][:, kt, t * P:(t + 1) * P] for p in range(2))
                                o = acc[kt // 8][t][:, :]
                                MM(o, a_hi, w_hi[:, r % 4, k, :], start=(kt % 8 == 0), stop=False)
                                MM(o, a_hi, w_lo[:, r % 4, k, :], start=False, stop=False)
                                last = MM(o, a_lo, w_hi[:, r % 4, k, :], start=False, stop=(kt % 8 == 7))
                        last.then_inc(granules_done, 1)
            pe.wait_ge(sg("y_ready"), 1)
            turn(pe, B_Y, lambda c, t: y_nat[:, t, c * P:(c + 1) * P], 8)
            pe.wait_ge(lt_lo_ready, B_Y + 8)
            pe.wait_ge(acc_taken[0], (J_WO + 1) // 2)
            with fori(2) as i:
                for c in range(2):
                    J = Lin(J_WO + c, [(2, i)])
                    multiply(pe, J, lt_a, J.c % 2)
            pe.wait_ge(sg("h_ready"), 2)
            turn(pe, B_LN2, lambda c, t: h_nat[:, t, c * P:(c + 1) * P], 8)
            pe.wait_ge(lt_lo_ready, B_LN2 + 8)
            with fori(4) as g:
                for c in range(8):
                    J = Lin(J_MLP + c, [(8, g)])

                    def hook(r, c=c):
                        if r == 3 and 1 <= c <= 4:
                            wait(pe, sg("u_ready"), Lin(c, [(4, g)]))
                            turn(pe, Lin(B_U + 2 * (c - 1), [(8, g)]),
                                 lambda k, t: u_nat[:, (c - 1) % 2, t, k * P:(k + 1) * P], 2)
                        if r == 6 and c == 4:
                            wait(pe, lt_lo_ready, Lin(B_U + 8, [(8, g)]))
                    if c == 4:
                        wait(pe, lt_lo_ready, Lin(B_U + 6, [(8, g)]))
                    multiply(pe, J, lt_a if c < 4 else lt_b, J.c % 2, hook)
            pe.wait_ge(sg("h_ready"), 3)
            turn(pe, B_LNF, lambda c, t: res[:, t, c * P:(c + 1) * P], 8)
            pe.wait_ge(lt_lo_ready, B_LNF + 8)

            pe.wait_ge(sg("fox_loaded"), 48)
            small_mm(small_ps, f_w, FOX_HEADS).then_inc(sg("f_logit_ready"), 1)
            pe.wait_ge(sg("f_arg_ready"), 1)
            pe.wait_ge(sg("f_ones_ready"), 1)
            with fori(4) as g:
                four = Lin(0, [(4, g)])
                for kind in range(4):
                    J = Lin(J_FOX + kind, [(4, g)])
                    multiply(pe, J, lt_a, J.c % 2)
                wait(pe, sg("fq_ready"), Lin(1, [(1, g)]))
                for h in range(HG):
                    MM(mx[:, h, 0:P], f_lg[:, 0, h:h + 1].to_broadcast([P, P]), tri[:, :], start=True, stop=True)
                    MM(mx[:, h, P:S], f_lg[:, 0, h:h + 1].to_broadcast([P, P]), f_ones[:, :],
                       start=True, stop=False)
                    last = MM(mx[:, h, P:S], f_lg[:, 1, h:h + 1].to_broadcast([P, P]), tri[:, :],
                              start=False, stop=True)
                last.then_inc(sg("f_cum_ready"), 1)
                wait(pe, sg("f_bias_ready"), Lin(1, [(1, g)]))
                for b in range(4):
                    for c in range(2):
                        i = 2 * b + c
                        for t in range(NT):
                            last = TR(mx[:, b, (2 * c + t) * P:(2 * c + t + 1) * P],
                                      f_nat[:, i // 4, t, (i % 4) * P:(i % 4 + 1) * P], ident[:, :])
                    last.then_inc(sg("fqk_turned"), 1)
                wait(pe, sg("fqk_copied"), four + 4)
                unit_pe(pe, Lin(4, [(1, g)]), f_sc, f_pt, lambda j: f_T[:, j, :], lambda j: f_T[:, 4 + j, :],
                        lambda j, t: f_nat[:, 2, t, j * HD:(j + 1) * HD])
                wait(pe, sg("fo_ready"), Lin(1, [(1, g)]))
                turn(pe, Lin(B_FO, [(2, g)]), lambda c, t: f_o[:, t, c, :], 2)
                wait(pe, lt_lo_ready, Lin(B_FO + 2, [(2, g)]))
            with fori(2) as i:
                for c in range(2):
                    J = Lin(J_FOXO + c, [(2, i)])
                    multiply(pe, J, lt_b, J.c % 2)
            pe.wait_ge(sg("ln_done"), 1)
            turn(pe, B_LNG, lambda c, t: res[:, t, c * P:(c + 1) * P], 8)
            pe.wait_ge(lt_lo_ready, B_LNG + 8)

            with fori(2) as h:
                with fori(2) as p:
                    pr = Lin(0, [(2, h), (1, p)])
                    J = Lin(J_RET, [(16, h), (6, p)])
                    for c in range(6):
                        multiply(pe, J + c, lt_a, (J + c).c % 2)
                    wait(pe, sg("rot_ready"), pr + 1)
                    for b in range(4):
                        for c in range(2):
                            i = 2 * b + c
                            for t in range(NT):
                                last = TR(mx[:, b, (2 * c + t) * P:(2 * c + t + 1) * P],
                                          r_nat[:, i // 4, t, (i % 4) * P:(i % 4 + 1) * P], ident[:, :])
                        last.then_inc(sg("rqk_turned"), 1)
                    wait(pe, sg("rqk_copied"), pr * 5 + 1)
                    for c in range(4):
                        last = TR(mx[:, 0, c * P:(c + 1) * P], r_tmp[:, 0, c * P:(c + 1) * P], ident[:, :])
                    last.then_inc(sg("rqk_turned"), 1)
                    wait(pe, sg("rqk_copied"), pr * 5 + 5)
                    for hh in range(2):
                        for t in range(NT):
                            for k in range(2):
                                i = 2 * hh + t
                                last = MM(mx[:, 1, i * P:(i + 1) * P], r_T[:, 4 + 2 * hh + k, t * P:(t + 1) * P],
                                          r_T[:, 2 * hh + k, t * P:(t + 1) * P], start=(k == 0), stop=(k == 1))
                    last.then_inc(sg("r_inner"), 1)
                    for hh in range(2):
                        for k in range(2):
                            last = MM(mx[:, 2 + k, :], r_kd[:, hh, k * P:(k + 1) * P], r_nat[:, 2 + hh, 0, :],
                                      start=True, stop=True)
                        last.then_inc(sg("r_R_ready"), 1)
                        wait(pe, sg("r_R_copied"), pr * 2 + hh + 1)
                    wait(pe, sg("r_in_ready"), pr + 1)
                    for hh in range(2):
                        if hh:
                            wait(pe, sg("r_o_taken"), pr * 2 + hh)
                        MM(mx[:, 0, :], r_in[:, 2 * hh, :], r_nat[:, 2 + hh, 0, :], start=True, stop=True)
                        MM(mx[:, 1, :], r_in[:, 2 * hh + 1, :], r_nat[:, 2 + hh, 1, :], start=True, stop=False)
                        for k in range(2):
                            last = MM(mx[:, 1, :], r_qdT[:, 2 * hh + k, :], r_R[:, 2 * hh + k, :],
                                      start=False, stop=(k == 1))
                        last.then_inc(sg("r_o_ready"), 1)
                    wait(pe, sg("r_y_ready"), pr + 1)
                    turn(pe, Lin(B_RO, [(8, h), (4, p)]),
                         lambda c, t: r_nat[:, 4 + c // 4, t, (c % 4) * P:(c % 4 + 1) * P], 4)
                wait(pe, lt_lo_ready, Lin(B_RO + 8, [(8, h)]))
                for c in range(4):
                    J = Lin(J_RET + 12 + c, [(16, h)])
                    multiply(pe, J, lt_b, J.c % 2)

        @block.vector
        def _(dve):
            TT, TS, STT = nc.vector.tensor_tensor, nc.vector.tensor_scalar, nc.vector.scalar_tensor_tensor
            copy = nc.vector.tensor_copy

            def fori(n):
                return dve.Fori(0, n)

            def splits(J):
                split_lo(dve, J, 4, 12)

            dve.wait_ge(sg("prep_ready"), 1)
            copy(distb[0:NH, :], mx[0:NH, 0, 0:384])
            copy(cwt[:, :], mx[:, 1, 0:96])
            copy(pet[:, :, :], mx[:, 2, 0:64].rearrange("p (a b) -> p a b", a=2)).then_inc(sg("prep_taken"), 1)
            rms_dve(dve, 0, h_nat)
            turn_lo(dve, B_LN1, whole(lt_a), 8)
            split_lo(dve, 0, 0, 4)
            ch = Chain(dve, sg("dve_step"))
            dve.wait_ge(sg("gates_done"), 1)
            dve.wait_ge(sg("const_loaded"), 16 * N_CONST)
            ch.link(TT(gt[1], gt[1], heads_bcast(dt_row, NT), ALU.add))
            STT(gt[0], gt[1], -1.0, gt[1], ALU.mult, ALU.min).then_inc(sg("softplus_arg"), 1)
            dve.wait_ge(sg("softplus_done"), 1)
            ch.link(STT(gt[2], gt[1], 0.0, gt[0], ALU.max, ALU.add))
            ch.link(STT(tok[:, G_G], gt[2], -1.0, heads_bcast(a_row, NT), ALU.mult, ALU.mult))
            splits(0)
            with fori(2) as i:
                for c in range(2):
                    splits(Lin(1 + c, [(2, i)]))

            for kv in range(2):
                dve.wait_ge(sg("nsa_copied"), 2)
                v = T[:, 8 + 2 * kv, :]
                win = bass.AP(tensor=v.tensor, offset=v.offset,
                              ap=[v.ap[0], [1, CMP_BLOCK], [S, NKV], [CMP_STRIDE, NCMP]])
                pos = pet[:, kv, :]
                pos = bass.AP(tensor=pos.tensor, offset=pos.offset, ap=[*pos.ap, [0, NKV], [0, NCMP]])
                TT(blk.rearrange("p (j g n) -> p j g n", g=NKV, n=NCMP), win, pos, ALU.add) \
                    .then_inc(sg("blocks_ready"), 1)
                dve.wait_ge(sg("blocks_hi"), kv + 1)
                TT(cb[1][:, kv, :], blk, cb[0][:, kv, :].bitcast(F32), ALU.subtract) \
                    .then_inc(sg("blocks_lo"), 1)
                dve.wait_ge(sg("blocks_lo"), kv + 1)
            splits(J_CMP)
            splits(J_CMP + 1)
            dve.wait_ge(sg("bias_masked"), 2)
            last0 = CMP_BLOCK - 1
            copy(bm[:, :, SEG:SEG + NC0], bm[:, :, last0:last0 + CMP_STRIDE * (NC0 - 1) + 1:CMP_STRIDE])
            ch.link(copy(bm[:, :, SEG + NC0:SEGC],
                         bm[:, :, P + last0:P + last0 + CMP_STRIDE * (NCMP - 1) + 1:CMP_STRIDE]))
            gate4 = gates[:, :, :].rearrange("p t (h b) -> p t h b", b=3)
            for g in range(NKV):
                hs = slice(HG * g, HG * g + HG)
                dve.wait_ge(sg("cmp_scores"), g + 1)
                ch.link(STT(scc, mx[:, :, 0:NC0 + NCMP], ATT_SCALE, bm[:, hs, SEG:SEGC], ALU.mult, ALU.add))
                nc.vector.tensor_reduce(rowmax[:, 0, :], scc[:, :, 0:NC0], AX.X, ALU.max, negate=True)
                nc.vector.tensor_reduce(rowmax[:, 1, :], scc[:, :, NC0:NC0 + NCMP], AX.X, ALU.max,
                                        negate=True).then_inc(sg("cmp_rowmax"), 1)
                dve.wait_ge(sg("cmp_exp"), g + 1)
                TT(scc[:, :, 0:NC0], scc[:, :, 0:NC0], heads_bcast(mask0, HG), ALU.mult) \
                    .then_inc(sg("cmp_probs"), 1)
                dve.wait_ge(sg("cmp_probs"), g + 1)
                nc.vector.tensor_reduce(esum[:, 0, :], scc[:, :, 0:NC0], AX.X, ALU.add)
                ch.link(nc.vector.tensor_reduce(esum[:, 1, :], scc[:, :, NC0:NC0 + NCMP], AX.X, ALU.add))
                ch.link(TS(coef[:, 0], esum[:, 0:2], 1e-30, None, ALU.max))
                ch.link(nc.vector.reciprocal(coef[:, 1], coef[:, 0]))
                ch.link(TT(coef[:, 2], coef[:, 1], gate4[:, :, hs, 0], ALU.mult))
                dve.wait_ge(sg("cmp_out_ready"), g + 1)
                for t in range(NT):
                    for j in range(HG):
                        last = TS(o_nat[:, t, j, :], mx[:, t, j * HD:(j + 1) * HD], coef[:, 2, t, j:j + 1],
                                  None, ALU.mult)
                last.then_inc(sg("cmp_out_taken"), 1)
                dve.wait_ge(sg("cmp_out_taken"), g + 1)
                for b in range(2):
                    unit_dve(dve, 2 * g + b, ch, sc, o_nat, bm[:, hs, 0:SEG], gate4[:, :, hs, 1 + b], False)
                    dve.wait_ge(att["att_out_taken"], 2 * g + b + 1)
                turn_lo(dve, B_OA + 2 * g, part(lt_b, 4 * g), 2)

            dve.wait_ge(sg("gsum_ready"), 1)
            sums = mx[:, 0, 0:4 * NH].rearrange("p (a h) -> p a h", h=NH)
            ch.link(copy(tok[:, G_CUM], sums[:, 0:2, :]))
            TT(tok[:, G_KD], sums[:, 2:4, :], tok[:, G_CUM], ALU.subtract).then_inc(sg("gcum_ready"), 1)
            dve.wait_ge(sg("gexp_done"), 1)
            ch.link(TT(tok[:, G_BEG], tok[:, G_BETA], tok[:, G_E], ALU.mult))
            with fori(2) as g:
                one = Lin(0, [(1, g)])
                gc = Chain(dve, sg("gdn_dve_step"), Lin(0, [(K_GDN_DVE, g)]))
                for kind in range(4):
                    splits(Lin(J_GDN + kind, [(4, g)]))
                copy(tg[:, :, :, :].rearrange("p a t h -> p (a t) h"),
                     tok[:, :, :, :].rearrange("p a t h -> p (a t) h")[:, :, bass.ds(g * HG, HG)])
                copy(cwg[:, :, :], cwt[:, :].rearrange("p (c h) -> p c h", h=NH)[:, :, bass.ds(g * HG, HG)])
                gc.link(nc.vector.memset(g_ct[:, :, 0:3], 0.0))
                wait(dve, sg("gct_copied"), Lin(6, [(6, g)]))
                for w in range(4):
                    for i in range(12):
                        s = cwg[:, 3 * w + i // 4, i % 4:i % 4 + 1]
                        if w == 0:
                            last = TS(g_cv[:, i, :], g_ct[:, i, 0:S], s, None, ALU.mult)
                        else:
                            last = STT(g_cv[:, i, :], g_ct[:, i, w:w + S], s, g_cv[:, i, :], ALU.mult, ALU.add)
                    if w < 3:
                        gc.link(last)
                last.then_inc(sg("conv_done"), 1)
                wait(dve, sg("grn_copied"), Lin(6, [(6, g)]))
                qk = g_rn[:, :, 0:8, :]
                gc.link(TT(g_sq[:, :, :, :], qk, qk, ALU.mult))
                gc.link(nc.vector.tensor_reduce(gss, g_sq[:, :, :, :], AX.X, ALU.add))
                TS(gss, gss, NORM_EPS, None, ALU.add).then_inc(sg("gss_ready"), 1)
                wait(dve, sg("grs_ready"), Lin(1, [(2, g)]))
                gc.link(TS(grs[:, :, 0:4], grs[:, :, 0:4], HD ** -0.5, None, ALU.mult))
                gc.link(TT(qk, qk, bcast(grs, HD), ALU.mult))
                qn, kn, vn = (g_rn[:, :, 4 * i:4 * i + 4, :] for i in range(3))
                TT(g_vb[:, :, :, :], vn, bcast(tg[:, G_BETA], HD), ALU.mult)
                TT(g_kbeg[:, :, :, :], kn, bcast(tg[:, G_BEG], HD), ALU.mult)
                TT(g_kdec[:, :, :, :], kn, bcast(tg[:, G_KD], HD), ALU.mult)
                TT(g_qg[:, :, :, :], qn, bcast(tg[:, G_E], HD), ALU.mult).then_inc(sg("g_normed"), 1)
                wait(dve, sg("gb_ready"), one + 1)
                for h in range(HG):
                    for t in range(NT):
                        i = h * NT + t
                        gb, s = mx[:, i // 4, (i % 4) * P:(i % 4 + 1) * P], tg[:, G_CUM, t, h:h + 1]
                        TS(g_dec[:, i, :], gb, s, 0.0, ALU.subtract, ALU.max)
                        TS(g_qkT[:, i, :], gb, s, 0.0, ALU.subtract, ALU.min)
                copy(egl, mx[:, 0:2, CHUNK - 1::CHUNK].rearrange("p b (i n) -> p (b i) n", n=2)) \
                    .then_inc(sg("gdiff_ready"), 1)
                wait(dve, sg("gdecay_ready"), one + 1)
                TT(g_dec[:, :, :], g_dec[:, :, :], heads_bcast(g_mask[:, M_STRICT, :], HG * NT), ALU.mult)
                gc.link(TT(g_qkT[:, :, :], g_qkT[:, :, :], heads_bcast(g_mask[:, M_TRI, :], HG * NT), ALU.mult))
                wait(dve, sg("kk_ready"), one + 1)
                for h in range(HG):
                    for t in range(NT):
                        i = h * NT + t
                        STT(g_A[:, i, :], mx[:, 2 + i // 4, (i % 4) * P:(i % 4 + 1) * P],
                            tg[:, G_BETA, t, h:h + 1], g_dec[:, i, :], ALU.mult, ALU.mult)
                wait(dve, sg("qk_ready"), one + 1)
                copy(g_X[:, :, :], heads_bcast(ident[:, :], HG * NT))
                copy(g_Y[:, :, :], heads_bcast(ident[:, :], HG * NT))
                gc.link(TT(g_qkT[:, :, :], mx[:, 0:2, :].rearrange("p b (c s) -> p (b c) s", s=P), g_qkT[:, :, :],
                           ALU.mult))
                TT(g_dec[:, :, :], g_A[:, :, :], heads_bcast(g_mask[:, 0, :], HG * NT), ALU.mult) \
                    .then_inc(sg("inv_c"), 1)
                with fori(LEVELS) as l:
                    wait(dve, sg("inv_q"), Lin(1, [(LEVELS, g), (1, l)]))
                    TT(g_Y[:, :, :], g_Y[:, :, :], mx[:, 2:4, :].rearrange("p b (c s) -> p (b c) s", s=P),
                       ALU.subtract)
                    TT(g_X[:, :, :], g_X[:, :, :], mx[:, 0:2, :].rearrange("p b (c s) -> p (b c) s", s=P),
                       ALU.subtract)
                    m = g_mask[:, bass.ds(l + 1, 1), :].to_broadcast([P, HG * NT, P])
                    TT(g_dec[:, :, :], g_A[:, :, :], m, ALU.mult).then_inc(sg("inv_c"), 1)
                wait(dve, sg("uw_copied"), one + 1)
                nc.vector.memset(g_S[:, :, :], 0.0).then_inc(sg("s_ready"), 1)
                U4 = g_U[:, :, :].rearrange("p (h t) d -> p h t d", t=NT)
                for n in range(4):
                    t, r = n // 2, slice(CHUNK * (n % 2), CHUNK * (n % 2) + CHUNK)
                    wait(dve, sg("ws_ready"), Lin(n + 1, [(4, g)]))
                    TT(g_V[r, :, :], U4[r, :, t, :], mx[r, 0, :].rearrange("p (h d) -> p h d", d=HD),
                       ALU.subtract).then_inc(sg("v_ready"), 1)
                    wait(dve, sg("su_ready"), Lin(n + 1, [(4, g)]))
                    wait(dve, sg("s_ready"), Lin(n + 1, [(5, g)]))
                    for h in range(HG):
                        last = STT(g_S[:, h, :], g_S[:, h, :], egl[:, h * NT + t, n % 2:n % 2 + 1],
                                   mx[:, 2, h * HD:(h + 1) * HD], ALU.mult, ALU.add)
                    last.then_inc(sg("s_ready"), 1)
                    if n % 2:
                        wait(dve, sg("in_ready"), Lin(n // 2 + 1, [(2, g)]))
                        wait(dve, sg("oq_copied"), Lin(n + 1, [(4, g)]))
                        gc.link(TT(g_o[:, t, :, :], mx[:, 3, :].rearrange("p (h d) -> p h d", d=HD),
                                   g_o[:, t, :, :], ALU.add))
                sq = g_Y[:, :, :]
                o8 = g_o[:, :, :, :].rearrange("p t h d -> p (t h) d")
                s8 = gss.rearrange("p a b -> p (a b)")[:, 0:8]
                gc.link(TT(sq, o8, o8, ALU.mult))
                gc.link(nc.vector.tensor_reduce(s8, sq, AX.X, ALU.add))
                TS(s8, s8, 1.0 / HD, NORM_EPS, ALU.mult, ALU.add).then_inc(sg("gss_ready"), 1)
                wait(dve, sg("grs_ready"), Lin(2, [(2, g)]))
                gc.link(TT(o8, o8, bcast(grs.rearrange("p a b -> p (a b)")[:, 0:8], HD), ALU.mult))
                gc.link(TT(o8, o8, heads_bcast(gnorm[:, :], 8), ALU.mult))
                TT(g_o[:, :, :, :].rearrange("p t h d -> p t (h d)"),
                   g_o[:, :, :, :].rearrange("p t h d -> p t (h d)"), g_nat[:, 3], ALU.mult) \
                    .then_inc(sg("go_ready"), 1)
                turn_lo(dve, Lin(B_OB, [(2, g)]), part(lt_b, g * HG + NH), 2)
                gc.end(K_GDN_DVE)

            with fori(4) as i:
                for c in range(2):
                    splits(Lin(J_MERGE + c, [(2, i)]))
            dve.wait_ge(acc_taken[0], (J_PAB - 1) // 2 + 1)
            with fori(2) as i:
                pc = Chain(dve, sg("pab_dve_step"), Lin(0, [(4, i)]))
                for c in range(2):
                    J = Lin(J_PAB + c, [(2, i)])
                    splits(J)
                    wait(dve, granules_done, J * GPJ + GPJ)
                    for b in range(2):
                        gate = mg[:, bass.ds(i * 2 + (c + 4 * b), 1), :, :].rearrange("p a t n -> p (a t) n")
                        for t in range(NT):
                            o = y_nat[:, t, bass.ds(i * (2 * NB) + c * NB, NB)] if b == 0 else y_tmp[:, t, :]
                            last = TT(o, acc[b][t][:, :], gate[:, t, :], ALU.mult)
                        if b == 0:
                            pc.link(last)
                    last.then_inc(acc_taken[J.c % 2], 1)
                    wait(dve, acc_taken[J.c % 2], J.half() + 1)
                    yy = y_nat[:, :, bass.ds(i * (2 * NB) + c * NB, NB)]
                    pc.link(TT(yy, yy, y_tmp[:, :, :], ALU.add))
                pc.end(4)
            nc.vector.memset(y_tmp[:, 0, 0:1], 0.0).then_inc(sg("y_ready"), 1)
            turn_lo(dve, B_Y, whole(lt_a), 8)

            def add_job(J, col, done=None):
                J = lin(J)
                par = J.c % 2
                wait(dve, granules_done, J * GPJ + GPJ)
                cs = slice(col, col + NB) if isinstance(col, int) else bass.ds(col, NB)
                for t in range(NT):
                    last = TT(res[:, t, cs], res[:, t, cs], acc[par][t][:, :], ALU.add)
                last.then_inc(acc_taken[par], 1)
                if done:
                    wait(dve, acc_taken[par], J.half() + 1)
                    nc.vector.memset(y_tmp[:, 0, 0:1], 0.0).then_inc(sg(done), 1)

            with fori(2) as i:
                for c in range(2):
                    J = Lin(J_WO + c, [(2, i)])
                    splits(J)
                    add_job(J, i * (2 * NB) + c * NB, "wo_done")
            rms_dve(dve, 1, h_nat)
            turn_lo(dve, B_LN2, whole(lt_a), 8)
            with fori(4) as g:
                for c in range(5):
                    J = Lin(J_MLP + c, [(8, g)])
                    split_lo(dve, J, 4, 6)
                    if c:
                        turn_lo(dve, Lin(B_U + 2 * (c - 1), [(8, g)]), part(lt_b, 4 * (c - 1)), 2)
                    split_lo(dve, J, 6, 12)
                    if c < 4:
                        wait(dve, acc_taken[J.c % 2], J.half() + 1)
                        TT(u_nat[:, c % 2], relu[:, :, :], relu[:, :, :], ALU.mult).then_inc(sg("u_ready"), 1)
                    else:
                        add_job(J, 0, "down_done")
                for c in range(5, 8):
                    J = Lin(J_MLP + c, [(8, g)])
                    splits(J)
                    add_job(J, (c - 4) * NB, "down_done")
            rms_dve(dve, 2, res)
            turn_lo(dve, B_LNF, whole(lt_a), 8)

            dve.wait_ge(sg("f_logit_ready"), 1)
            ch.link(TT(f_t[0], small_ps[:, :, 0:FOX_HEADS], heads_bcast(bf_row, NT), ALU.add))
            STT(f_t[1], f_t[0], -1.0, f_t[0], ALU.mult, ALU.min).then_inc(sg("f_arg_ready"), 1)
            dve.wait_ge(sg("f_ln_done"), 1)
            ch.link(STT(f_logf, f_t[0], 0.0, f_t[1], ALU.min, ALU.subtract))
            with fori(4) as g:
                one = Lin(1, [(1, g)])
                fc = Chain(dve, sg("fox_dve_step"), Lin(0, [(K_FOX_DVE, g)]))
                for kind in range(4):
                    splits(Lin(J_FOX + kind, [(4, g)]))
                wait(dve, acc_taken[1], Lin((J_FOX + 2) // 2 + 1, [(2, g)]))
                wait(dve, acc_taken[0], Lin((J_FOX + 3) // 2 + 1, [(2, g)]))
                copy(f_lg[:, :, :], f_logf[:, :, bass.ds(g * HG, HG)])
                qk = f_nat[:, 0:2].rearrange("p k t (h d) -> p (k t h) d", d=HD)
                sq = at(6144, 16, HD)
                rs = f_rs[:, :, :].rearrange("p a b -> p (a b)")
                ss = f_ss[:, :, :].rearrange("p a b -> p (a b)")
                fc.link(TT(sq, qk, qk, ALU.mult))
                fc.link(nc.vector.tensor_reduce(ss, sq, AX.X, ALU.add))
                TS(ss, ss, 1.0 / HD, NORM_EPS, ALU.mult, ALU.add).then_inc(sg("f_ms_ready"), 1)
                wait(dve, sg("f_rs_ready"), one)
                fc.link(TT(qk, qk, bcast(rs, HD), ALU.mult))
                for kind in range(2):
                    v = f_nat[:, kind].rearrange("p t (h d) -> p (t h) d", d=HD)
                    last = TT(v, v, heads_bcast(fgain[:, kind, :], 8), ALU.mult)
                last.then_inc(sg("fq_ready"), 1)
                wait(dve, sg("f_cum_ready"), one)
                STT(f_bias[:, :, 0:P], mx[:, :, 0:P], -1.0, heads_bcast(f_causal[:, 0:P], HG), ALU.mult, ALU.add)
                STT(f_bias[:, :, P:SEG], mx[:, :, 0:S], -1.0, heads_bcast(f_causal[:, P:SEG], HG), ALU.mult,
                    ALU.add).then_inc(sg("f_bias_ready"), 1)
                wait(dve, sg("f_bias_ready"), one)
                unit_dve(dve, Lin(4, [(1, g)]), fc, f_sc, f_o, f_bias[:, :, :], None, True)
                wait(dve, att["att_out_taken"], Lin(5, [(1, g)]))
                fo = f_o[:, :, :, :].rearrange("p t h d -> p t (h d)")
                TT(fo, fo, f_nat[:, 3], ALU.mult).then_inc(sg("fo_ready"), 1)
                turn_lo(dve, Lin(B_FO, [(2, g)]), part(lt_b, g * HG), 2)
                fc.end(K_FOX_DVE)

            def layer_norm(k):
                for t in range(NT):
                    for c in range(4):
                        last = nc.vector.bn_stats(lnst[:, t, c, :], res[:, t, c * NB:(c + 1) * NB])
                ch.link(last)
                for t in range(NT):
                    last = nc.vector.bn_aggr(lnmv[:, t, :], lnst[:, t, :, :].rearrange("p a b -> p (a b)"))
                ch.link(last)
                TS(lnr, lnmv[:, :, 1], LN_EPS, None, ALU.add).then_inc(sg("ln_ms_ready"), 1)
                dve.wait_ge(sg("ln_rs_ready"), k + 1)
                dve.wait_ge(sg("ln_row_loaded"), 32 * (k + 1))
                for t in range(NT):
                    last = TS(res[:, t, :], res[:, t, :], lnmv[:, t, 0:1], rstd[:, t:t + 1], ALU.subtract, ALU.mult)
                ch.link(last)
                ch.link(TT(res[:, :, :], res[:, :, :], heads_bcast(w_row[:, 0, :], NT), ALU.mult))
                TT(res[:, :, :], res[:, :, :], heads_bcast(w_row[:, 1, :], NT), ALU.add) \
                    .then_inc(sg("ln_done"), 1)

            with fori(2) as i:
                for c in range(2):
                    J = Lin(J_FOXO + c, [(2, i)])
                    splits(J)
                    wait(dve, granules_done, J * GPJ + GPJ)
                    cs = bass.ds(i * (2 * NB) + c * NB, NB)
                    for t in range(NT):
                        last = STT(res[:, t, cs], res[:, t, cs], ALPHA, acc[J.c % 2][t][:, :], ALU.mult, ALU.add)
                    last.then_inc(acc_taken[J.c % 2], 1)
            dve.wait_ge(acc_taken[0], (J_RET - 1) // 2 + 1)
            dve.wait_ge(acc_taken[1], (J_RET - 1) // 2)
            layer_norm(0)
            turn_lo(dve, B_LNG, whole(lt_a), 8)

            dve.wait_ge(sg("ln_done"), 1)
            ch.link(TS(res[:, :, :], res[:, :, :], ALPHA, None, ALU.mult))
            dve.wait_ge(sg("ret_loaded"), 32)
            with fori(2) as h:
                with fori(2) as p:
                    pr = Lin(0, [(2, h), (1, p)])
                    J = Lin(J_RET, [(16, h), (6, p)])
                    rc = Chain(dve, sg("ret_dve_step"), pr * K_RET_DVE)
                    for c in range(6):
                        splits(J + c)
                    wait(dve, acc_taken[1], (J + 5).half())
                    wait(dve, acc_taken[0], (J + 5).half() + 1)
                    for kind in range(2):
                        v = r_nat[:, kind].rearrange("p t (h d) -> p t h d", h=2)
                        x1, x2 = v[:, :, :, 0:P], v[:, :, :, P:2 * P]
                        tmp = [r_tmp[:, i, :].rearrange("p (t h d) -> p t h d", t=NT, h=2) for i in range(4)]

                        def rope(i):
                            a = r_cs[:, i]
                            return bass.AP(tensor=a.tensor, offset=a.offset, ap=[a.ap[0], a.ap[1], [0, 2], a.ap[2]])
                        TT(tmp[0], x1, rope(0), ALU.mult)
                        TT(tmp[1], x2, rope(1), ALU.mult)
                        TT(tmp[2], x1, rope(1), ALU.mult)
                        rc.link(TT(tmp[3], x2, rope(0), ALU.mult))
                        TT(x1, tmp[0], tmp[1], ALU.subtract)
                        rc.link(TT(x2, tmp[2], tmp[3], ALU.add))
                    for hh in range(2):
                        cs = slice(hh * RET_QK, (hh + 1) * RET_QK)
                        hd = h * 4 + p * 2 + hh
                        TS(r_tmp[:, 0, cs], r_nat[:, 0, 1, cs], r_dec[:, 0, bass.ds(hd, 1)], None, ALU.mult)
                        last = TS(r_kd[:, hh, :], r_nat[:, 1, 0, cs], r_dec[:, 1, bass.ds(hd, 1)], None, ALU.mult)
                    last.then_inc(sg("rot_ready"), 1)
                    wait(dve, sg("r_inner"), pr + 1)
                    wait(dve, sg("r_D_loaded"), pr * 16 + 16)
                    for hh in range(2):
                        last = TT(r_in[:, 2 * hh:2 * hh + 2, :],
                                  mx[:, 1, 2 * hh * P:(2 * hh + 2) * P].rearrange("p (t c) -> p t c", c=P),
                                  heads_bcast(r_D[:, hh, :], NT), ALU.mult)
                    last.then_inc(sg("r_in_ready"), 1)
                    for hh in range(2):
                        wait(dve, sg("r_o_ready"), pr * 2 + hh + 1)
                        for t in range(NT):
                            last = nc.vector.bn_stats(r_st[:, t, :], mx[:, t, :])
                        rc.link(last)
                        nc.vector.memset(r_tmp[:, 1, 0:1], 0.0)
                        for t in range(NT):
                            last = nc.vector.bn_aggr(r_mv[:, t, :], r_st[:, t, :])
                        rc.link(last)
                        TS(r_rs, r_mv[:, :, 1], NORM_EPS, None, ALU.add).then_inc(sg("r_ms_ready"), 1)
                        wait(dve, sg("r_rs_ready"), pr * 2 + hh + 1)
                        for t in range(NT):
                            last = TS(r_tmp[:, 2 + t, :], mx[:, t, :], r_mv[:, t, 0:1], r_rs[:, t:t + 1],
                                      ALU.subtract, ALU.mult)
                        last.then_inc(sg("r_o_taken"), 1)
                        wait(dve, sg("r_o_taken"), pr * 2 + hh + 1)
                        rc.link(TT(r_nat[:, 4 + hh], r_tmp[:, 2:4, :], r_nat[:, 4 + hh], ALU.mult))
                    nc.vector.memset(r_tmp[:, 0, 0:1], 0.0).then_inc(sg("r_y_ready"), 1)
                    turn_lo(dve, Lin(B_RO, [(8, h), (4, p)]), part(lt_b, p * 8), 4)
                    rc.end(K_RET_DVE)
                for c in range(4):
                    J = Lin(J_RET + 12 + c, [(16, h)])
                    splits(J)
                    add_job(J, c * NB)
            dve.wait_ge(acc_taken[0], (J_END - 1) // 2 + 1)
            dve.wait_ge(acc_taken[1], (J_END - 1) // 2)
            layer_norm(1)


def t5_bucket(dist):
    n = np.maximum(dist, 0)
    exact = BUCKETS // 2
    nf = np.maximum(n, 1).astype(np.float32)
    large = exact + (np.log(nf / np.float32(exact)) / np.float32(math.log(MAX_DIST / exact))
                     * np.float32(BUCKETS - exact)).astype(np.int32)
    return np.where(n < exact, n, np.minimum(large, BUCKETS - 1))


def constants():
    f = np.float32
    dist = 2 * P - 1 - np.arange(384)
    onehot = (t5_bucket(dist)[None, :] == np.arange(BUCKETS)[:, None]).astype(f)
    c, s = np.arange(P)[:, None], np.arange(P)[None, :]
    masks = []
    for lv in range(LEVELS):
        b = 2 ** lv
        masks.append((c // (2 * b) == s // (2 * b)) & (c // b == s // b + 1))
    same = c // CHUNK == s // CHUNK
    masks += [same & (c > s), same & (c <= s), same, c <= s]
    masks = np.stack(masks).astype(f)
    key = np.concatenate([np.arange(P), np.arange(S) - P])[None, :]
    causal = np.where(key <= np.arange(P)[:, None], 0.0, NEG).astype(f)
    inv = f(10000.0) ** (-np.arange(0, RET_QK, 2, dtype=f) / f(RET_QK))
    ang = np.arange(S, dtype=f)[:, None] * inv[None, :]
    rope = np.stack([np.cos(ang), np.sin(ang)]).astype(f)
    lg = np.log1p(-np.exp2(-5.0 - np.arange(RET_HEADS, dtype=f)).astype(f)).astype(f)
    pos = np.arange(P, dtype=f)
    diff = pos[None, :] - pos[:, None]
    intra = np.where(diff[:, None, :] >= 0, np.exp(np.maximum(diff, 0)[:, None, :] * lg[None, :, None]), 0.0)
    decay = np.stack([np.exp((pos[:, None] + 1) * lg[None, :]), np.exp((P - 1 - pos[:, None]) * lg[None, :])])
    return {"c_onehot": onehot, "c_masks": masks, "c_causal": causal, "c_rope": rope,
            "c_intra": intra.astype(f), "c_decay": decay.astype(f)}


_INS = ["x", "rel_table", "ln1_w", "w_in", "cmp_pe_k", "cmp_pe_v", "cmp_w1_k", "cmp_w2_k", "cmp_w1_v",
        "cmp_w2_v", "conv_w", "a_log", "dt_bias", "gdn_norm_w", "w_pa", "w_pb", "w_o", "ln2_w", "w_up",
        "w_down", "ln_f_w", "fox_w_in_2", "fox_b_f_2", "fox_q_gain_2", "fox_k_gain_2", "fox_w_out_2",
        "ret_w_in_2", "ret_w_out_2", "ln_gain_2", "ln_bias_2"]


def kernel(**inputs):
    import concourse.bacc as bacc
    from concourse.bass_utils import run_bass_kernel_spmd

    nc = bacc.Bacc("TRN2", target_bir_lowering=False, num_devices=1)
    arrays, args = {}, []

    def add(name, a):
        arrays[name] = a
        args.append(nc.dram_tensor(name, a.shape, mybir.dt.from_np(a.dtype), kind="ExternalInput").ap())

    for name in _INS:
        a = np.ascontiguousarray(inputs[name])
        if a.ndim > 1 and a.shape[0] == 1:
            a = a[0]
        add("in_" + name, a)
    for name, a in constants().items():
        add(name, np.ascontiguousarray(a))
    args.append(nc.dram_tensor("out_x", (S, D), F32, kind="ExternalOutput").ap())
    build(nc, *args)
    r = run_bass_kernel_spmd(nc, [arrays], core_ids=[0])
    return r.results[0]["out_x"].reshape(1, S, D)
```

```python
import math
from contextlib import ExitStack

import numpy as np

import concourse.bass as bass
from concourse import mybir

F32 = mybir.dt.float32
F32R = mybir.dt.float32r
ALU = mybir.AluOpType
ACT = mybir.ActivationFunctionType
AX = mybir.AxisListType

P = 128
S = 256
NT = S // P
D = 2048
KT = D // P
NB = 512
GPJ = 8
CPJ = 4
HD = 128
NH = 8
HG = 4
CMP_BLOCK, CMP_STRIDE = 32, 16
NCMP = S // CMP_STRIDE - 1
NC0 = (P - CMP_BLOCK) // CMP_STRIDE + 1
NKV = 2
CMP_HIDDEN = 256
BUCKETS, MAX_DIST = 32, 128
CHUNK = 64
LEVELS = 6
FOX_HEADS = 16
RET_HEADS, RET_QK, RET_V = 8, 256, 512
NEG = -1e30
NORM_EPS, LN_EPS = 1e-6, 1e-5
ALPHA = (2.0 * 2) ** 0.25
SEG = P + S
SEGC = SEG + NC0 + NCMP
ATT_SCALE = HD ** -0.5

C_NSA = 0
C_GATE = NH * HD + 6 * NKV * HD
C_GDN = C_GATE + 3 * NH
C_AB = C_GDN + 4 * NH * HD
C_MERGE = C_AB + 2 * NH

J_NSA = 0
J_CMP = J_NSA + (NH * HD + 6 * NKV * HD) // NB
J_GDN = J_CMP + 2
J_MERGE = J_GDN + 8
J_PAB = J_MERGE + 8
J_WO = J_PAB + 4
J_MLP = J_WO + 4
J_FOX = J_MLP + 32
J_FOXO = J_FOX + 16
J_RET = J_FOXO + 4
J_END = J_RET + 32


class Lin:

    def __init__(self, c, terms=()):
        self.c, self.terms = c, tuple(terms)

    def __add__(self, k):
        if isinstance(k, Lin):
            return Lin(self.c + k.c, self.terms + k.terms)
        return Lin(self.c + k, self.terms)

    def __sub__(self, k):
        return Lin(self.c - k, self.terms)

    def __mul__(self, k):
        return Lin(self.c * k, [(a * k, v) for a, v in self.terms])

    def half(self):
        assert all(a % 2 == 0 for a, _ in self.terms)
        return Lin(self.c // 2, [(a // 2, v) for a, v in self.terms])

    def value(self):
        v = self.c
        for a, r in self.terms:
            v = r * a + v
        return v


def lin(i):
    return i if isinstance(i, Lin) else Lin(0, [(1, i)]) if not isinstance(i, int) else Lin(i)


def wait(eng, sem, n):
    n = lin(n)
    assert n.c > 0 or not n.terms, "a wait against a register that is 0 in the first round"
    if n.c > 0:
        eng.wait_ge(sem, n.value())


class Chain:

    def __init__(self, eng, sem, start=0):
        self.eng, self.sem, self.start, self.k = eng, sem, lin(start), 0

    def link(self, ins):
        ins.then_inc(self.sem, 1)
        self.k += 1
        wait(self.eng, self.sem, self.start + self.k)

    def end(self, k):
        assert self.k == k, f"the chain has {self.k} steps, not {k}"


K_FOX_DVE, K_RET_DVE = 9, 8


def build(nc, x, rel_table, ln1_w, w_in, pe_k, pe_v, w1_k, w2_k, w1_v, w2_v, conv_w, a_log, dt_bias,
          gdn_norm_w, w_pa, w_pb, w_o, ln2_w, w_up, w_down, ln_f_w, fox_w_in, fox_b_f, fox_q_gain,
          fox_k_gain, fox_w_out, ret_w_in, ret_w_out, ln_gain, ln_bias,
          c_onehot, c_masks, c_causal, c_rope, c_intra, c_decay, out):
    ctx = ExitStack()
    with ctx:
        def sb(name, shape, dt=F32):
            return ctx.enter_context(nc.sbuf_tensor(name, shape, dt))

        def sem(name):
            return ctx.enter_context(nc.semaphore(name))

        raw = sb("raw", [P, CPJ, 4, NB])
        w_hi = sb("w_hi", [P, 4, 2, NB], F32R)
        w_lo = sb("w_lo", [P, 4, 2, NB], F32R)
        lt_a = [sb("lt_a_hi", [P, KT, S], F32R), sb("lt_a_lo", [P, KT, S], F32R)]
        lt_b = [sb("lt_b_hi", [P, KT, S], F32R), sb("lt_b_lo", [P, KT, S], F32R)]
        res = sb("res", [P, NT, D])
        ARENA = 14592
        arena = sb("arena", [P, ARENA])
        ident = sb("ident", [P, P])
        w2 = sb("w2", [P, 2, 2, HD])
        cwt = sb("cwt", [P, 4 * 24])
        pet = sb("pet", [P, 2, CMP_BLOCK])
        gnorm = sb("gnorm", [P, HD])
        fgain = sb("fgain", [P, 2, HD])
        gates = sb("gates", [P, NT, 3 * NH])
        sm = sb("sm", [P, 320])

        def at(off, *shape):
            n = math.prod(shape)
            assert off + n <= ARENA, (off, shape)
            v = arena[:, off:off + n]
            if len(shape) == 2:
                v = v.rearrange("p (a b) -> p a b", b=shape[1])
            if len(shape) == 3:
                v = v.rearrange("p (a b c) -> p a b c", b=shape[1], c=shape[2])
            if len(shape) == 4:
                v = v.rearrange("p (a b c d) -> p a b c d", b=shape[1], c=shape[2], d=shape[3])
            return v

        used = [0]

        def small(*shape):
            n = math.prod(shape)
            v = sm[:, used[0]:used[0] + n]
            used[0] += n
            assert used[0] <= 320
            if len(shape) == 2:
                v = v.rearrange("p (a b) -> p a b", b=shape[1])
            if len(shape) == 3:
                v = v.rearrange("p (a b c) -> p a b c", b=shape[1], c=shape[2])
            return v

        mhalf = small(32)
        ssum = small(NT)
        rstd = small(NT)
        a_row = small(NH)
        dt_row = small(NH)
        bf_row = small(FOX_HEADS)
        lnst = small(NT, 4, 6)
        lnmv = small(NT, 2)
        lnr = small(NT)

        acc = [[ctx.enter_context(nc.psum_tensor(f"acc{a}{t}", [P, NB], F32)) for t in range(NT)]
               for a in range(2)]
        mx = ctx.enter_context(nc.psum_tensor("mx", [P, 4, NB], F32))

        raw_loaded = [sem(f"raw_loaded{i}") for i in range(CPJ)]
        hi_ready = sem("hi_ready")
        lo_ready = sem("lo_ready")
        granules_done = sem("granules_done")
        acc_taken = [sem("acc_taken0"), sem("acc_taken1")]
        lt_turned = sem("lt_turned")
        lt_hi_ready = sem("lt_hi_ready")
        lt_lo_ready = sem("lt_lo_ready")
        S_ = {}

        def sg(name):
            if name not in S_:
                S_[name] = sem(name)
            return S_[name]

        names = ("const_loaded x_loaded w_loaded ident_ready row_loaded toep_loaded toep_stored store_done "
                 "sq_done ms_ready rstd_ready h_ready").split()
        for n in names:
            sg(n)

        block = ctx.enter_context(nc.Block())

        def load_job(sp, J, src, rows=512, chunks=CPJ):
            J = lin(J)
            for q in range(chunks):
                wait(sp, lo_ready, J * GPJ + 2 * q + 2 - GPJ)
                w = src(q)
                sp.dma_start(raw[:, q, :, :].rearrange("p a b -> p (a b)").rearrange(
                    "p (j n) -> p j n", j=rows // P), w.rearrange("(j p) n -> p j n", p=P)) \
                    .then_inc(raw_loaded[q], 16)

        def block_of(w, row0, col):
            def src(q):
                r = row0 + q * 512 if isinstance(row0, int) else row0 + q * 512
                rs = slice(r, r + 512) if isinstance(r, int) else bass.ds(r, 512)
                cs = slice(col, col + NB) if isinstance(col, int) else bass.ds(col, NB)
                return w[rs, cs]
            return src

        def split_hi(act, J, r0, r1):
            J = lin(J)
            for r in range(r0, r1):
                slot, half = (r % GPJ) // 2, r % 2
                if half == 0:
                    wait(act, raw_loaded[slot], (J + (1 + r // GPJ)) * 16)
                wait(act, granules_done, J * GPJ + r - 3)
                nc.scalar.activation(w_hi[:, r % 4], raw[:, slot, 2 * half:2 * half + 2, :],
                                     ACT.Copy).then_inc(hi_ready, 1)

        def split_lo(dve, J, r0, r1):
            J = lin(J)
            for r in range(r0, r1):
                slot, half = (r % GPJ) // 2, r % 2
                wait(dve, hi_ready, J * GPJ + r + 1)
                nc.vector.tensor_tensor(w_lo[:, r % 4], raw[:, slot, 2 * half:2 * half + 2, :],
                                        w_hi[:, r % 4].bitcast(F32), ALU.subtract) \
                    .then_inc(lo_ready, 1)

        def ahead(J):
            return GPJ + 4

        def multiply(pe, J, lt, par, hook=None, free=None, mix=None):
            J = lin(J)
            assert J.c % 2 == par
            if free is None:
                wait(pe, acc_taken[par], J.half())
            else:
                wait(pe, *free)
            for r in range(GPJ):
                if hook:
                    hook(r)
                step(mix)
                wait(pe, lo_ready, J * GPJ + r + 1)
                for k in range(2):
                    kt = 2 * r + k
                    hi, lo = w_hi[:, r % 4, k, :], w_lo[:, r % 4, k, :]
                    for t in range(NT):
                        a_hi = lt[0][:, kt, t * P:(t + 1) * P]
                        a_lo = lt[1][:, kt, t * P:(t + 1) * P]
                        o = acc[par][t][:, :]
                        nc.tensor.matmul(o, a_hi, hi, start=(kt == 0), stop=False)
                        nc.tensor.matmul(o, a_hi, lo, start=False, stop=False)
                        last = nc.tensor.matmul(o, a_lo, hi, start=False, stop=(kt == KT - 1))
                last.then_inc(granules_done, 1)

        def step(mix):
            if mix is not None:
                next(mix, None)

        def split_job(split, eng, J, mix=None):
            for r in range(GPJ):
                step(mix)
                split(eng, J, r + 4, r + 5)

        def take(eng, J, par, ops):
            wait(eng, granules_done, lin(J) * GPJ + GPJ)
            for t in range(NT):
                last = ops(t)
            last.then_inc(acc_taken[par], 1)

        def turn(pe, B, src, n):
            B = lin(B)
            wait(pe, lt_lo_ready, B)
            for b in range(n):
                if b >= 4:
                    wait(pe, lt_lo_ready, B + b - 3)
                for c in range(2):
                    for t in range(NT):
                        last = nc.tensor.transpose(mx[:, b % 4, (2 * c + t) * P:(2 * c + t + 1) * P],
                                                   src(2 * b + c, t), ident[:, :])
                last.then_inc(lt_turned, 1)

        def turn_hi(act, B, dst, n):
            B = lin(B)
            for b in range(n):
                wait(act, lt_turned, B + b + 1)
                nc.scalar.activation(dst(b)[0], mx[:, b % 4, :].rearrange("p (c s) -> p c s", s=S),
                                     ACT.Copy).then_inc(lt_hi_ready, 1)

        def turn_lo(dve, B, dst, n):
            B = lin(B)
            for b in range(n):
                wait(dve, lt_hi_ready, B + b + 1)
                hi, lo = dst(b)
                nc.vector.tensor_tensor(lo, mx[:, b % 4, :].rearrange("p (c s) -> p c s", s=S),
                                        hi.bitcast(F32), ALU.subtract).then_inc(lt_lo_ready, 1)

        def whole(lt):
            return lambda b: (lt[0][:, 2 * b:2 * b + 2, :], lt[1][:, 2 * b:2 * b + 2, :])

        def part(lt, kt):
            return lambda b: (lt[0][:, bass.ds(kt + 2 * b, 2), :], lt[1][:, bass.ds(kt + 2 * b, 2), :])

        B_LN1, B_OA = 0, 8
        B_OB = B_OA + 4
        B_Y = B_OB + 4
        B_LN2 = B_Y + 8
        B_U = B_LN2 + 8
        B_LNF = B_U + 32
        B_FO = B_LNF + 8
        B_LNG = B_FO + 8
        B_RO = B_LNG + 8

        h_nat = at(0, NT, D)
        w_row = at(NT * D, 2, D)

        def rms_act(act, k):
            for t in range(NT):
                last = nc.scalar.activation(h_nat[:, t, :], res[:, t, :], ACT.Square,
                                            accum_out=ssum[:, t:t + 1])
            last.then_inc(sg("sq_done"), 1)

        def rms_dve(dve, k, dst):
            dve.wait_ge(sg("sq_done"), k + 1)
            nc.vector.tensor_scalar(ssum, ssum, 1.0 / D, NORM_EPS, ALU.mult, ALU.add) \
                .then_inc(sg("ms_ready"), 1)
            dve.wait_ge(sg("rstd_ready"), k + 1)
            dve.wait_ge(sg("row_loaded"), 16 * k) if k else dve.wait_ge(sg("first_row_loaded"), 16)
            for t in range(NT):
                last = nc.vector.scalar_tensor_tensor(dst[:, t, :], res[:, t, :], rstd[:, t:t + 1],
                                                      w_row[:, 0, :], ALU.mult, ALU.mult)
            last.then_inc(sg("h_ready"), 1)

        def root_pool(pool, src_ready, n, base, dst, w, done):
            wait(pool, src_ready, n)
            nc.gpsimd.tensor_tensor(dst, base, mhalf[:, 0:w], ALU.pow).then_inc(done, 1)

        nat = at(0, 5, NT, NB)
        T = at(5120, 16, S)
        bm = at(9216, NH, SEGC)
        sc = at(0, HG, SEG)
        scc = at(1536, HG, NC0 + NCMP)
        pt = at(12464, HG, SEG)
        o_nat = at(5120 + 8 * S, NT, HG, HD)
        blk = at(2 * 1024, 960)
        wsmall = at(12464, KT, 40)
        onehot = at(9216, 384)
        tabl = at(9216 + 384, NH)
        distb = at(9216 + 400, 384)
        pe_nat = at(14000, 2, HD)
        cw_nat = at(14000 + 256, HD)
        cmp_hid = at(2048 + 0, 2, CMP_HIDDEN)
        cmp_hT = at(2048 + 512, 4, NKV * NCMP)
        kcT = at(2048 + 632, NKV * NCMP)
        vc = at(2048 + 662, NKV, HD)
        cb = [lt.rearrange("p a b -> p (a b)")[:, 0:2 * 960].rearrange("p (v n) -> p v n", v=2)
              for lt in (lt_b[0][:, :, :], lt_b[1][:, :, :])]
        mask0 = small(NC0)
        rowmax = small(4, HG)
        esum = small(4, HG)
        coef = small(3, NT, HG)
        att = {n: sg(n) for n in ("scores_ready scores_taken rowmax_ready exp_done probs_turned probs_copied "
                                  "att_out_ready att_out_taken").split()}

        def unit_pe(pe, u, sc, pt, q, k, v):
            u = lin(u)
            wait(pe, att["att_out_taken"], u)
            for j in range(HG):
                nc.tensor.matmul(mx[:, j, 0:P], q(j)[:, 0:P], k(j)[:, 0:P], start=True, stop=True)
                last = nc.tensor.matmul(mx[:, j, P:SEG], q(j)[:, P:S], k(j), start=True, stop=True)
            last.then_inc(att["scores_ready"], 1)
            yield
            yield
            yield
            yield
            wait(pe, att["exp_done"], u + 1)
            for j in range(HG):
                for b in range(3):
                    last = nc.tensor.transpose(mx[:, j, b * P:(b + 1) * P], sc[:, j, b * P:(b + 1) * P],
                                               ident[:, :])
            last.then_inc(att["probs_turned"], 1)
            yield
            wait(pe, att["probs_copied"], u + 1)
            for j in range(HG):
                nc.tensor.matmul(mx[:, 0, j * HD:(j + 1) * HD], pt[:, j, 0:P], v(j, 0), start=True, stop=True)
                nc.tensor.matmul(mx[:, 1, j * HD:(j + 1) * HD], pt[:, j, P:S], v(j, 0), start=True, stop=False)
                last = nc.tensor.matmul(mx[:, 1, j * HD:(j + 1) * HD], pt[:, j, S:SEG], v(j, 1),
                                        start=False, stop=True)
            last.then_inc(att["att_out_ready"], 1)
            yield

        def unit_act(act, u, sc, pt):
            u = lin(u)
            yield
            yield
            wait(act, att["rowmax_ready"], u + 1)
            for t, (a, b) in enumerate(((0, P), (P, SEG))):
                for j in range(HG):
                    last = nc.scalar.activation(sc[:, j, a:b], sc[:, j, a:b], ACT.Exp,
                                                bias=rowmax[:, t, j:j + 1], accum_out=esum[:, t, j:j + 1])
                if t == 0:
                    yield
            last.then_inc(att["exp_done"], 1)
            yield
            wait(act, att["probs_turned"], u + 1)
            nc.scalar.activation(pt[:, :, :], mx[:, :, 0:SEG], ACT.Copy).then_inc(att["probs_copied"], 1)
            yield
            yield

        def unit_dve(dve, u, ch, sc, o_nat, bias, gate, first):
            u = lin(u)
            wait(dve, att["scores_ready"], u + 1)
            ch.link(nc.vector.scalar_tensor_tensor(sc[:, :, :], mx[:, :, 0:SEG], ATT_SCALE, bias,
                                                   ALU.mult, ALU.add))
            yield
            nc.vector.tensor_reduce(rowmax[:, 0, :], sc[:, :, 0:P], AX.X, ALU.max, negate=True)
            nc.vector.tensor_reduce(rowmax[:, 1, :], sc[:, :, P:SEG], AX.X, ALU.max, negate=True) \
                .then_inc(att["rowmax_ready"], 1)
            yield
            yield
            yield
            wait(dve, att["exp_done"], u + 1)
            ch.link(nc.vector.tensor_scalar(coef[:, 0], esum[:, 0:2], 1e-30, None, ALU.max))
            ch.link(nc.vector.reciprocal(coef[:, 1], coef[:, 0]))
            if gate is None:
                gate = coef[:, 1]
            else:
                ch.link(nc.vector.tensor_tensor(coef[:, 2], coef[:, 1], gate, ALU.mult))
                gate = coef[:, 2]
            yield
            wait(dve, att["att_out_ready"], u + 1)
            for t in range(NT):
                for j in range(HG):
                    o = o_nat[:, t, j, :]
                    ps = mx[:, t, j * HD:(j + 1) * HD]
                    c = gate[:, t, j:j + 1]
                    if first:
                        last = nc.vector.tensor_scalar(o, ps, c, None, ALU.mult)
                    else:
                        last = nc.vector.scalar_tensor_tensor(o, ps, c, o, ALU.mult, ALU.add)
            last.then_inc(att["att_out_taken"], 1)
            wait(dve, att["att_out_taken"], u + 1)
            yield

        g_nat = res[:, :, :].rearrange("p a b -> p (a b)").rearrange("p (k t n) -> p k t n", k=4, t=NT)
        g_z = at(3072, NT, NB)
        g_ct = at(4096, 12, 260)
        g_cv = at(7216, 12, S)
        g_rn = at(10288, NT, 12, HD)
        g_mask = at(13360, LEVELS + 3, P)
        M_STRICT, M_TRI, M_ONES = LEVELS, LEVELS + 1, LEVELS + 2
        g_sq = at(4096, NT, 8, HD)
        g_vb, g_kbeg, g_kdec = (at(i * 1024, NT, HG, HD) for i in range(3))
        g_qg = at(4096 + 2048, NT, HG, HD)
        g_qT, g_kT, g_qgT = (at(7216 + i * 1024, HG, S) for i in range(3))
        g_dec, g_qkT, g_A = (at(10288 + i * 1024, HG * NT, P) for i in range(3))
        g_X, g_Y, g_P1 = (at(4096 + i * 1024, HG * NT, P) for i in range(3))
        g_U = g_dec
        g_wT = g_A
        g_o = at(4096, NT, HG, HD)
        g_S = at(4096 + 2048, HG, HD)
        g_V = at(4096 + 2048 + 512, HG, HD)
        G_G, G_BETA, G_CUM, G_E, G_KD, G_BEG = range(6)
        tok = sb("tok", [P, 6, NT, NH])
        tg = sb("tg", [P, 6, NT, HG])
        cwg = sb("cwg", [P, 12, HG])
        gss = small(NT, 8)
        grs = small(NT, 8)
        egl = small(HG * NT, 2)
        gt = [small(NT, NH) for _ in range(3)]

        f_nat = at(0, 4, NT, NB)
        f_T = at(4096, 8, S)
        f_sc = at(6144, HG, SEG)
        f_pt = at(7680, HG, SEG)
        f_o = at(9216, NT, HG, HD)
        f_bias = at(10240, HG, SEG)
        f_causal = at(11776, SEG)
        f_logf = at(12160, NT, FOX_HEADS)
        f_lg = at(12192, NT, HG)
        f_ones = at(12208, P)
        f_t = [at(12336 + 32 * i, NT, FOX_HEADS) for i in range(3)]
        f_w = at(12448, KT, FOX_HEADS)
        f_ss = at(12704, NT, 8)
        f_rs = at(12720, NT, 8)
        tri = at(12736, P)

        mg_a = g_nat
        mg_b = at(4096, 4, NT, NB)
        y_nat = at(8192, NT, D)
        y_tmp = at(12288, NT, NB)
        relu = at(0, NT, NB)
        u_nat = at(1024, 2, NT, NB)

        r_nat = at(0, 6, NT, NB)
        r_T = at(6144, 8, S)
        r_qdT = at(8192, HG, P)
        r_kd = at(8704, 2, RET_QK)
        r_in = at(9216, 4, P)
        r_R = at(9728, 4, RET_V)
        r_D = at(11776, 2, P)
        r_cs = at(12032, 2, NT, P)
        r_tmp = at(12544, 4, NT * 2 * P)
        r_dec = small(2, RET_HEADS)
        r_st = small(NT, 6)
        r_mv = small(NT, 2)
        r_rs = small(NT)

        bias_dram = nc.dram_tensor("bias_by_distance", [NH, P, 384], F32).ap()

        def bcast(ap, n):
            return bass.AP(tensor=ap.tensor, offset=ap.offset, ap=[*ap.ap, [0, n]])

        def heads_bcast(ap, n):
            return bass.AP(tensor=ap.tensor, offset=ap.offset, ap=[ap.ap[0], [0, n], *ap.ap[1:]])

        N_CONST = 15
        NSA_ORDER = [4, 5, 0, 1, 2, 3, 6, 7]
        NSA_TILES = [(i // 4, i % 4) for i in range(8)] + [(2, 0), (2, 1), (2, 2), (2, 3), (3, 0), (3, 1),
                                                          (4, 0), (4, 1)]
        small_ps = mx[:, 0, 0:128].rearrange("p (t n) -> p t n", t=NT)

        @block.sync
        def _(sp):
            def fori(n):
                return sp.Fori(0, n)
            sp.dma_start(res[:, :, :], x.rearrange("(t p) d -> p t d", p=P)).then_inc(sg("x_loaded"), 16)
            sp.dma_start(w_row[:, 0, :], ln1_w.partition_broadcast(P)).then_inc(sg("first_row_loaded"), 16)
            load_job(sp, 0, block_of(w_in, 0, C_NSA))
            with fori(2) as i:
                for c in range(2):
                    load_job(sp, Lin(1 + c, [(2, i)]), block_of(w_in, 0, i * (2 * NB) + (C_NSA + (1 + c) * NB)))
            for c, w in enumerate((w1_k, w1_v)):
                load_job(sp, J_CMP + c, lambda q, w=w: w[q * 1024:(q + 1) * 1024, :], rows=1024)
            with fori(2) as g:
                for kind in range(4):
                    load_job(sp, Lin(J_GDN + kind, [(4, g)]),
                             block_of(w_in, 0, g * NB + (C_GDN + kind * NH * HD)))
            with fori(4) as i:
                for c in range(2):
                    load_job(sp, Lin(J_MERGE + c, [(2, i)]), block_of(w_in, 0, i * (2 * NB) + (C_MERGE + c * NB)))
            with fori(2) as i:
                for c in range(2):
                    col = i * (2 * NB) + c * NB
                    load_job(sp, Lin(J_PAB + c, [(2, i)]),
                             lambda q, col=col: (w_pa, w_pb)[q // 2][(q % 2) * 512:(q % 2 + 1) * 512,
                                                                    bass.ds(col, NB)])
            with fori(2) as i:
                for c in range(2):
                    load_job(sp, Lin(J_WO + c, [(2, i)]), block_of(w_o, 0, i * (2 * NB) + c * NB))
            with fori(4) as g:
                for c in range(4):
                    load_job(sp, Lin(J_MLP + c, [(8, g)]), block_of(w_up, 0, g * D + c * NB))
                for c in range(4):
                    load_job(sp, Lin(J_MLP + 4 + c, [(8, g)]), block_of(w_down, g * D, c * NB))
            with fori(4) as g:
                for kind in range(4):
                    load_job(sp, Lin(J_FOX + kind, [(4, g)]), block_of(fox_w_in, 0, g * NB + kind * D))
            with fori(2) as i:
                for c in range(2):
                    load_job(sp, Lin(J_FOXO + c, [(2, i)]), block_of(fox_w_out, 0, i * (2 * NB) + c * NB))
            with fori(2) as h:
                with fori(2) as p:
                    J = Lin(J_RET, [(16, h), (6, p)])
                    load_job(sp, J, block_of(ret_w_in, 0, h * 1024 + p * NB))
                    load_job(sp, J + 1, block_of(ret_w_in, 0, h * 1024 + p * NB + D))
                    for c in range(4):
                        load_job(sp, J + 2 + c, block_of(ret_w_in, 0, h * 2048 + p * 1024
                                                         + (2 * D + (c // 2) * 2 * D + (c % 2) * NB)))
                for c in range(4):
                    load_job(sp, Lin(J_RET + 12 + c, [(16, h)]), block_of(ret_w_out, h * D, c * NB))
            load_job(sp, J_END, block_of(ret_w_out, 0, 0), chunks=2)
            sp.wait_ge(sg("ln_done"), 2)
            sp.dma_start(out.rearrange("(t p) d -> p t d", p=P), res[:, :, :]).then_inc(sg("store_done"), 16)
            sp.wait_ge(sg("store_done"), 16)

        @block.gpsimd
        def _(pool):
            def fori(n):
                return pool.Fori(0, n)
            ch = Chain(pool, sg("pool_step"))

            def load(dst, src, s, n=None):
                pool.dma_start(dst, src).then_inc(sg(s), 16)

            ch.link(nc.gpsimd.memset(ident[:, :], 0.0))
            nc.gpsimd.affine_select(out=ident[:, :], in_=ident[:, :], compare_op=ALU.not_equal, fill=1.0,
                                    base=0, pattern=[[-1, P]], channel_multiplier=1) \
                .then_inc(sg("ident_ready"), 1)
            ch.link(nc.gpsimd.memset(mhalf, -0.5))
            ch.link(nc.gpsimd.memset(mask0, 1.0))
            ch.link(nc.gpsimd.affine_select(out=mask0, in_=mask0, compare_op=ALU.is_ge, fill=0.0,
                                            base=-(CMP_BLOCK - 1), pattern=[[-CMP_STRIDE, NC0]],
                                            channel_multiplier=1))
            root_pool(pool, sg("ms_ready"), 1, ssum, rstd, NT, sg("rstd_ready"))

            pool.wait_ge(sg("prep_taken"), 1)
            src = distb[0:NH, :]
            pool.dma_start(bias_dram, bass.AP(tensor=src.tensor, offset=src.offset,
                                              ap=[src.ap[0], [0, P], src.ap[1]])).then_inc(sg("toep_stored"), 16)
            pool.wait_ge(sg("toep_stored"), 16)
            for a, b, off in ((0, P, 2 * P - 1), (P, SEG, P - 1)):
                src = bass.AP(tensor=bias_dram.tensor, offset=off, ap=[[384 - 1, P], [384 * P, NH], [1, b - a]])
                pool.dma_start(bm[:, :, a:b], src).then_inc(sg("toep_loaded"), 16)
            pool.wait_ge(sg("toep_loaded"), 32)
            nc.gpsimd.affine_select(out=bm[:, :, 0:P], in_=bm[:, :, 0:P], compare_op=ALU.is_ge, fill=NEG,
                                    base=0, pattern=[[0, NH], [-1, P]], channel_multiplier=1) \
                .then_inc(sg("bias_masked"), 1)
            nc.gpsimd.affine_select(out=bm[:, :, P:SEG], in_=bm[:, :, P:SEG], compare_op=ALU.is_ge, fill=NEG,
                                    base=P, pattern=[[0, NH], [-1, S]], channel_multiplier=1) \
                .then_inc(sg("bias_masked"), 1)
            pool.wait_ge(lt_lo_ready, B_OB)
            load(g_mask[:, :, :], c_masks[0:LEVELS + 3].rearrange("m p c -> p m c"), "mask_loaded")
            with fori(2) as g:
                root_pool(pool, sg("gss_ready"), Lin(1, [(2, g)]),
                          gss.rearrange("p a b -> p (a b)"), grs.rearrange("p a b -> p (a b)"), 16,
                          sg("grs_ready"))
                root_pool(pool, sg("gss_ready"), Lin(2, [(2, g)]),
                          gss.rearrange("p a b -> p (a b)")[:, 0:8],
                          grs.rearrange("p a b -> p (a b)")[:, 0:8], 8, sg("grs_ready"))
            pool.wait_ge(sg("y_ready"), 1)
            load(res[:, :, :], x.rearrange("(t p) d -> p t d", p=P), "x_again")
            load(w_row[:, 0, :], ln2_w.partition_broadcast(P), "row_loaded")
            root_pool(pool, sg("ms_ready"), 2, ssum, rstd, NT, sg("rstd_ready"))
            pool.wait_ge(sg("h_ready"), 2)
            load(w_row[:, 0, :], ln_f_w.partition_broadcast(P), "row_loaded")
            root_pool(pool, sg("ms_ready"), 3, ssum, rstd, NT, sg("rstd_ready"))
            pool.wait_ge(sg("h_ready"), 3)
            load(f_causal, c_causal, "fox_loaded")
            load(tri, c_masks[LEVELS + 3], "fox_loaded")
            load(f_w, fox_w_in[:, 4 * D:4 * D + FOX_HEADS].rearrange("(k p) n -> p k n", p=P), "fox_loaded")
            nc.gpsimd.memset(f_ones[:, :], 1.0).then_inc(sg("f_ones_ready"), 1)
            with fori(4) as g:
                for kind in range(2):
                    root_pool(pool, sg("f_ms_ready"), Lin(kind + 1, [(2, g)]), f_ss[:, kind, :], f_rs[:, kind, :],
                              8, sg("f_rs_ready"))
            pool.wait_ge(sg("fo_ready"), 4)
            for i in range(2):
                load(w_row[:, i, :], (ln_gain, ln_bias)[i][0, :].partition_broadcast(P), "ln_row_loaded")
            root_pool(pool, sg("ln_ms_ready"), 1, lnr, rstd, NT, sg("ln_rs_ready"))
            pool.wait_ge(sg("ln_done"), 1)
            load(r_cs[:, :, :, :], c_rope.rearrange("a (t p) n -> p a t n", p=P), "ret_loaded")
            load(r_dec, c_decay.rearrange("a p n -> p a n"), "ret_loaded")
            with fori(2) as h:
                with fori(2) as p:
                    pr = Lin(0, [(2, h), (1, p)])
                    wait(pool, acc_taken[1], Lin(J_RET, [(16, h), (6, p)]).half() + 1)
                    pool.dma_start(r_D[:, :, :], c_intra[:, bass.ds(h * 4 + p * 2, 2), :]) \
                        .then_inc(sg("r_D_loaded"), 16)
                    for hh in range(2):
                        root_pool(pool, sg("r_ms_ready"), pr * 2 + (hh + 1), r_rs, r_rs, NT,
                                  sg("r_rs_ready"))
            for i in range(2):
                if i == 0:
                    pool.wait_ge(lt_lo_ready, B_RO + 16)
                load(w_row[:, i, :], (ln_gain, ln_bias)[i][1, :].partition_broadcast(P), "ln_row_loaded")
            root_pool(pool, sg("ln_ms_ready"), 2, lnr, rstd, NT, sg("ln_rs_ready"))

        @block.scalar
        def _(act):
            A = nc.scalar.activation

            def fori(n):
                return act.Fori(0, n)

            loads = [(onehot[0:BUCKETS, :], c_onehot), (tabl[0:BUCKETS, :], rel_table),
                     (cw_nat[0:96, :], conv_w.rearrange("w (c p) -> (w c) p", p=P)),
                     (pe_nat[0:CMP_BLOCK, 0, :], pe_k), (pe_nat[0:CMP_BLOCK, 1, :], pe_v),
                     (wsmall[:, :, 0:24], w_in[:, C_GATE:C_GDN].rearrange("(k p) n -> p k n", p=P)),
                     (wsmall[:, :, 24:40], w_in[:, C_AB:C_MERGE].rearrange("(k p) n -> p k n", p=P)),
                     (w2[:, 0, :, :], w2_k.rearrange("(c p) n -> p c n", p=P)),
                     (w2[:, 1, :, :], w2_v.rearrange("(c p) n -> p c n", p=P)),
                     (a_row, a_log.partition_broadcast(P)), (dt_row, dt_bias.partition_broadcast(P)),
                     (bf_row, fox_b_f.partition_broadcast(P)), (gnorm[:, :], gdn_norm_w.partition_broadcast(P)),
                     (fgain[:, 0, :], fox_q_gain.partition_broadcast(P)),
                     (fgain[:, 1, :], fox_k_gain.partition_broadcast(P))]
            for dst, src in loads:
                act.dma_start(dst, src).then_inc(sg("const_loaded"), 16)
            assert N_CONST == len(loads)

            act.wait_ge(sg("x_loaded"), 16)
            rms_act(act, 0)
            split_hi(act, 0, 0, 4)
            turn_hi(act, B_LN1, whole(lt_a), 8)
            act.wait_ge(sg("gates_ready"), 1)
            A(gates[:, :, :], small_ps[:, :, 0:24], ACT.Sigmoid)
            A(gt[1], small_ps[:, :, 24:32], ACT.Copy)
            A(tok[:, G_BETA], small_ps[:, :, 32:40], ACT.Sigmoid).then_inc(sg("gates_done"), 1)
            act.wait_ge(sg("softplus_arg"), 1)
            act.wait_ge(sg("const_loaded"), 16 * N_CONST)
            A(gt[0], gt[0], ACT.Exp).then_inc(sg("act_step"), 1)
            act.wait_ge(sg("act_step"), 1)
            A(gt[0], gt[0], ACT.Ln, bias=1.0)
            A(a_row, a_row, ACT.Exp).then_inc(sg("softplus_done"), 1)

            def copy_job(J, dst, func=ACT.Copy, scale=1.0, mix=None):
                split_job(split_hi, act, J, mix)
                take(act, J, lin(J).c % 2, lambda t: A(dst(t), acc[lin(J).c % 2][t][:, :], func, scale=scale))

            copy_job(0, lambda t: nat[:, 0, t, :])
            with fori(2) as i:
                for c in range(2):
                    copy_job(Lin(1 + c, [(2, i)]),
                             lambda t: nat[:, bass.ds(i * 2 + (1 + c), 1), t, :].rearrange("p a n -> p (a n)"))
            for n, b in enumerate(NSA_ORDER):
                act.wait_ge(sg("nsa_turned"), n + 1)
                A(T[:, 2 * b:2 * b + 2, :], mx[:, n % 4, :].rearrange("p (c s) -> p c s", s=S),
                  ACT.Copy).then_inc(sg("nsa_copied"), 1)
            for kv in range(2):
                act.wait_ge(sg("blocks_ready"), kv + 1)
                A(cb[0][:, kv, :], blk, ACT.Copy).then_inc(sg("blocks_hi"), 1)
            split_hi(act, J_CMP, 4, 12)
            split_hi(act, J_CMP + 1, 4, 12)
            for kv in range(2):
                par = (J_CMP + kv) % 2
                wait(act, granules_done, (J_CMP + kv + 1) * GPJ)
                A(cmp_hid[0:NKV * NCMP, kv, :], acc[par][0][0:NKV * NCMP, 0:CMP_HIDDEN],
                  ACT.Gelu_apprx_tanh).then_inc(acc_taken[par], 1)
            act.wait_ge(sg("hid_turned"), 1)
            A(cmp_hT, mx[:, 0, 0:4 * NKV * NCMP].rearrange("p (a b) -> p a b", a=4), ACT.Copy) \
                .then_inc(sg("hid_copied"), 1)
            act.wait_ge(sg("cmp_ready"), 1)
            A(kcT, mx[:, 1, 0:NKV * NCMP], ACT.Copy)
            A(vc[0:NCMP, :, :], mx[0:NCMP, 2, 0:NKV * HD].rearrange("p (g d) -> p g d", g=NKV), ACT.Copy) \
                .then_inc(sg("cmp_copied"), 1)
            for g in range(NKV):
                act.wait_ge(sg("cmp_rowmax"), g + 1)
                for j in range(HG):
                    for t, (a, b) in enumerate(((0, NC0), (NC0, NC0 + NCMP))):
                        last = A(scc[:, j, a:b], scc[:, j, a:b], ACT.Exp, bias=rowmax[:, t, j:j + 1])
                last.then_inc(sg("cmp_exp"), 1)
                act.wait_ge(sg("cmp_turned"), g + 1)
                A(pt[0:NC0, :, 0:P], mx[0:NC0, :, 0:P], ACT.Copy)
                A(pt[0:NCMP, :, P:S], mx[0:NCMP, :, P:S], ACT.Copy).then_inc(sg("cmp_probs_copied"), 1)
                for b in range(2):
                    for _ in unit_act(act, 2 * g + b, sc, pt):
                        pass
                turn_hi(act, B_OA + 2 * g, part(lt_b, 4 * g), 2)

            def gdn_mix(g):
                for b in range(6):
                    wait(act, sg("gct_turned"), 6 * g + b + 1)
                    A(g_ct[:, 2 * b:2 * b + 2, 3:3 + S], mx[:, b % 4, :].rearrange("p (c s) -> p c s", s=S),
                      ACT.Copy).then_inc(sg("gct_copied"), 1)
                    if b % 2:
                        yield
                for kind in range(3):
                    wait(act, sg("conv_done"), 3 * g + kind + 1)
                    A(g_cv[:, 4 * kind:4 * kind + 4, :], g_cv[:, 4 * kind:4 * kind + 4, :], ACT.Silu) \
                        .then_inc(sg("silu_done"), 1)
                    if kind == 2:
                        wait(act, acc_taken[0], (J_GDN + 4 * g + 3) // 2 + 1)
                        A(g_z[:, :, :], g_nat[:, 3], ACT.Silu)
                    yield
                    for t in range(NT):
                        b = 2 * kind + t
                        wait(act, sg("grn_turned"), 6 * g + b + 1)
                        A(g_rn[:, t, 4 * kind:4 * kind + 4, :], mx[:, b % 4, :].rearrange("p (c s) -> p c s", s=HD),
                          ACT.Copy).then_inc(sg("grn_copied"), 1)
                    if g == 0 and kind == 0:
                        act.wait_ge(sg("gcum_ready"), 1)
                        A(tok[:, G_E], tok[:, G_CUM], ACT.Exp)
                        A(tok[:, G_KD], tok[:, G_KD], ACT.Exp).then_inc(sg("gexp_done"), 1)
                    yield
                for _ in range(3):
                    yield
                for b in range(6):
                    wait(act, sg("gqk_turned"), 6 * g + b + 1)
                    A(g_cv[:, 2 * b:2 * b + 2, :], mx[:, b % 4, :].rearrange("p (c s) -> p c s", s=S),
                      ACT.Copy).then_inc(sg("gqk_copied"), 1)
                    if b % 3 == 2:
                        yield
                yield
                wait(act, sg("gdiff_ready"), g + 1)
                A(g_dec[:, :, :], g_dec[:, :, :], ACT.Exp, scale=-1.0)
                A(egl, egl, ACT.Exp)
                A(g_qkT[:, :, :], g_qkT[:, :, :], ACT.Exp).then_inc(sg("gdecay_ready"), 1)
                yield
                yield
                yield
                for lv in range(LEVELS * g, LEVELS * g + LEVELS):
                    for b in range(2):
                        wait(act, sg("inv_p"), 2 * lv + b + 1)
                        A(g_P1[:, 4 * b:4 * b + 4, :], mx[:, b, :].rearrange("p (c s) -> p c s", s=P),
                          ACT.Copy).then_inc(sg("inv_p_copied"), 1)
                    yield
                wait(act, sg("uw_ready"), g + 1)
                A(g_U[:, :, :], mx[:, 0:2, :].rearrange("p b (c s) -> p (b c) s", s=P), ACT.Copy)
                A(g_wT[:, :, :], mx[:, 2:4, :].rearrange("p b (c s) -> p (b c) s", s=P), ACT.Copy) \
                    .then_inc(sg("uw_copied"), 1)
                yield
                for n in range(4):
                    t, r = n // 2, slice(CHUNK * (n % 2), CHUNK * (n % 2) + CHUNK)
                    wait(act, sg("ws_ready"), 4 * g + n + 1)
                    A(g_o[r, t, :, :], mx[r, 1, :].rearrange("p (h d) -> p h d", d=HD), ACT.Copy) \
                        .then_inc(sg("oq_copied"), 1)
                    yield

            for kind in range(4):
                copy_job(J_GDN + kind, lambda t, kind=kind: g_nat[:, kind, t, :])
            mix = gdn_mix(0)
            for kind in range(4):
                copy_job(J_GDN + 4 + kind, lambda t, kind=kind: g_nat[:, kind, t, :], mix=mix)
            turn_hi(act, B_OB, part(lt_b, NH), 2)

            mix = gdn_mix(1)
            for c in range(4):
                copy_job(J_MERGE + c, lambda t, c=c: mg_a[:, c, t, :], ACT.Sigmoid, mix=mix)
            turn_hi(act, B_OB + 2, part(lt_b, NH + HG), 2)
            with fori(2) as i:
                for c in range(2):
                    copy_job(Lin(J_MERGE + 4 + c, [(2, i)]),
                             lambda t: mg_b[:, bass.ds(i * 2 + c, 1), t, :].rearrange("p a n -> p (a n)"),
                             ACT.Sigmoid)
            with fori(2) as i:
                for c in range(2):
                    split_hi(act, Lin(J_PAB + c, [(2, i)]), 4, 12)
            turn_hi(act, B_Y, whole(lt_a), 8)
            with fori(2) as i:
                for c in range(2):
                    split_hi(act, Lin(J_WO + c, [(2, i)]), 4, 12)
            act.wait_ge(sg("wo_done"), 4)
            rms_act(act, 1)
            turn_hi(act, B_LN2, whole(lt_a), 8)
            with fori(4) as g:
                for c in range(5):
                    J = Lin(J_MLP + c, [(8, g)])
                    split_hi(act, J, 4, 6)
                    if c:
                        turn_hi(act, Lin(B_U + 2 * (c - 1), [(8, g)]), part(lt_b, 4 * (c - 1)), 2)
                    split_hi(act, J, 6, 12)
                    if c < 4:
                        wait(act, granules_done, J * GPJ + GPJ)
                        for t in range(NT):
                            last = A(relu[:, t, :], acc[J.c % 2][t][:, :], ACT.Relu)
                        last.then_inc(acc_taken[J.c % 2], 1)
                for c in range(5, 8):
                    split_hi(act, Lin(J_MLP + c, [(8, g)]), 4, 12)
            act.wait_ge(sg("down_done"), 16)
            rms_act(act, 2)
            turn_hi(act, B_LNF, whole(lt_a), 8)

            act.wait_ge(sg("f_arg_ready"), 1)
            A(f_t[1], f_t[1], ACT.Exp).then_inc(sg("act_step"), 1)
            act.wait_ge(sg("act_step"), 2)
            A(f_t[1], f_t[1], ACT.Ln, bias=1.0).then_inc(sg("f_ln_done"), 1)
            def fox_mix(g):
                for kind in range(2):
                    for _ in range(4):
                        yield
                    for b in range(2 * kind, 2 * kind + 2):
                        wait(act, sg("fqk_turned"), Lin(b + 1, [(4, g)]))
                        A(f_T[:, 2 * b:2 * b + 2, :], mx[:, b % 2, :].rearrange("p (c s) -> p c s", s=S),
                          ACT.Copy).then_inc(sg("fqk_copied"), 1)
                    yield
                    if kind == 0:
                        for _ in range(3):
                            yield
                yield from unit_act(act, Lin(4, [(1, g)]), f_sc, f_pt)

            with fori(4) as g:
                mix = None
                for kind in range(4):
                    if kind == 1:
                        mix = fox_mix(g)
                    copy_job(Lin(J_FOX + kind, [(4, g)]), lambda t, kind=kind: f_nat[:, kind, t, :],
                             ACT.Silu if kind == 3 else ACT.Copy, mix=mix)
                turn_hi(act, Lin(B_FO, [(2, g)]), part(lt_b, g * HG), 2)
            with fori(2) as i:
                for c in range(2):
                    split_hi(act, Lin(J_FOXO + c, [(2, i)]), 4, 12)
            turn_hi(act, B_LNG, whole(lt_a), 8)

            def ret_mix(h, p):
                pr = Lin(0, [(2, h), (1, p)])
                for _ in range(7):
                    yield
                for b in range(4):
                    wait(act, sg("rqk_turned"), pr * 5 + b + 1)
                    A(r_T[:, 2 * b:2 * b + 2, :], mx[:, b % 4, :].rearrange("p (c s) -> p c s", s=S),
                      ACT.Copy).then_inc(sg("rqk_copied"), 1)
                    if b % 2:
                        yield
                wait(act, sg("rqk_turned"), pr * 5 + 5)
                A(r_qdT[:, :, :], mx[:, 0, :].rearrange("p (c s) -> p c s", s=P), ACT.Copy) \
                    .then_inc(sg("rqk_copied"), 1)
                yield
                yield
                for hh in range(2):
                    wait(act, sg("r_R_ready"), pr * 2 + hh + 1)
                    A(r_R[:, 2 * hh:2 * hh + 2, :], mx[:, 2:4, :], ACT.Copy) \
                        .then_inc(sg("r_R_copied"), 1)
                    for _ in range(6 if hh == 0 else 8):
                        yield
                turn_hi(act, Lin(B_RO, [(8, h), (4, p)]), part(lt_b, p * 8), 2)
                yield

            with fori(2) as h:
                with fori(2) as p:
                    J = Lin(J_RET, [(16, h), (6, p)])
                    mix = None
                    for c in range(6):
                        if c == 2:
                            mix = ret_mix(h, p)
                        copy_job(J + c, lambda t, c=c: r_nat[:, c, t, :],
                                 ACT.Silu if c > 3 else ACT.Copy, RET_QK ** -0.5 if c == 1 else 1.0, mix=mix)
                    turn_hi(act, Lin(B_RO + 2, [(8, h), (4, p)]), part(lt_b, p * 8 + 4), 2)
                for c in range(4):
                    split_hi(act, Lin(J_RET + 12 + c, [(16, h)]), 4, 12)

        @block.tensor
        def _(pe):
            MM, TR = nc.tensor.matmul, nc.tensor.transpose

            def fori(n):
                return pe.Fori(0, n)

            def small_mm(dst, w, n):
                for t in range(NT):
                    for kt in range(KT):
                        for p in range(2):
                            last = MM(dst[:, t, 0:n], lt_a[p][:, kt, t * P:(t + 1) * P].bitcast(F32),
                                      w[:, kt, 0:n], start=(kt + p == 0), stop=(kt == KT - 1 and p == 1))
                return last

            pe.wait_ge(sg("const_loaded"), 16 * N_CONST)
            pe.wait_ge(sg("ident_ready"), 1)
            MM(mx[0:NH, 0, 0:384], tabl[0:BUCKETS, :], onehot[0:BUCKETS, :], start=True, stop=True)
            TR(mx[:, 1, 0:96], cw_nat[0:96, :], ident[0:96, 0:96])
            for kv in range(2):
                last = TR(mx[:, 2, 32 * kv:32 * kv + 32], pe_nat[0:CMP_BLOCK, kv, :],
                          ident[0:CMP_BLOCK, 0:CMP_BLOCK])
            last.then_inc(sg("prep_ready"), 1)
            pe.wait_ge(sg("prep_taken"), 1)
            pe.wait_ge(sg("h_ready"), 1)
            turn(pe, B_LN1, lambda c, t: h_nat[:, t, c * P:(c + 1) * P], 8)
            pe.wait_ge(lt_lo_ready, B_LN1 + 8)
            small_mm(small_ps, wsmall, 40).then_inc(sg("gates_ready"), 1)

            multiply(pe, 0, lt_a, 0)
            with fori(2) as i:
                for c in range(2):
                    multiply(pe, Lin(1 + c, [(2, i)]), lt_a, (1 + c) % 2,
                             free=(acc_taken[0], Lin(1, [(1, i)])) if c == 0 else None)
            pe.wait_ge(acc_taken[0], 3)
            pe.wait_ge(sg("gates_done"), 1)
            for n, b in enumerate(NSA_ORDER):
                if n >= 4:
                    pe.wait_ge(sg("nsa_copied"), n - 3)
                for c in range(2):
                    blkno, col = NSA_TILES[2 * b + c]
                    for t in range(NT):
                        last = TR(mx[:, n % 4, (2 * c + t) * P:(2 * c + t + 1) * P],
                                  nat[:, blkno, t, col * P:(col + 1) * P], ident[:, :])
                last.then_inc(sg("nsa_turned"), 1)
            for kv in range(2):
                J, par = J_CMP + kv, (J_CMP + kv) % 2
                pe.wait_ge(acc_taken[par], J // 2)
                pe.wait_ge(sg("blocks_lo"), kv + 1)
                for r in range(GPJ):
                    pe.wait_ge(lo_ready, J * GPJ + r + 1)
                    for k in range(4):
                        j = 4 * r + k
                        hi, lo = (w[:, r % 4].rearrange("p a b -> p (a b)")[:, k * 256:(k + 1) * 256]
                                  for w in (w_hi, w_lo))
                        b_hi, b_lo = (cb[p][:, kv, j * 30:(j + 1) * 30] for p in range(2))
                        o = acc[par][0][0:NKV * NCMP, 0:CMP_HIDDEN]
                        MM(o, b_hi, hi, start=(j == 0), stop=False)
                        MM(o, b_hi, lo, start=False, stop=False)
                        last = MM(o, b_lo, hi, start=False, stop=(j == CMP_BLOCK - 1))
                    last.then_inc(granules_done, 1)
            n = NKV * NCMP
            pe.wait_ge(acc_taken[J_CMP % 2], J_CMP // 2 + 1)
            pe.wait_ge(acc_taken[(J_CMP + 1) % 2], (J_CMP + 1) // 2 + 1)
            pe.wait_ge(sg("nsa_copied"), 8)
            for kv in range(2):
                for c in range(2):
                    last = TR(mx[:, 0, (2 * kv + c) * n:(2 * kv + c + 1) * n],
                              cmp_hid[0:n, kv, c * P:(c + 1) * P], ident[0:n, 0:n])
            last.then_inc(sg("hid_turned"), 1)
            pe.wait_ge(sg("hid_copied"), 1)
            for c in range(2):
                MM(mx[:, 1, 0:n], w2[:, 0, c, :], cmp_hT[:, c, :], start=(c == 0), stop=(c == 1))
            for g in range(NKV):
                for c in range(2):
                    last = MM(mx[0:NCMP, 2, g * HD:(g + 1) * HD], cmp_hT[:, 2 + c, g * NCMP:(g + 1) * NCMP],
                              w2[:, 1, c, :], start=(c == 0), stop=(c == 1))
            last.then_inc(sg("cmp_ready"), 1)
            pe.wait_ge(sg("cmp_copied"), 1)
            for g in range(NKV):
                kc = kcT[:, g * NCMP:(g + 1) * NCMP]
                for j in range(HG):
                    MM(mx[:, j, 0:NC0], T[:, HG * g + j, 0:P], kc[:, 0:NC0], start=True, stop=True)
                    last = MM(mx[:, j, NC0:NC0 + NCMP], T[:, HG * g + j, P:S], kc, start=True, stop=True)
                last.then_inc(sg("cmp_scores"), 1)
                pe.wait_ge(sg("cmp_probs"), g + 1)
                for j in range(HG):
                    TR(mx[0:NC0, j, 0:P], scc[:, j, 0:NC0], ident[:, :])
                    last = TR(mx[0:NCMP, j, P:S], scc[:, j, NC0:NC0 + NCMP], ident[:, :])
                last.then_inc(sg("cmp_turned"), 1)
                pe.wait_ge(sg("cmp_probs_copied"), g + 1)
                for j in range(HG):
                    MM(mx[:, 0, j * HD:(j + 1) * HD], pt[0:NC0, j, 0:P], vc[0:NC0, g, :], start=True, stop=True)
                    last = MM(mx[:, 1, j * HD:(j + 1) * HD], pt[0:NCMP, j, P:S], vc[0:NCMP, g, :],
                              start=True, stop=True)
                last.then_inc(sg("cmp_out_ready"), 1)
                pe.wait_ge(sg("cmp_out_taken"), g + 1)
                for b in range(2):
                    for _ in unit_pe(pe, 2 * g + b, sc, pt, lambda j: T[:, HG * g + j, :],
                                     lambda j: T[:, 12 + 2 * b + g, :],
                                     lambda j, t: nat[:, 3 + b, t, (2 + g) * HD:(3 + g) * HD]):
                        pass
                pe.wait_ge(att["att_out_taken"], 2 * g + 2)
                turn(pe, B_OA + 2 * g, lambda c, t: o_nat[:, t, c, :], 2)
                pe.wait_ge(lt_lo_ready, B_OA + 2 * g + 2)

            def gdn_mix(g):
                for b in range(6):
                    if b >= 4:
                        wait(pe, sg("gct_copied"), 6 * g + b - 3)
                    for c in range(2):
                        i = 2 * b + c
                        for t in range(NT):
                            last = TR(mx[:, b % 4, (2 * c + t) * P:(2 * c + t + 1) * P],
                                      g_nat[:, i // 4, t, (i % 4) * P:(i % 4 + 1) * P], ident[:, :])
                    last.then_inc(sg("gct_turned"), 1)
                    if b % 2:
                        yield
                if g == 0:
                    pe.wait_ge(sg("mask_loaded"), 16)
                    pe.wait_ge(sg("gct_copied"), 3)
                    for t in range(NT):
                        MM(mx[:, 2, t * NH:(t + 1) * NH], g_mask[:, M_TRI, :], tok[:, G_G, t, :],
                           start=True, stop=True)
                        last = MM(mx[:, 2, (2 + t) * NH:(3 + t) * NH], g_mask[:, M_ONES, :], tok[:, G_G, t, :],
                                  start=True, stop=True)
                    last.then_inc(sg("gsum_ready"), 1)
                yield
                for kind in range(3):
                    wait(pe, sg("silu_done"), 3 * g + kind + 1)
                    if kind == 0:
                        wait(pe, sg("gct_copied"), 6 * g + 6)
                    if kind == 1:
                        pe.wait_ge(sg("gcum_ready"), 1)
                    if kind == 2:
                        wait(pe, sg("grn_copied"), 6 * g + 2)
                    for t in range(NT):
                        b = 2 * kind + t
                        for c in range(4):
                            last = TR(mx[:, b % 4, c * P:(c + 1) * P],
                                      g_cv[:, 4 * kind + c, t * P:(t + 1) * P], ident[:, :])
                        last.then_inc(sg("grn_turned"), 1)
                    yield
                    yield
                yield
                yield
                wait(pe, sg("g_normed"), g + 1)
                for b in range(6):
                    if b >= 4:
                        wait(pe, sg("gqk_copied"), 6 * g + b - 3)
                    for c in range(2):
                        i = 2 * b + c
                        for t in range(NT):
                            src = g_rn[:, t, i, :] if i < 8 else g_qg[:, t, i - 8, :]
                            last = TR(mx[:, b % 4, (2 * c + t) * P:(2 * c + t + 1) * P], src, ident[:, :])
                    last.then_inc(sg("gqk_turned"), 1)
                    if b % 3 == 2:
                        yield
                wait(pe, sg("gqk_copied"), 6 * g + 6)
                for i in range(HG * NT):
                    last = MM(mx[:, i // 4, (i % 4) * P:(i % 4 + 1) * P],
                              tg[:, G_G, i % NT, i // NT:i // NT + 1].to_broadcast([P, P]), g_mask[:, M_TRI, :],
                              start=True, stop=True)
                last.then_inc(sg("gb_ready"), 1)
                for i in range(HG * NT):
                    k = g_kT[:, i // NT, (i % NT) * P:(i % NT + 1) * P]
                    last = MM(mx[:, 2 + i // 4, (i % 4) * P:(i % 4 + 1) * P], k, k, start=True, stop=True)
                last.then_inc(sg("kk_ready"), 1)
                yield
                yield
                wait(pe, sg("gdiff_ready"), g + 1)
                for i in range(HG * NT):
                    ts = slice((i % NT) * P, (i % NT + 1) * P)
                    last = MM(mx[:, i // 4, (i % 4) * P:(i % 4 + 1) * P], g_kT[:, i // NT, ts],
                              g_qT[:, i // NT, ts], start=True, stop=True)
                last.then_inc(sg("qk_ready"), 1)
                yield
                yield
                for l in range(LEVELS):
                    for b in range(2):
                        wait(pe, sg("inv_c"), 2 * ((LEVELS + 1) * g + l) + b + 1)
                        for i in range(4 * b, 4 * b + 4):
                            last = MM(mx[:, b, (i % 4) * P:(i % 4 + 1) * P], g_dec[:, i, :], g_Y[:, i, :],
                                      start=True, stop=True)
                        last.then_inc(sg("inv_p"), 1)
                    for b in range(2):
                        wait(pe, sg("inv_p_copied"), 2 * (LEVELS * g + l) + b + 1)
                        for i in range(4 * b, 4 * b + 4):
                            MM(mx[:, 2 + b, (i % 4) * P:(i % 4 + 1) * P], g_X[:, i, :], g_P1[:, i, :],
                               start=True, stop=True)
                        for i in range(4 * b, 4 * b + 4):
                            last = MM(mx[:, b, (i % 4) * P:(i % 4 + 1) * P], g_P1[:, i, :], g_X[:, i, :],
                                      start=True, stop=True)
                        last.then_inc(sg("inv_q"), 1)
                    yield
                wait(pe, sg("inv_c"), 2 * (LEVELS + 1) * (g + 1))
                for i in range(HG * NT):
                    t, h = i % NT, i // NT
                    MM(mx[:, i // 4, (i % 4) * P:(i % 4 + 1) * P], g_Y[:, i, :], g_vb[:, t, h, :],
                       start=True, stop=True)
                    last = MM(mx[:, 2 + i // 4, (i % 4) * P:(i % 4 + 1) * P], g_kbeg[:, t, h, :],
                              g_Y[:, i, :], start=True, stop=True)
                last.then_inc(sg("uw_ready"), 1)
                yield
                wait(pe, sg("uw_copied"), g + 1)
                for n in range(4):
                    t, r = n // 2, slice(CHUNK * (n % 2), CHUNK * (n % 2) + CHUNK)
                    wait(pe, sg("s_ready"), 5 * g + n + 1)
                    if n:
                        wait(pe, sg("oq_copied"), 4 * g + n)
                    for h in range(HG):
                        MM(mx[:, 0, h * HD:(h + 1) * HD], g_wT[:, h * NT + t, :], g_S[:, h, :],
                           start=True, stop=True)
                    for h in range(HG):
                        last = MM(mx[r, 1, h * HD:(h + 1) * HD], g_qgT[:, h, t * P + r.start:t * P + r.stop],
                                  g_S[:, h, :], start=True, stop=True)
                    last.then_inc(sg("ws_ready"), 1)
                    wait(pe, sg("v_ready"), 4 * g + n + 1)
                    for h in range(HG):
                        last = MM(mx[:, 2, h * HD:(h + 1) * HD], g_kdec[r, t, h, :], g_V[r, h, :],
                                  start=True, stop=True)
                    last.then_inc(sg("su_ready"), 1)
                    if n % 2:
                        for h in range(HG):
                            last = MM(mx[:, 3, h * HD:(h + 1) * HD], g_qkT[:, h * NT + t, :], g_V[:, h, :],
                                      start=True, stop=True)
                        last.then_inc(sg("in_ready"), 1)
                    yield

            for kind in range(4):
                multiply(pe, J_GDN + kind, lt_a, (J_GDN + kind) % 2)
            for g in range(2):
                mix = gdn_mix(g)
                for kind in range(4):
                    J = (J_GDN + 4 if g == 0 else J_MERGE) + kind
                    multiply(pe, J, lt_a, J % 2, mix=mix)
                wait(pe, sg("go_ready"), g + 1)
                turn(pe, B_OB + 2 * g, lambda c, t: g_o[:, t, c, :], 2)
                wait(pe, lt_lo_ready, B_OB + 2 * g + 2)

            with fori(2) as i:
                for c in range(2):
                    J = Lin(J_MERGE + 4 + c, [(2, i)])
                    multiply(pe, J, lt_a, J.c % 2)
            with fori(2) as i:
                for c in range(2):
                    J = Lin(J_PAB + c, [(2, i)])
                    wait(pe, acc_taken[0], (J + 1).half() if J.c % 2 else J.half())
                    wait(pe, acc_taken[1], J.half())
                    for r in range(GPJ):
                        wait(pe, lo_ready, J * GPJ + r + 1)
                        for k in range(2):
                            kt = 2 * r + k
                            for t in range(NT):
                                a_hi, a_lo = (lt_b[p][:, kt, t * P:(t + 1) * P] for p in range(2))
                                o = acc[kt // 8][t][:, :]
                                MM(o, a_hi, w_hi[:, r % 4, k, :], start=(kt % 8 == 0), stop=False)
                                MM(o, a_hi, w_lo[:, r % 4, k, :], start=False, stop=False)
                                last = MM(o, a_lo, w_hi[:, r % 4, k, :], start=False, stop=(kt % 8 == 7))
                        last.then_inc(granules_done, 1)
            pe.wait_ge(sg("y_ready"), 1)
            turn(pe, B_Y, lambda c, t: y_nat[:, t, c * P:(c + 1) * P], 8)
            pe.wait_ge(lt_lo_ready, B_Y + 8)
            pe.wait_ge(acc_taken[0], (J_WO + 1) // 2)
            with fori(2) as i:
                for c in range(2):
                    J = Lin(J_WO + c, [(2, i)])
                    multiply(pe, J, lt_a, J.c % 2)
            pe.wait_ge(sg("h_ready"), 2)
            turn(pe, B_LN2, lambda c, t: h_nat[:, t, c * P:(c + 1) * P], 8)
            pe.wait_ge(lt_lo_ready, B_LN2 + 8)
            with fori(4) as g:
                for c in range(8):
                    J = Lin(J_MLP + c, [(8, g)])

                    def hook(r, c=c):
                        if r == 3 and 1 <= c <= 4:
                            wait(pe, sg("u_ready"), Lin(c, [(4, g)]))
                            turn(pe, Lin(B_U + 2 * (c - 1), [(8, g)]),
                                 lambda k, t: u_nat[:, (c - 1) % 2, t, k * P:(k + 1) * P], 2)
                        if r == 6 and c == 4:
                            wait(pe, lt_lo_ready, Lin(B_U + 8, [(8, g)]))
                    if c == 4:
                        wait(pe, lt_lo_ready, Lin(B_U + 6, [(8, g)]))
                    multiply(pe, J, lt_a if c < 4 else lt_b, J.c % 2, hook)
            pe.wait_ge(sg("h_ready"), 3)
            turn(pe, B_LNF, lambda c, t: res[:, t, c * P:(c + 1) * P], 8)
            pe.wait_ge(lt_lo_ready, B_LNF + 8)

            pe.wait_ge(sg("fox_loaded"), 48)
            small_mm(small_ps, f_w, FOX_HEADS).then_inc(sg("f_logit_ready"), 1)
            pe.wait_ge(sg("f_arg_ready"), 1)
            pe.wait_ge(sg("f_ones_ready"), 1)
            def fox_mix(g):
                one, two = Lin(1, [(1, g)]), Lin(0, [(2, g)])
                for kind in range(2):
                    for _ in range(4):
                        yield
                    wait(pe, sg("fq_ready"), two + kind + 1)
                    for b in range(2):
                        for c in range(2):
                            for t in range(NT):
                                i = 2 * b + c
                                last = TR(mx[:, b, (2 * c + t) * P:(2 * c + t + 1) * P],
                                          f_nat[:, kind, t, i * P:(i + 1) * P], ident[:, :])
                        last.then_inc(sg("fqk_turned"), 1)
                    yield
                    wait(pe, sg("fqk_copied"), Lin(2 * kind + 2, [(4, g)]))
                    if kind == 0:
                        for h in range(HG):
                            MM(mx[:, h, 0:P], f_lg[:, 0, h:h + 1].to_broadcast([P, P]), tri[:, :],
                               start=True, stop=True)
                            MM(mx[:, h, P:S], f_lg[:, 0, h:h + 1].to_broadcast([P, P]), f_ones[:, :],
                               start=True, stop=False)
                            last = MM(mx[:, h, P:S], f_lg[:, 1, h:h + 1].to_broadcast([P, P]), tri[:, :],
                                      start=False, stop=True)
                        last.then_inc(sg("f_cum_ready"), 1)
                        for _ in range(3):
                            yield
                        wait(pe, sg("f_bias_ready"), one)
                yield from unit_pe(pe, Lin(4, [(1, g)]), f_sc, f_pt, lambda j: f_T[:, j, :],
                                   lambda j: f_T[:, 4 + j, :],
                                   lambda j, t: f_nat[:, 2, t, j * HD:(j + 1) * HD])

            with fori(4) as g:
                mix = None
                for kind in range(4):
                    J = Lin(J_FOX + kind, [(4, g)])
                    if kind == 1:
                        mix = fox_mix(g)
                    multiply(pe, J, lt_a, J.c % 2, mix=mix)
                assert next(mix, "over") == "over"
                wait(pe, sg("fo_ready"), Lin(1, [(1, g)]))
                turn(pe, Lin(B_FO, [(2, g)]), lambda c, t: f_o[:, t, c, :], 2)
            pe.wait_ge(lt_lo_ready, B_FO + 8)
            with fori(2) as i:
                for c in range(2):
                    J = Lin(J_FOXO + c, [(2, i)])
                    multiply(pe, J, lt_b, J.c % 2)
            pe.wait_ge(sg("ln_done"), 1)
            turn(pe, B_LNG, lambda c, t: res[:, t, c * P:(c + 1) * P], 8)
            pe.wait_ge(lt_lo_ready, B_LNG + 8)

            def turn_y(h, p, hh):
                wait(pe, sg("r_y_ready"), Lin(hh + 1, [(4, h), (2, p)]))
                turn(pe, Lin(B_RO + 2 * hh, [(8, h), (4, p)]),
                     lambda c, t: r_nat[:, 4 + hh, t, c * P:(c + 1) * P], 2)

            def ret_mix(h, p):
                pr = Lin(0, [(2, h), (1, p)])
                J = Lin(J_RET, [(16, h), (6, p)])
                for _ in range(7):
                    yield
                wait(pe, sg("rot_ready"), pr + 1)
                for b in range(4):
                    for c in range(2):
                        i = 2 * b + c
                        for t in range(NT):
                            last = TR(mx[:, b, (2 * c + t) * P:(2 * c + t + 1) * P],
                                      r_nat[:, i // 4, t, (i % 4) * P:(i % 4 + 1) * P], ident[:, :])
                    last.then_inc(sg("rqk_turned"), 1)
                    if b % 2:
                        yield
                wait(pe, sg("rqk_copied"), pr * 5 + 1)
                for c in range(4):
                    last = TR(mx[:, 0, c * P:(c + 1) * P], r_tmp[:, 0, c * P:(c + 1) * P], ident[:, :])
                last.then_inc(sg("rqk_turned"), 1)
                yield
                wait(pe, sg("rqk_copied"), pr * 5 + 5)
                for hh in range(2):
                    for t in range(NT):
                        for k in range(2):
                            i = 2 * hh + t
                            last = MM(mx[:, 1, i * P:(i + 1) * P], r_T[:, 4 + 2 * hh + k, t * P:(t + 1) * P],
                                      r_T[:, 2 * hh + k, t * P:(t + 1) * P], start=(k == 0), stop=(k == 1))
                last.then_inc(sg("r_inner"), 1)
                yield
                for hh in range(2):
                    wait(pe, acc_taken[1 - hh], (J + 2 + hh).half() + 1)
                    for k in range(2):
                        last = MM(mx[:, 2 + k, :], r_kd[:, hh, k * P:(k + 1) * P], r_nat[:, 2 + hh, 0, :],
                                  start=True, stop=True)
                    last.then_inc(sg("r_R_ready"), 1)
                    yield
                    if hh == 0:
                        wait(pe, sg("r_in_ready"), pr + 1)
                    else:
                        wait(pe, sg("r_o_taken"), pr * 2 + hh)
                    MM(mx[:, 0, :], r_in[:, 2 * hh, :], r_nat[:, 2 + hh, 0, :], start=True, stop=True)
                    MM(mx[:, 1, :], r_in[:, 2 * hh + 1, :], r_nat[:, 2 + hh, 1, :], start=True, stop=False)
                    wait(pe, sg("r_R_copied"), pr * 2 + hh + 1)
                    for k in range(2):
                        last = MM(mx[:, 1, :], r_qdT[:, 2 * hh + k, :], r_R[:, 2 * hh + k, :],
                                  start=False, stop=(k == 1))
                    last.then_inc(sg("r_o_ready"), 1)
                    for _ in range(5 if hh == 0 else 7):
                        yield
                turn_y(h, p, 0)
                yield

            with fori(2) as h:
                with fori(2) as p:
                    J = Lin(J_RET, [(16, h), (6, p)])
                    mix = None
                    for c in range(6):
                        if c == 2:
                            mix = ret_mix(h, p)
                        multiply(pe, J + c, lt_a, (J + c).c % 2, mix=mix)
                    turn_y(h, p, 1)
                wait(pe, lt_lo_ready, Lin(B_RO + 8, [(8, h)]))
                for c in range(4):
                    J = Lin(J_RET + 12 + c, [(16, h)])
                    multiply(pe, J, lt_b, J.c % 2)

        @block.vector
        def _(dve):
            TT, TS, STT = nc.vector.tensor_tensor, nc.vector.tensor_scalar, nc.vector.scalar_tensor_tensor
            copy = nc.vector.tensor_copy

            def fori(n):
                return dve.Fori(0, n)

            def splits(J, mix=None):
                split_job(split_lo, dve, J, mix)

            dve.wait_ge(sg("prep_ready"), 1)
            copy(distb[0:NH, :], mx[0:NH, 0, 0:384])
            copy(cwt[:, :], mx[:, 1, 0:96])
            copy(pet[:, :, :], mx[:, 2, 0:64].rearrange("p (a b) -> p a b", a=2)).then_inc(sg("prep_taken"), 1)
            rms_dve(dve, 0, h_nat)
            turn_lo(dve, B_LN1, whole(lt_a), 8)
            split_lo(dve, 0, 0, 4)
            ch = Chain(dve, sg("dve_step"))
            dve.wait_ge(sg("gates_done"), 1)
            dve.wait_ge(sg("const_loaded"), 16 * N_CONST)
            ch.link(TT(gt[1], gt[1], heads_bcast(dt_row, NT), ALU.add))
            STT(gt[0], gt[1], -1.0, gt[1], ALU.mult, ALU.min).then_inc(sg("softplus_arg"), 1)
            dve.wait_ge(sg("softplus_done"), 1)
            ch.link(STT(gt[2], gt[1], 0.0, gt[0], ALU.max, ALU.add))
            ch.link(STT(tok[:, G_G], gt[2], -1.0, heads_bcast(a_row, NT), ALU.mult, ALU.mult))
            splits(0)
            with fori(2) as i:
                for c in range(2):
                    splits(Lin(1 + c, [(2, i)]))

            for kv in range(2):
                dve.wait_ge(sg("nsa_copied"), 2)
                v = T[:, 8 + 2 * kv, :]
                win = bass.AP(tensor=v.tensor, offset=v.offset,
                              ap=[v.ap[0], [1, CMP_BLOCK], [S, NKV], [CMP_STRIDE, NCMP]])
                pos = pet[:, kv, :]
                pos = bass.AP(tensor=pos.tensor, offset=pos.offset, ap=[*pos.ap, [0, NKV], [0, NCMP]])
                TT(blk.rearrange("p (j g n) -> p j g n", g=NKV, n=NCMP), win, pos, ALU.add) \
                    .then_inc(sg("blocks_ready"), 1)
                dve.wait_ge(sg("blocks_hi"), kv + 1)
                TT(cb[1][:, kv, :], blk, cb[0][:, kv, :].bitcast(F32), ALU.subtract) \
                    .then_inc(sg("blocks_lo"), 1)
                dve.wait_ge(sg("blocks_lo"), kv + 1)
            splits(J_CMP)
            splits(J_CMP + 1)
            dve.wait_ge(sg("bias_masked"), 2)
            last0 = CMP_BLOCK - 1
            copy(bm[:, :, SEG:SEG + NC0], bm[:, :, last0:last0 + CMP_STRIDE * (NC0 - 1) + 1:CMP_STRIDE])
            ch.link(copy(bm[:, :, SEG + NC0:SEGC],
                         bm[:, :, P + last0:P + last0 + CMP_STRIDE * (NCMP - 1) + 1:CMP_STRIDE]))
            gate4 = gates[:, :, :].rearrange("p t (h b) -> p t h b", b=3)
            for g in range(NKV):
                hs = slice(HG * g, HG * g + HG)
                dve.wait_ge(sg("cmp_scores"), g + 1)
                ch.link(STT(scc, mx[:, :, 0:NC0 + NCMP], ATT_SCALE, bm[:, hs, SEG:SEGC], ALU.mult, ALU.add))
                nc.vector.tensor_reduce(rowmax[:, 0, :], scc[:, :, 0:NC0], AX.X, ALU.max, negate=True)
                nc.vector.tensor_reduce(rowmax[:, 1, :], scc[:, :, NC0:NC0 + NCMP], AX.X, ALU.max,
                                        negate=True).then_inc(sg("cmp_rowmax"), 1)
                dve.wait_ge(sg("cmp_exp"), g + 1)
                TT(scc[:, :, 0:NC0], scc[:, :, 0:NC0], heads_bcast(mask0, HG), ALU.mult) \
                    .then_inc(sg("cmp_probs"), 1)
                dve.wait_ge(sg("cmp_probs"), g + 1)
                nc.vector.tensor_reduce(esum[:, 0, :], scc[:, :, 0:NC0], AX.X, ALU.add)
                ch.link(nc.vector.tensor_reduce(esum[:, 1, :], scc[:, :, NC0:NC0 + NCMP], AX.X, ALU.add))
                ch.link(TS(coef[:, 0], esum[:, 0:2], 1e-30, None, ALU.max))
                ch.link(nc.vector.reciprocal(coef[:, 1], coef[:, 0]))
                ch.link(TT(coef[:, 2], coef[:, 1], gate4[:, :, hs, 0], ALU.mult))
                dve.wait_ge(sg("cmp_out_ready"), g + 1)
                for t in range(NT):
                    for j in range(HG):
                        last = TS(o_nat[:, t, j, :], mx[:, t, j * HD:(j + 1) * HD], coef[:, 2, t, j:j + 1],
                                  None, ALU.mult)
                last.then_inc(sg("cmp_out_taken"), 1)
                dve.wait_ge(sg("cmp_out_taken"), g + 1)
                for b in range(2):
                    for _ in unit_dve(dve, 2 * g + b, ch, sc, o_nat, bm[:, hs, 0:SEG], gate4[:, :, hs, 1 + b],
                                      False):
                        pass
                turn_lo(dve, B_OA + 2 * g, part(lt_b, 4 * g), 2)

            def gdn_mix(g):
                copy(cwg[:, :, :], cwt[:, :].rearrange("p (c h) -> p c h", h=NH)[:, :, g * HG:(g + 1) * HG])
                ch.link(nc.vector.memset(g_ct[:, :, 0:3], 0.0))
                yield
                for kind in range(3):
                    wait(dve, sg("gct_copied"), 6 * g + 2 * kind + 2)
                    for w in range(4):
                        for i in range(4 * kind, 4 * kind + 4):
                            s = cwg[:, 3 * w + i // 4, i % 4:i % 4 + 1]
                            if w == 0:
                                last = TS(g_cv[:, i, :], g_ct[:, i, 0:S], s, None, ALU.mult)
                            else:
                                last = STT(g_cv[:, i, :], g_ct[:, i, w:w + S], s, g_cv[:, i, :],
                                           ALU.mult, ALU.add)
                        if w < 3:
                            ch.link(last)
                        if w % 2 == 0:
                            continue
                        if w == 3:
                            last.then_inc(sg("conv_done"), 1)
                        if g == 0 and kind == 1 and w == 1:
                            dve.wait_ge(sg("gsum_ready"), 1)
                            sums = mx[:, 2, 0:4 * NH].rearrange("p (a h) -> p a h", h=NH)
                            ch.link(copy(tok[:, G_CUM], sums[:, 0:2, :]))
                            TT(tok[:, G_KD], sums[:, 2:4, :], tok[:, G_CUM], ALU.subtract) \
                                .then_inc(sg("gcum_ready"), 1)
                        yield
                if g == 0:
                    dve.wait_ge(sg("gexp_done"), 1)
                    ch.link(TT(tok[:, G_BEG], tok[:, G_BETA], tok[:, G_E], ALU.mult))
                copy(tg[:, :, :, :].rearrange("p a t h -> p (a t) h"),
                     tok[:, :, :, :].rearrange("p a t h -> p (a t) h")[:, :, g * HG:(g + 1) * HG])
                wait(dve, sg("grn_copied"), 6 * g + 4)
                qk = g_rn[:, :, 0:8, :]
                ch.link(TT(g_sq[:, :, :, :], qk, qk, ALU.mult))
                yield
                ch.link(nc.vector.tensor_reduce(gss, g_sq[:, :, :, :], AX.X, ALU.add))
                TS(gss, gss, NORM_EPS, None, ALU.add).then_inc(sg("gss_ready"), 1)
                yield
                wait(dve, sg("grs_ready"), 2 * g + 1)
                ch.link(TS(grs[:, :, 0:4], grs[:, :, 0:4], HD ** -0.5, None, ALU.mult))
                ch.link(TT(qk, qk, bcast(grs, HD), ALU.mult))
                yield
                wait(dve, sg("grn_copied"), 6 * g + 6)
                qn, kn, vn = (g_rn[:, :, 4 * i:4 * i + 4, :] for i in range(3))
                TT(g_vb[:, :, :, :], vn, bcast(tg[:, G_BETA], HD), ALU.mult)
                TT(g_kbeg[:, :, :, :], kn, bcast(tg[:, G_BEG], HD), ALU.mult)
                yield
                TT(g_kdec[:, :, :, :], kn, bcast(tg[:, G_KD], HD), ALU.mult)
                TT(g_qg[:, :, :, :], qn, bcast(tg[:, G_E], HD), ALU.mult).then_inc(sg("g_normed"), 1)
                yield
                copy(g_X[:, :, :], heads_bcast(ident[:, :], HG * NT))
                yield
                copy(g_Y[:, :, :], heads_bcast(ident[:, :], HG * NT))
                yield
                wait(dve, sg("gb_ready"), g + 1)
                wait(dve, sg("gqk_turned"), 6 * g + 6)
                for i in range(HG * NT):
                    gb, s = mx[:, i // 4, (i % 4) * P:(i % 4 + 1) * P], tg[:, G_CUM, i % NT, i // NT:i // NT + 1]
                    TS(g_dec[:, i, :], gb, s, 0.0, ALU.subtract, ALU.max)
                    TS(g_qkT[:, i, :], gb, s, 0.0, ALU.subtract, ALU.min)
                    if i == 4:
                        yield
                copy(egl, mx[:, 0:2, CHUNK - 1::CHUNK].rearrange("p b (i n) -> p (b i) n", n=2)) \
                    .then_inc(sg("gdiff_ready"), 1)
                yield
                wait(dve, sg("gdecay_ready"), g + 1)
                TT(g_dec[:, :, :], g_dec[:, :, :], heads_bcast(g_mask[:, M_STRICT, :], HG * NT), ALU.mult)
                ch.link(TT(g_qkT[:, :, :], g_qkT[:, :, :], heads_bcast(g_mask[:, M_TRI, :], HG * NT), ALU.mult))
                yield
                wait(dve, sg("kk_ready"), g + 1)
                for i in range(HG * NT):
                    STT(g_A[:, i, :], mx[:, 2 + i // 4, (i % 4) * P:(i % 4 + 1) * P],
                        tg[:, G_BETA, i % NT, i // NT:i // NT + 1], g_dec[:, i, :], ALU.mult, ALU.mult)
                wait(dve, sg("qk_ready"), g + 1)
                ch.link(TT(g_qkT[:, :, :], mx[:, 0:2, :].rearrange("p b (c s) -> p (b c) s", s=P), g_qkT[:, :, :],
                           ALU.mult))
                for b in range(2):
                    TT(g_dec[:, 4 * b:4 * b + 4, :], g_A[:, 4 * b:4 * b + 4, :],
                       heads_bcast(g_mask[:, 0, :], 4), ALU.mult).then_inc(sg("inv_c"), 1)
                yield
                for l in range(LEVELS):
                    for b in range(2):
                        wait(dve, sg("inv_q"), 2 * (LEVELS * g + l) + b + 1)
                        hs = slice(4 * b, 4 * b + 4)
                        TT(g_Y[:, hs, :], g_Y[:, hs, :], mx[:, 2 + b, :].rearrange("p (c s) -> p c s", s=P),
                           ALU.subtract)
                        last = TT(g_X[:, hs, :], g_X[:, hs, :], mx[:, b, :].rearrange("p (c s) -> p c s", s=P),
                                  ALU.subtract)
                        if l + 1 < LEVELS:
                            last = TT(g_dec[:, hs, :], g_A[:, hs, :], heads_bcast(g_mask[:, l + 1, :], 4), ALU.mult)
                        last.then_inc(sg("inv_c"), 1)
                    yield
                yield
                wait(dve, sg("uw_copied"), g + 1)
                nc.vector.memset(g_S[:, :, :], 0.0).then_inc(sg("s_ready"), 1)
                U4 = g_U[:, :, :].rearrange("p (h t) d -> p h t d", t=NT)
                for n in range(4):
                    t, r = n // 2, slice(CHUNK * (n % 2), CHUNK * (n % 2) + CHUNK)
                    wait(dve, sg("ws_ready"), 4 * g + n + 1)
                    TT(g_V[r, :, :], U4[r, :, t, :], mx[r, 0, :].rearrange("p (h d) -> p h d", d=HD),
                       ALU.subtract).then_inc(sg("v_ready"), 1)
                    wait(dve, sg("su_ready"), 4 * g + n + 1)
                    wait(dve, sg("s_ready"), 5 * g + n + 1)
                    for h in range(HG):
                        last = STT(g_S[:, h, :], g_S[:, h, :], egl[:, h * NT + t, n % 2:n % 2 + 1],
                                   mx[:, 2, h * HD:(h + 1) * HD], ALU.mult, ALU.add)
                    last.then_inc(sg("s_ready"), 1)
                    if n % 2:
                        wait(dve, sg("in_ready"), 2 * g + n // 2 + 1)
                        wait(dve, sg("oq_copied"), 4 * g + n + 1)
                        ch.link(TT(g_o[:, t, :, :], mx[:, 3, :].rearrange("p (h d) -> p h d", d=HD),
                                   g_o[:, t, :, :], ALU.add))
                    yield
                sq = g_Y[:, :, :]
                o8 = g_o[:, :, :, :].rearrange("p t h d -> p (t h) d")
                s8 = gss.rearrange("p a b -> p (a b)")[:, 0:8]
                ch.link(TT(sq, o8, o8, ALU.mult))
                ch.link(nc.vector.tensor_reduce(s8, sq, AX.X, ALU.add))
                TS(s8, s8, 1.0 / HD, NORM_EPS, ALU.mult, ALU.add).then_inc(sg("gss_ready"), 1)
                yield
                wait(dve, sg("grs_ready"), 2 * g + 2)
                ch.link(TT(o8, o8, bcast(grs.rearrange("p a b -> p (a b)")[:, 0:8], HD), ALU.mult))
                yield
                ch.link(TT(o8, o8, heads_bcast(gnorm[:, :], 8), ALU.mult))
                TT(g_o[:, :, :, :].rearrange("p t h d -> p t (h d)"),
                   g_o[:, :, :, :].rearrange("p t h d -> p t (h d)"), g_z[:, :, :], ALU.mult) \
                    .then_inc(sg("go_ready"), 1)
                yield

            for kind in range(4):
                splits(J_GDN + kind)
            for g in range(2):
                mix = gdn_mix(g)
                for kind in range(4):
                    splits((J_GDN + 4 if g == 0 else J_MERGE) + kind, mix)
                assert next(mix, "over") == "over"
                turn_lo(dve, B_OB + 2 * g, part(lt_b, NH + g * HG), 2)

            with fori(2) as i:
                for c in range(2):
                    splits(Lin(J_MERGE + 4 + c, [(2, i)]))
            dve.wait_ge(acc_taken[0], (J_PAB - 1) // 2 + 1)
            with fori(2) as i:
                pc = Chain(dve, sg("pab_dve_step"), Lin(0, [(4, i)]))
                for c in range(2):
                    J = Lin(J_PAB + c, [(2, i)])
                    splits(J)
                    wait(dve, granules_done, J * GPJ + GPJ)
                    for b in range(2):
                        gate = (mg_a, mg_b)[b][:, bass.ds(i * 2 + c, 1), :, :].rearrange("p a t n -> p (a t) n")
                        for t in range(NT):
                            o = y_nat[:, t, bass.ds(i * (2 * NB) + c * NB, NB)] if b == 0 else y_tmp[:, t, :]
                            last = TT(o, acc[b][t][:, :], gate[:, t, :], ALU.mult)
                        if b == 0:
                            pc.link(last)
                    last.then_inc(acc_taken[J.c % 2], 1)
                    wait(dve, acc_taken[J.c % 2], J.half() + 1)
                    yy = y_nat[:, :, bass.ds(i * (2 * NB) + c * NB, NB)]
                    pc.link(TT(yy, yy, y_tmp[:, :, :], ALU.add))
                pc.end(4)
            nc.vector.memset(y_tmp[:, 0, 0:1], 0.0).then_inc(sg("y_ready"), 1)
            turn_lo(dve, B_Y, whole(lt_a), 8)

            def add_job(J, col, done=None):
                J = lin(J)
                par = J.c % 2
                wait(dve, granules_done, J * GPJ + GPJ)
                cs = slice(col, col + NB) if isinstance(col, int) else bass.ds(col, NB)
                for t in range(NT):
                    last = TT(res[:, t, cs], res[:, t, cs], acc[par][t][:, :], ALU.add)
                last.then_inc(acc_taken[par], 1)
                if done:
                    wait(dve, acc_taken[par], J.half() + 1)
                    nc.vector.memset(y_tmp[:, 0, 0:1], 0.0).then_inc(sg(done), 1)

            dve.wait_ge(sg("x_again"), 16)
            with fori(2) as i:
                for c in range(2):
                    J = Lin(J_WO + c, [(2, i)])
                    splits(J)
                    add_job(J, i * (2 * NB) + c * NB, "wo_done")
            rms_dve(dve, 1, h_nat)
            turn_lo(dve, B_LN2, whole(lt_a), 8)
            with fori(4) as g:
                for c in range(5):
                    J = Lin(J_MLP + c, [(8, g)])
                    split_lo(dve, J, 4, 6)
                    if c:
                        turn_lo(dve, Lin(B_U + 2 * (c - 1), [(8, g)]), part(lt_b, 4 * (c - 1)), 2)
                    split_lo(dve, J, 6, 12)
                    if c < 4:
                        wait(dve, acc_taken[J.c % 2], J.half() + 1)
                        TT(u_nat[:, c % 2], relu[:, :, :], relu[:, :, :], ALU.mult).then_inc(sg("u_ready"), 1)
                    else:
                        add_job(J, 0, "down_done")
                for c in range(5, 8):
                    J = Lin(J_MLP + c, [(8, g)])
                    splits(J)
                    add_job(J, (c - 4) * NB, "down_done")
            rms_dve(dve, 2, res)
            turn_lo(dve, B_LNF, whole(lt_a), 8)

            dve.wait_ge(sg("f_logit_ready"), 1)
            ch.link(TT(f_t[0], small_ps[:, :, 0:FOX_HEADS], heads_bcast(bf_row, NT), ALU.add))
            STT(f_t[1], f_t[0], -1.0, f_t[0], ALU.mult, ALU.min).then_inc(sg("f_arg_ready"), 1)
            dve.wait_ge(sg("f_ln_done"), 1)
            ch.link(STT(f_logf, f_t[0], 0.0, f_t[1], ALU.min, ALU.subtract))
            def fox_mix(g, fc):
                one = Lin(1, [(1, g)])
                for kind in range(2):
                    J = Lin(J_FOX + kind, [(4, g)])
                    wait(dve, acc_taken[J.c % 2], J.half() + 1)
                    v = f_nat[:, kind].rearrange("p t (h d) -> p (t h) d", d=HD)
                    sq = f_sc[:, :, :].rearrange("p h k -> p (h k)")[:, 0:8 * HD].rearrange(
                        "p (h d) -> p h d", d=HD)
                    ss, rs = f_ss[:, kind, :], f_rs[:, kind, :]
                    fc.link(TT(sq, v, v, ALU.mult))
                    yield
                    if kind == 0:
                        copy(f_lg[:, :, :], f_logf[:, :, bass.ds(g * HG, HG)])
                    fc.link(nc.vector.tensor_reduce(ss, sq, AX.X, ALU.add))
                    TS(ss, ss, 1.0 / HD, NORM_EPS, ALU.mult, ALU.add).then_inc(sg("f_ms_ready"), 1)
                    yield
                    wait(dve, sg("f_rs_ready"), Lin(kind + 1, [(2, g)]))
                    fc.link(TT(v, v, bcast(rs, HD), ALU.mult))
                    yield
                    TT(v, v, heads_bcast(fgain[:, kind, :], 8), ALU.mult).then_inc(sg("fq_ready"), 1)
                    yield
                    yield
                    if kind == 0:
                        wait(dve, sg("f_cum_ready"), one)
                        STT(f_bias[:, :, 0:P], mx[:, :, 0:P], -1.0, heads_bcast(f_causal[:, 0:P], HG),
                            ALU.mult, ALU.add)
                        yield
                        STT(f_bias[:, :, P:SEG], mx[:, :, 0:S], -1.0, heads_bcast(f_causal[:, P:SEG], HG),
                            ALU.mult, ALU.add).then_inc(sg("f_bias_ready"), 1)
                        yield
                        yield
                yield from unit_dve(dve, Lin(4, [(1, g)]), fc, f_sc, f_o, f_bias[:, :, :], None, True)

            with fori(4) as g:
                fc = Chain(dve, sg("fox_dve_step"), Lin(0, [(K_FOX_DVE, g)]))
                mix = None
                for kind in range(4):
                    if kind == 1:
                        mix = fox_mix(g, fc)
                    splits(Lin(J_FOX + kind, [(4, g)]), mix)
                wait(dve, acc_taken[0], Lin((J_FOX + 3) // 2 + 1, [(2, g)]))
                fo = f_o[:, :, :, :].rearrange("p t h d -> p t (h d)")
                TT(fo, fo, f_nat[:, 3], ALU.mult).then_inc(sg("fo_ready"), 1)
                turn_lo(dve, Lin(B_FO, [(2, g)]), part(lt_b, g * HG), 2)
                fc.end(K_FOX_DVE)

            def layer_norm(k):
                for t in range(NT):
                    for c in range(4):
                        last = nc.vector.bn_stats(lnst[:, t, c, :], res[:, t, c * NB:(c + 1) * NB])
                ch.link(last)
                for t in range(NT):
                    last = nc.vector.bn_aggr(lnmv[:, t, :], lnst[:, t, :, :].rearrange("p a b -> p (a b)"))
                ch.link(last)
                TS(lnr, lnmv[:, :, 1], LN_EPS, None, ALU.add).then_inc(sg("ln_ms_ready"), 1)
                dve.wait_ge(sg("ln_rs_ready"), k + 1)
                dve.wait_ge(sg("ln_row_loaded"), 32 * (k + 1))
                for t in range(NT):
                    last = TS(res[:, t, :], res[:, t, :], lnmv[:, t, 0:1], rstd[:, t:t + 1], ALU.subtract, ALU.mult)
                ch.link(last)
                ch.link(TT(res[:, :, :], res[:, :, :], heads_bcast(w_row[:, 0, :], NT), ALU.mult))
                TT(res[:, :, :], res[:, :, :], heads_bcast(w_row[:, 1, :], NT), ALU.add) \
                    .then_inc(sg("ln_done"), 1)

            with fori(2) as i:
                for c in range(2):
                    J = Lin(J_FOXO + c, [(2, i)])
                    splits(J)
                    wait(dve, granules_done, J * GPJ + GPJ)
                    cs = bass.ds(i * (2 * NB) + c * NB, NB)
                    for t in range(NT):
                        last = STT(res[:, t, cs], res[:, t, cs], ALPHA, acc[J.c % 2][t][:, :], ALU.mult, ALU.add)
                    last.then_inc(acc_taken[J.c % 2], 1)
            dve.wait_ge(acc_taken[0], (J_RET - 1) // 2 + 1)
            dve.wait_ge(acc_taken[1], (J_RET - 1) // 2)
            layer_norm(0)
            turn_lo(dve, B_LNG, whole(lt_a), 8)

            dve.wait_ge(sg("ln_done"), 1)
            ch.link(TS(res[:, :, :], res[:, :, :], ALPHA, None, ALU.mult))
            dve.wait_ge(sg("ret_loaded"), 32)
            def gate_y(J, pr, hh):
                wait(dve, acc_taken[1 - hh], (J + 4 + hh).half() + 1)
                wait(dve, sg("r_o_taken"), pr * 2 + hh + 1)
                TT(r_nat[:, 4 + hh], r_nat[:, 2 + hh], r_nat[:, 4 + hh], ALU.mult) \
                    .then_inc(sg("r_y_ready"), 1)

            def ret_mix(h, p, rc):
                pr = Lin(0, [(2, h), (1, p)])
                J = Lin(J_RET, [(16, h), (6, p)])
                for kind in range(2):
                    wait(dve, acc_taken[1 - kind], (J + kind).half() + 1)
                    v = r_nat[:, kind].rearrange("p t (h d) -> p t h d", h=2)
                    x1, x2 = v[:, :, :, 0:P], v[:, :, :, P:2 * P]
                    tmp = [r_tmp[:, i, :].rearrange("p (t h d) -> p t h d", t=NT, h=2) for i in range(4)]

                    def rope(i):
                        a = r_cs[:, i]
                        return bass.AP(tensor=a.tensor, offset=a.offset, ap=[a.ap[0], a.ap[1], [0, 2], a.ap[2]])
                    TT(tmp[0], x1, rope(0), ALU.mult)
                    TT(tmp[1], x2, rope(1), ALU.mult)
                    yield
                    TT(tmp[2], x1, rope(1), ALU.mult)
                    rc.link(TT(tmp[3], x2, rope(0), ALU.mult))
                    yield
                    TT(x1, tmp[0], tmp[1], ALU.subtract)
                    rc.link(TT(x2, tmp[2], tmp[3], ALU.add))
                    yield
                for hh in range(2):
                    cs = slice(hh * RET_QK, (hh + 1) * RET_QK)
                    hd = h * 4 + p * 2 + hh
                    TS(r_tmp[:, 0, cs], r_nat[:, 0, 1, cs], r_dec[:, 0, bass.ds(hd, 1)], None, ALU.mult)
                    last = TS(r_kd[:, hh, :], r_nat[:, 1, 0, cs], r_dec[:, 1, bass.ds(hd, 1)], None, ALU.mult)
                last.then_inc(sg("rot_ready"), 1)
                for _ in range(4):
                    yield
                wait(dve, sg("r_inner"), pr + 1)
                wait(dve, sg("r_D_loaded"), pr * 16 + 16)
                for hh in range(2):
                    last = TT(r_in[:, 2 * hh:2 * hh + 2, :],
                              mx[:, 1, 2 * hh * P:(2 * hh + 2) * P].rearrange("p (t c) -> p t c", c=P),
                              heads_bcast(r_D[:, hh, :], NT), ALU.mult)
                last.then_inc(sg("r_in_ready"), 1)
                yield
                yield
                for hh in range(2):
                    wait(dve, sg("r_o_ready"), pr * 2 + hh + 1)
                    for t in range(NT):
                        last = nc.vector.bn_stats(r_st[:, t, :], mx[:, t, :])
                    rc.link(last)
                    yield
                    nc.vector.memset(r_tmp[:, 1, 0:1], 0.0)
                    for t in range(NT):
                        last = nc.vector.bn_aggr(r_mv[:, t, :], r_st[:, t, :])
                    rc.link(last)
                    TS(r_rs, r_mv[:, :, 1], NORM_EPS, None, ALU.add).then_inc(sg("r_ms_ready"), 1)
                    yield
                    wait(dve, sg("r_rs_ready"), pr * 2 + hh + 1)
                    for t in range(NT):
                        last = TS(r_nat[:, 2 + hh, t, :], mx[:, t, :], r_mv[:, t, 0:1], r_rs[:, t:t + 1],
                                  ALU.subtract, ALU.mult)
                    last.then_inc(sg("r_o_taken"), 1)
                    for _ in range(4):
                        yield
                gate_y(J, pr, 0)
                yield
                turn_lo(dve, Lin(B_RO, [(8, h), (4, p)]), part(lt_b, p * 8), 2)
                yield

            with fori(2) as h:
                with fori(2) as p:
                    pr = Lin(0, [(2, h), (1, p)])
                    J = Lin(J_RET, [(16, h), (6, p)])
                    rc = Chain(dve, sg("ret_dve_step"), pr * K_RET_DVE)
                    mix = None
                    for c in range(6):
                        if c == 2:
                            mix = ret_mix(h, p, rc)
                        splits(J + c, mix)
                    gate_y(J, pr, 1)
                    turn_lo(dve, Lin(B_RO + 2, [(8, h), (4, p)]), part(lt_b, p * 8 + 4), 2)
                    rc.end(K_RET_DVE)
                for c in range(4):
                    J = Lin(J_RET + 12 + c, [(16, h)])
                    splits(J)
                    add_job(J, c * NB)
            dve.wait_ge(acc_taken[0], (J_END - 1) // 2 + 1)
            dve.wait_ge(acc_taken[1], (J_END - 1) // 2)
            layer_norm(1)


def t5_bucket(dist):
    n = np.maximum(dist, 0)
    exact = BUCKETS // 2
    nf = np.maximum(n, 1).astype(np.float32)
    large = exact + (np.log(nf / np.float32(exact)) / np.float32(math.log(MAX_DIST / exact))
                     * np.float32(BUCKETS - exact)).astype(np.int32)
    return np.where(n < exact, n, np.minimum(large, BUCKETS - 1))


def constants():
    f = np.float32
    dist = 2 * P - 1 - np.arange(384)
    onehot = (t5_bucket(dist)[None, :] == np.arange(BUCKETS)[:, None]).astype(f)
    c, s = np.arange(P)[:, None], np.arange(P)[None, :]
    masks = []
    for lv in range(LEVELS):
        b = 2 ** lv
        masks.append((c // (2 * b) == s // (2 * b)) & (c // b == s // b + 1))
    same = c // CHUNK == s // CHUNK
    masks += [same & (c > s), same & (c <= s), same, c <= s]
    masks = np.stack(masks).astype(f)
    key = np.concatenate([np.arange(P), np.arange(S) - P])[None, :]
    causal = np.where(key <= np.arange(P)[:, None], 0.0, NEG).astype(f)
    inv = f(10000.0) ** (-np.arange(0, RET_QK, 2, dtype=f) / f(RET_QK))
    ang = np.arange(S, dtype=f)[:, None] * inv[None, :]
    rope = np.stack([np.cos(ang), np.sin(ang)]).astype(f)
    lg = np.log1p(-np.exp2(-5.0 - np.arange(RET_HEADS, dtype=f)).astype(f)).astype(f)
    pos = np.arange(P, dtype=f)
    diff = pos[None, :] - pos[:, None]
    intra = np.where(diff[:, None, :] >= 0, np.exp(np.maximum(diff, 0)[:, None, :] * lg[None, :, None]), 0.0)
    decay = np.stack([np.exp((pos[:, None] + 1) * lg[None, :]), np.exp((P - 1 - pos[:, None]) * lg[None, :])])
    return {"c_onehot": onehot, "c_masks": masks, "c_causal": causal, "c_rope": rope,
            "c_intra": intra.astype(f), "c_decay": decay.astype(f)}


_INS = ["x", "rel_table", "ln1_w", "w_in", "cmp_pe_k", "cmp_pe_v", "cmp_w1_k", "cmp_w2_k", "cmp_w1_v",
        "cmp_w2_v", "conv_w", "a_log", "dt_bias", "gdn_norm_w", "w_pa", "w_pb", "w_o", "ln2_w", "w_up",
        "w_down", "ln_f_w", "fox_w_in_2", "fox_b_f_2", "fox_q_gain_2", "fox_k_gain_2", "fox_w_out_2",
        "ret_w_in_2", "ret_w_out_2", "ln_gain_2", "ln_bias_2"]


def kernel(**inputs):
    import concourse.bacc as bacc
    from concourse.bass_utils import run_bass_kernel_spmd

    nc = bacc.Bacc("TRN2", target_bir_lowering=False, num_devices=1)
    arrays, args = {}, []

    def add(name, a):
        arrays[name] = a
        args.append(nc.dram_tensor(name, a.shape, mybir.dt.from_np(a.dtype), kind="ExternalInput").ap())

    for name in _INS:
        a = np.ascontiguousarray(inputs[name])
        if a.ndim > 1 and a.shape[0] == 1:
            a = a[0]
        add("in_" + name, a)
    for name, a in constants().items():
        add(name, np.ascontiguousarray(a))
    args.append(nc.dram_tensor("out_x", (S, D), F32, kind="ExternalOutput").ap())
    build(nc, *args)
    r = run_bass_kernel_spmd(nc, [arrays], core_ids=[0])
    return r.results[0]["out_x"].reshape(1, S, D)
```

```python
import math
from contextlib import ExitStack

import numpy as np

import concourse.bass as bass
from concourse import mybir

F32 = mybir.dt.float32
F32R = mybir.dt.float32r
ALU = mybir.AluOpType
ACT = mybir.ActivationFunctionType
AX = mybir.AxisListType

P = 128
S = 256
NT = S // P
D = 2048
KT = D // P
NB = 512
GPJ = 8
CPJ = 4
HD = 128
NH = 8
HG = 4
CMP_BLOCK, CMP_STRIDE = 32, 16
NCMP = S // CMP_STRIDE - 1
NC0 = (P - CMP_BLOCK) // CMP_STRIDE + 1
NKV = 2
CMP_HIDDEN = 256
BUCKETS, MAX_DIST = 32, 128
CHUNK = 64
LEVELS = 6
FOX_HEADS = 16
RET_HEADS, RET_QK, RET_V = 8, 256, 512
NEG = -1e30
NORM_EPS, LN_EPS = 1e-6, 1e-5
ALPHA = (2.0 * 2) ** 0.25
SEG = P + S
SEGC = SEG + NC0 + NCMP
ATT_SCALE = HD ** -0.5

C_NSA = 0
C_GATE = NH * HD + 6 * NKV * HD
C_GDN = C_GATE + 3 * NH
C_AB = C_GDN + 4 * NH * HD
C_MERGE = C_AB + 2 * NH

J_NSA = 0
J_CMP = J_NSA + (NH * HD + 6 * NKV * HD) // NB
J_GDN = J_CMP + 2
J_MERGE = J_GDN + 8
J_PAB = J_MERGE + 8
J_WO = J_PAB + 4
J_MLP = J_WO + 4
J_FOX = J_MLP + 32
J_FOXO = J_FOX + 16
J_RET = J_FOXO + 4
J_END = J_RET + 32


class Lin:

    def __init__(self, c, terms=()):
        self.c, self.terms = c, tuple(terms)

    def __add__(self, k):
        if isinstance(k, Lin):
            return Lin(self.c + k.c, self.terms + k.terms)
        return Lin(self.c + k, self.terms)

    def __sub__(self, k):
        return Lin(self.c - k, self.terms)

    def __mul__(self, k):
        return Lin(self.c * k, [(a * k, v) for a, v in self.terms])

    def half(self):
        assert all(a % 2 == 0 for a, _ in self.terms)
        return Lin(self.c // 2, [(a // 2, v) for a, v in self.terms])

    def value(self):
        v = self.c
        for a, r in self.terms:
            v = r * a + v
        return v


def lin(i):
    return i if isinstance(i, Lin) else Lin(0, [(1, i)]) if not isinstance(i, int) else Lin(i)


def wait(eng, sem, n):
    n = lin(n)
    assert n.c > 0 or not n.terms, "a wait against a register that is 0 in the first round"
    if n.c > 0:
        eng.wait_ge(sem, n.value())


class Chain:

    def __init__(self, eng, sem, start=0):
        self.eng, self.sem, self.start, self.k = eng, sem, lin(start), 0

    def link(self, ins):
        ins.then_inc(self.sem, 1)
        self.k += 1
        wait(self.eng, self.sem, self.start + self.k)

    def end(self, k):
        assert self.k == k, f"the chain has {self.k} steps, not {k}"


K_FOX_DVE, K_RET_DVE = 9, 8


def build(nc, x, rel_table, ln1_w, w_in, pe_k, pe_v, w1_k, w2_k, w1_v, w2_v, conv_w, a_log, dt_bias,
          gdn_norm_w, w_pa, w_pb, w_o, ln2_w, w_up, w_down, ln_f_w, fox_w_in, fox_b_f, fox_q_gain,
          fox_k_gain, fox_w_out, ret_w_in, ret_w_out, ln_gain, ln_bias,
          c_onehot, c_masks, c_causal, c_rope, c_intra, c_decay, out):
    ctx = ExitStack()
    with ctx:
        def sb(name, shape, dt=F32):
            return ctx.enter_context(nc.sbuf_tensor(name, shape, dt))

        def sem(name):
            return ctx.enter_context(nc.semaphore(name))

        raw = sb("raw", [P, CPJ, 4, NB])
        w_hi = sb("w_hi", [P, 4, 2, NB], F32R)
        w_lo = sb("w_lo", [P, 4, 2, NB], F32R)
        lt_a = [sb("lt_a_hi", [P, KT, S], F32R), sb("lt_a_lo", [P, KT, S], F32R)]
        lt_b = [sb("lt_b_hi", [P, KT, S], F32R), sb("lt_b_lo", [P, KT, S], F32R)]
        res = sb("res", [P, NT, D])
        ARENA = 14592
        arena = sb("arena", [P, ARENA])
        ident = sb("ident", [P, P])
        w2 = sb("w2", [P, 2, 2, HD])
        cwt = sb("cwt", [P, 4 * 24])
        pet = sb("pet", [P, 2, CMP_BLOCK])
        gnorm = sb("gnorm", [P, HD])
        fgain = sb("fgain", [P, 2, HD])
        gates = sb("gates", [P, NT, 3 * NH])
        sm = sb("sm", [P, 320])

        def at(off, *shape):
            n = math.prod(shape)
            assert off + n <= ARENA, (off, shape)
            v = arena[:, off:off + n]
            if len(shape) == 2:
                v = v.rearrange("p (a b) -> p a b", b=shape[1])
            if len(shape) == 3:
                v = v.rearrange("p (a b c) -> p a b c", b=shape[1], c=shape[2])
            if len(shape) == 4:
                v = v.rearrange("p (a b c d) -> p a b c d", b=shape[1], c=shape[2], d=shape[3])
            return v

        used = [0]

        def small(*shape):
            n = math.prod(shape)
            v = sm[:, used[0]:used[0] + n]
            used[0] += n
            assert used[0] <= 320
            if len(shape) == 2:
                v = v.rearrange("p (a b) -> p a b", b=shape[1])
            if len(shape) == 3:
                v = v.rearrange("p (a b c) -> p a b c", b=shape[1], c=shape[2])
            return v

        mhalf = small(32)
        ssum = small(NT)
        rstd = small(NT)
        a_row = small(NH)
        dt_row = small(NH)
        bf_row = small(FOX_HEADS)
        lnst = small(NT, 4, 6)
        lnmv = small(NT, 2)
        lnr = small(NT)

        acc = [[ctx.enter_context(nc.psum_tensor(f"acc{a}{t}", [P, NB], F32)) for t in range(NT)]
               for a in range(2)]
        mx = ctx.enter_context(nc.psum_tensor("mx", [P, 4, NB], F32))

        x_loaded = [sem(f"x_loaded{t}") for t in range(NT)]
        raw_loaded = [sem(f"raw_loaded{i}") for i in range(CPJ)]
        hi_ready = sem("hi_ready")
        lo_ready = sem("lo_ready")
        granules_done = sem("granules_done")
        acc_taken = [sem("acc_taken0"), sem("acc_taken1")]
        lt_turned = sem("lt_turned")
        lt_hi_ready = sem("lt_hi_ready")
        lt_lo_ready = sem("lt_lo_ready")
        S_ = {}

        def sg(name):
            if name not in S_:
                S_[name] = sem(name)
            return S_[name]

        names = ("const_loaded w_loaded ident_ready row_loaded toep_loaded toep_stored store_done "
                 "sq_done ms_ready rstd_ready h_ready").split()
        for n in names:
            sg(n)

        block = ctx.enter_context(nc.Block())

        def load_job(sp, J, src, rows=512, chunks=CPJ):
            J = lin(J)
            for q in range(chunks):
                wait(sp, lo_ready, J * GPJ + 2 * q + 2 - GPJ)
                w = src(q)
                sp.dma_start(raw[:, q, :, :].rearrange("p a b -> p (a b)").rearrange(
                    "p (j n) -> p j n", j=rows // P), w.rearrange("(j p) n -> p j n", p=P)) \
                    .then_inc(raw_loaded[q], 16)

        def block_of(w, row0, col):
            def src(q):
                r = row0 + q * 512 if isinstance(row0, int) else row0 + q * 512
                rs = slice(r, r + 512) if isinstance(r, int) else bass.ds(r, 512)
                cs = slice(col, col + NB) if isinstance(col, int) else bass.ds(col, NB)
                return w[rs, cs]
            return src

        def split_hi(act, J, r0, r1):
            J = lin(J)
            for r in range(r0, r1):
                slot, half = (r % GPJ) // 2, r % 2
                if half == 0:
                    wait(act, raw_loaded[slot], (J + (1 + r // GPJ)) * 16)
                wait(act, granules_done, J * GPJ + r - 3)
                nc.scalar.activation(w_hi[:, r % 4], raw[:, slot, 2 * half:2 * half + 2, :],
                                     ACT.Copy).then_inc(hi_ready, 1)

        def split_lo(dve, J, r0, r1):
            J = lin(J)
            for r in range(r0, r1):
                slot, half = (r % GPJ) // 2, r % 2
                wait(dve, hi_ready, J * GPJ + r + 1)
                nc.vector.tensor_tensor(w_lo[:, r % 4], raw[:, slot, 2 * half:2 * half + 2, :],
                                        w_hi[:, r % 4].bitcast(F32), ALU.subtract) \
                    .then_inc(lo_ready, 1)

        def ahead(J):
            return GPJ + 4

        def multiply(pe, J, lt, par, hook=None, mix=None, fresh=None):
            J = lin(J)
            assert J.c % 2 == par
            wait(pe, acc_taken[par], J.half())
            for r in range(GPJ):
                if hook:
                    hook(r)
                step(mix)
                if fresh is not None:
                    wait(pe, lt_lo_ready, fresh + r + 1)
                wait(pe, lo_ready, J * GPJ + r + 1)
                for k in range(2):
                    kt = 2 * r + k
                    hi, lo = w_hi[:, r % 4, k, :], w_lo[:, r % 4, k, :]
                    for t in range(NT):
                        a_hi = lt[0][:, kt, t * P:(t + 1) * P]
                        a_lo = lt[1][:, kt, t * P:(t + 1) * P]
                        o = acc[par][t][:, :]
                        nc.tensor.matmul(o, a_hi, hi, start=(kt == 0), stop=False)
                        nc.tensor.matmul(o, a_hi, lo, start=False, stop=False)
                        last = nc.tensor.matmul(o, a_lo, hi, start=False, stop=(kt == KT - 1))
                last.then_inc(granules_done, 1)

        def step(mix):
            if mix is not None:
                next(mix, None)

        def split_job(split, eng, J, mix=None):
            for r in range(GPJ):
                step(mix)
                split(eng, J, r + 4, r + 5)

        def take(eng, J, par, ops):
            wait(eng, granules_done, lin(J) * GPJ + GPJ)
            for t in range(NT):
                last = ops(t)
            last.then_inc(acc_taken[par], 1)

        def turn(pe, B, src, n, ready=None):
            B = lin(B)
            wait(pe, lt_lo_ready, B)
            for b in range(n):
                if ready and b % 2 == 0:
                    wait(pe, ready[0], ready[1] + b // 2 + 1)
                if b >= 4:
                    wait(pe, lt_lo_ready, B + b - 3)
                for c in range(2):
                    for t in range(NT):
                        last = nc.tensor.transpose(mx[:, b % 4, (2 * c + t) * P:(2 * c + t + 1) * P],
                                                   src(2 * b + c, t), ident[:, :])
                last.then_inc(lt_turned, 1)

        def turn_hi(act, B, dst, n):
            B = lin(B)
            for b in range(n):
                wait(act, lt_turned, B + b + 1)
                nc.scalar.activation(dst(b)[0], mx[:, b % 4, :].rearrange("p (c s) -> p c s", s=S),
                                     ACT.Copy).then_inc(lt_hi_ready, 1)

        def turn_lo(dve, B, dst, n):
            B = lin(B)
            for b in range(n):
                wait(dve, lt_hi_ready, B + b + 1)
                hi, lo = dst(b)
                nc.vector.tensor_tensor(lo, mx[:, b % 4, :].rearrange("p (c s) -> p c s", s=S),
                                        hi.bitcast(F32), ALU.subtract).then_inc(lt_lo_ready, 1)

        def whole(lt):
            return lambda b: (lt[0][:, 2 * b:2 * b + 2, :], lt[1][:, 2 * b:2 * b + 2, :])

        def part(lt, kt):
            return lambda b: (lt[0][:, bass.ds(kt + 2 * b, 2), :], lt[1][:, bass.ds(kt + 2 * b, 2), :])

        B_LN1, B_OA = 0, 8
        B_OB = B_OA + 4
        B_Y = B_OB + 4
        B_LN2 = B_Y + 8
        B_U = B_LN2 + 8
        B_LNF = B_U + 32
        B_FO = B_LNF + 8
        B_LNG = B_FO + 8
        B_RO = B_LNG + 8

        h_nat = at(0, NT, D)
        w_row = at(NT * D, 2, D)

        def rms_act(act, k):
            for t in range(NT):
                if k == 0:
                    act.wait_ge(x_loaded[t], 16)
                last = nc.scalar.activation(h_nat[:, t, :], res[:, t, :], ACT.Square,
                                            accum_out=ssum[:, t:t + 1])
            last.then_inc(sg("sq_done"), 1)

        def rms_dve(dve, k, dst):
            dve.wait_ge(sg("sq_done"), k + 1)
            nc.vector.tensor_scalar(ssum, ssum, 1.0 / D, NORM_EPS, ALU.mult, ALU.add) \
                .then_inc(sg("ms_ready"), 1)
            dve.wait_ge(sg("rstd_ready"), k + 1)
            dve.wait_ge(sg("row_loaded"), 16 * k) if k else dve.wait_ge(sg("first_row_loaded"), 16)
            for c in range(D // NB):
                cs = slice(c * NB, c * NB + NB)
                for t in range(NT):
                    last = nc.vector.scalar_tensor_tensor(dst[:, t, cs], res[:, t, cs], rstd[:, t:t + 1],
                                                          w_row[:, 0, cs], ALU.mult, ALU.mult)
                last.then_inc(sg("h_ready"), 1)

        def root_pool(pool, src_ready, n, base, dst, w, done):
            wait(pool, src_ready, n)
            nc.gpsimd.tensor_tensor(dst, base, mhalf[:, 0:w], ALU.pow).then_inc(done, 1)

        nat = at(0, 5, NT, NB)
        T = at(5120, 16, S)
        bm = at(9216, NH, SEGC)
        sc = at(0, HG, SEG)
        scc = at(1536, NH, NC0 + NCMP)
        pt = at(12464, HG, SEG)
        o_nat = at(5120 + 8 * S, NT, HG, HD)
        blk = at(2 * 1024, 960)
        wsmall = at(12464, KT, 40)
        onehot = at(9216, 384)
        tabl = at(9216 + 384, NH)
        distb = at(9216 + 400, 384)
        pe_nat = at(14000, 2, HD)
        cw_nat = at(14000 + 256, HD)
        cmp_hid = at(2048 + 0, 2, CMP_HIDDEN)
        cmp_hT = at(2048 + 512, 4, NKV * NCMP)
        kcT = at(2048 + 632, NKV * NCMP)
        vc = at(2048 + 662, NKV, HD)
        cb = [lt.rearrange("p a b -> p (a b)")[:, 0:2 * 960].rearrange("p (v n) -> p v n", v=2)
              for lt in (lt_b[0][:, :, :], lt_b[1][:, :, :])]
        mask0 = small(NC0)
        rowmax = small(2, HG)
        esum = small(2, HG)
        c_max = small(2, NH)
        c_sum = small(2, NH)
        c_coef = at(14000, 3, NT, NH)
        coef = small(3, NT, HG)
        att = {n: sg(n) for n in ("scores_ready scores_taken rowmax_ready exp_done probs_turned probs_copied "
                                  "att_out_ready att_out_taken").split()}

        def unit_pe(pe, u, sc, pt, q, k, v, slots=6):
            u = lin(u)
            wait(pe, att["att_out_taken"], u)
            for j in range(HG):
                nc.tensor.matmul(mx[:, j, 0:P], q(j)[:, 0:P], k(j)[:, 0:P], start=True, stop=True)
                last = nc.tensor.matmul(mx[:, j, P:SEG], q(j)[:, P:S], k(j), start=True, stop=True)
            last.then_inc(att["scores_ready"], 1)
            for _ in range(slots - 2):
                yield
            wait(pe, att["exp_done"], u + 1)
            for j in range(HG):
                for b in range(3):
                    last = nc.tensor.transpose(mx[:, j, b * P:(b + 1) * P], sc[:, j, b * P:(b + 1) * P],
                                               ident[:, :])
            last.then_inc(att["probs_turned"], 1)
            yield
            wait(pe, att["probs_copied"], u + 1)
            for j in range(HG):
                nc.tensor.matmul(mx[:, 0, j * HD:(j + 1) * HD], pt[:, j, 0:P], v(j, 0), start=True, stop=True)
                nc.tensor.matmul(mx[:, 1, j * HD:(j + 1) * HD], pt[:, j, P:S], v(j, 0), start=True, stop=False)
                last = nc.tensor.matmul(mx[:, 1, j * HD:(j + 1) * HD], pt[:, j, S:SEG], v(j, 1),
                                        start=False, stop=True)
            last.then_inc(att["att_out_ready"], 1)
            yield

        def unit_act(act, u, sc, pt, slots=6):
            u = lin(u)
            for _ in range(slots - 4):
                yield
            wait(act, att["rowmax_ready"], u + 1)
            for t, (a, b) in enumerate(((0, P), (P, SEG))):
                for j in range(HG):
                    last = nc.scalar.activation(sc[:, j, a:b], sc[:, j, a:b], ACT.Exp,
                                                bias=rowmax[:, t, j:j + 1], accum_out=esum[:, t, j:j + 1])
                if t == 0:
                    yield
            last.then_inc(att["exp_done"], 1)
            yield
            wait(act, att["probs_turned"], u + 1)
            nc.scalar.activation(pt[:, :, :], mx[:, :, 0:SEG], ACT.Copy).then_inc(att["probs_copied"], 1)
            yield
            yield

        def unit_dve(dve, u, ch, sc, o_nat, bias, gate, first, slots=6):
            u = lin(u)
            wait(dve, att["scores_ready"], u + 1)
            ch.link(nc.vector.scalar_tensor_tensor(sc[:, :, :], mx[:, :, 0:SEG], ATT_SCALE, bias,
                                                   ALU.mult, ALU.add))
            yield
            nc.vector.tensor_reduce(rowmax[:, 0, :], sc[:, :, 0:P], AX.X, ALU.max, negate=True)
            nc.vector.tensor_reduce(rowmax[:, 1, :], sc[:, :, P:SEG], AX.X, ALU.max, negate=True) \
                .then_inc(att["rowmax_ready"], 1)
            for _ in range(slots - 3):
                yield
            wait(dve, att["exp_done"], u + 1)
            ch.link(nc.vector.tensor_scalar(coef[:, 0], esum[:, 0:2], 1e-30, None, ALU.max))
            ch.link(nc.vector.reciprocal(coef[:, 1], coef[:, 0]))
            if gate is None:
                gate = coef[:, 1]
            else:
                ch.link(nc.vector.tensor_tensor(coef[:, 2], coef[:, 1], gate, ALU.mult))
                gate = coef[:, 2]
            yield
            wait(dve, att["att_out_ready"], u + 1)
            for t in range(NT):
                for j in range(HG):
                    o = o_nat[:, t, j, :]
                    ps = mx[:, t, j * HD:(j + 1) * HD]
                    c = gate[:, t, j:j + 1]
                    if first:
                        last = nc.vector.tensor_scalar(o, ps, c, None, ALU.mult)
                    else:
                        last = nc.vector.scalar_tensor_tensor(o, ps, c, o, ALU.mult, ALU.add)
            last.then_inc(att["att_out_taken"], 1)
            wait(dve, att["att_out_taken"], u + 1)
            yield

        g_nat = res[:, :, :].rearrange("p a b -> p (a b)").rearrange("p (k t n) -> p k t n", k=4, t=NT)
        g_z = at(3072, NT, NB)
        g_ct = at(4096, 12, 260)
        g_cv = at(7216, 12, S)
        g_rn = at(10288, NT, 12, HD)
        g_mask = at(13360, LEVELS + 3, P)
        M_STRICT, M_TRI, M_ONES = LEVELS, LEVELS + 1, LEVELS + 2
        g_sq = at(4096, NT, 8, HD)
        g_vb, g_kbeg, g_kdec = (at(i * 1024, NT, HG, HD) for i in range(3))
        g_qg = at(4096 + 2048, NT, HG, HD)
        g_qT, g_kT, g_qgT = (at(7216 + i * 1024, HG, S) for i in range(3))
        g_dec, g_qkT, g_A = (at(10288 + i * 1024, HG * NT, P) for i in range(3))
        g_X, g_Y, g_P1 = (at(4096 + i * 1024, HG * NT, P) for i in range(3))
        g_U = g_dec
        g_wT = g_A
        g_o = at(4096, NT, HG, HD)
        g_S = at(4096 + 2048, HG, HD)
        g_V = at(4096 + 2048 + 512, HG, HD)
        G_G, G_BETA, G_CUM, G_E, G_KD, G_BEG = range(6)
        tok = sb("tok", [P, 6, NT, NH])
        tg = sb("tg", [P, 6, NT, HG])
        cwg = sb("cwg", [P, 12, HG])
        gss = small(NT, 8)
        grs = small(NT, 8)
        egl = small(HG * NT, 2)
        gt = [at(13200 + NT * NH * i, NT, NH) for i in range(3)]

        f_nat = at(0, 4, NT, NB)
        f_T = at(4096, 8, S)
        f_sc = at(6144, HG, SEG)
        f_pt = at(7680, HG, SEG)
        f_o = at(9216, NT, HG, HD)
        f_bias = at(10240, HG, SEG)
        f_causal = at(11776, SEG)
        f_logf = at(12160, NT, FOX_HEADS)
        f_lg = at(12192, NT, HG)
        f_ones = at(12208, P)
        f_t = [at(12336 + 32 * i, NT, FOX_HEADS) for i in range(3)]
        f_w = at(12448, KT, FOX_HEADS)
        f_ss = at(12704, NT, 8)
        f_rs = at(12720, NT, 8)
        tri = at(12736, P)

        mg_a = g_nat
        mg_b = at(4096, 4, NT, NB)
        y_nat = at(8192, NT, D)
        y_tmp = at(12288, NT, NB)
        relu = at(0, NT, NB)
        u_nat = at(1024, 2, NT, NB)

        r_nat = at(0, 6, NT, NB)
        r_T = at(6144, 8, S)
        r_qdT = at(8192, HG, P)
        r_kd = at(8704, 2, RET_QK)
        r_in = at(9216, 4, P)
        r_R = at(9728, 4, RET_V)
        r_D = at(11776, 2, P)
        r_cs = at(12032, 2, NT, P)
        r_tmp = at(12544, 4, NT * 2 * P)
        r_dec = small(2, RET_HEADS)
        r_st = small(NT, 6)
        r_mv = small(NT, 2)
        r_rs = small(NT)

        bias_dram = nc.dram_tensor("bias_by_distance", [NH, P, 384], F32).ap()

        def bcast(ap, n):
            return bass.AP(tensor=ap.tensor, offset=ap.offset, ap=[*ap.ap, [0, n]])

        def heads_bcast(ap, n):
            return bass.AP(tensor=ap.tensor, offset=ap.offset, ap=[ap.ap[0], [0, n], *ap.ap[1:]])

        N_CONST = 15
        NSA_BLOCKS = [2, 0, 1, 3, 4]
        NSA_ORDER = [4, 5, 0, 1, 2, 3, 6, 7]
        NSA_TILES = [(i // 4, i % 4) for i in range(8)] + [(2, 0), (2, 1), (2, 2), (2, 3), (3, 0), (3, 1),
                                                          (4, 0), (4, 1)]
        small_ps = mx[:, 0, 0:128].rearrange("p (t n) -> p t n", t=NT)

        def few(n):
            return [lt[:, 8:KT, :].rearrange("p a b -> p (a b)")[:, 0:KT * n].rearrange("p (k n) -> p k n", n=n)
                    for lt in (lt_b[0], lt_b[1])]

        few_ps = mx[:, 0, S:2 * S]
        few_T = at(NT * D, S)

        def few_copy(act, n, k):
            act.wait_ge(sg("few_ready"), k + 1)
            nc.scalar.activation(few_T[0:n, :], few_ps[0:n, :], ACT.Copy).then_inc(sg("few_copied"), 1)

        def few_hi(w, n):
            nc.scalar.activation(few(n)[0], w, ACT.Copy).then_inc(sg("small_hi"), 1)

        def few_lo(dve, w, n, k):
            dve.wait_ge(sg("small_hi"), k + 1)
            nc.vector.tensor_tensor(few(n)[1], w, few(n)[0].bitcast(F32), ALU.subtract).then_inc(sg("small_lo"), 1)

        @block.sync
        def _(sp):
            def fori(n):
                return sp.Fori(0, n)
            for t in range(NT):
                sp.dma_start(res[:, t, :], x[t * P:(t + 1) * P, :]).then_inc(x_loaded[t], 16)
            sp.dma_start(w_row[:, 0, :], ln1_w.partition_broadcast(P)).then_inc(sg("first_row_loaded"), 16)
            load_job(sp, 0, block_of(w_in, 0, C_NSA + NSA_BLOCKS[0] * NB))
            with fori(2) as i:
                for c in range(2):
                    assert NSA_BLOCKS[1 + c] == c and NSA_BLOCKS[3 + c] == 3 + c
                    load_job(sp, Lin(1 + c, [(2, i)]), block_of(w_in, 0, i * (3 * NB) + (C_NSA + c * NB)))
            for c, w in enumerate((w1_k, w1_v)):
                load_job(sp, J_CMP + c, lambda q, w=w: w[q * 1024:(q + 1) * 1024, :], rows=1024)
            with fori(2) as g:
                for kind in range(4):
                    load_job(sp, Lin(J_GDN + kind, [(4, g)]),
                             block_of(w_in, 0, g * NB + (C_GDN + kind * NH * HD)))
            with fori(4) as i:
                for c in range(2):
                    load_job(sp, Lin(J_MERGE + c, [(2, i)]), block_of(w_in, 0, i * (2 * NB) + (C_MERGE + c * NB)))
            with fori(2) as i:
                for c in range(2):
                    col = i * (2 * NB) + c * NB
                    load_job(sp, Lin(J_PAB + c, [(2, i)]),
                             lambda q, col=col: (w_pa, w_pb)[q // 2][(q % 2) * 512:(q % 2 + 1) * 512,
                                                                    bass.ds(col, NB)])
            with fori(2) as i:
                for c in range(2):
                    load_job(sp, Lin(J_WO + c, [(2, i)]), block_of(w_o, 0, i * (2 * NB) + c * NB))
            with fori(4) as g:
                for c in range(4):
                    load_job(sp, Lin(J_MLP + c, [(8, g)]), block_of(w_up, 0, g * D + c * NB))
                for c in range(4):
                    load_job(sp, Lin(J_MLP + 4 + c, [(8, g)]), block_of(w_down, g * D, c * NB))
            with fori(4) as g:
                for kind in range(4):
                    load_job(sp, Lin(J_FOX + kind, [(4, g)]), block_of(fox_w_in, 0, g * NB + kind * D))
            with fori(2) as i:
                for c in range(2):
                    load_job(sp, Lin(J_FOXO + c, [(2, i)]), block_of(fox_w_out, 0, i * (2 * NB) + c * NB))
            with fori(2) as h:
                with fori(2) as p:
                    J = Lin(J_RET, [(16, h), (6, p)])
                    load_job(sp, J, block_of(ret_w_in, 0, h * 1024 + p * NB))
                    load_job(sp, J + 1, block_of(ret_w_in, 0, h * 1024 + p * NB + D))
                    for c in range(4):
                        load_job(sp, J + 2 + c, block_of(ret_w_in, 0, h * 2048 + p * 1024
                                                         + (2 * D + (c // 2) * 2 * D + (c % 2) * NB)))
                for c in range(4):
                    load_job(sp, Lin(J_RET + 12 + c, [(16, h)]), block_of(ret_w_out, h * D, c * NB))
            load_job(sp, J_END, block_of(ret_w_out, 0, 0), chunks=2)
            for c in range(D // NB):
                sp.wait_ge(sg("ln_done"), D // NB + c + 1)
                sp.dma_start(out[:, c * NB:(c + 1) * NB].rearrange("(t p) d -> p t d", p=P),
                             res[:, :, c * NB:(c + 1) * NB]).then_inc(sg("store_done"), 16)
            sp.wait_ge(sg("store_done"), 16 * (D // NB))

        @block.gpsimd
        def _(pool):
            def fori(n):
                return pool.Fori(0, n)
            ch = Chain(pool, sg("pool_step"))

            def load(dst, src, s, n=None):
                pool.dma_start(dst, src).then_inc(sg(s), 16)

            ch.link(nc.gpsimd.memset(ident[:, :], 0.0))
            nc.gpsimd.affine_select(out=ident[:, :], in_=ident[:, :], compare_op=ALU.not_equal, fill=1.0,
                                    base=0, pattern=[[-1, P]], channel_multiplier=1) \
                .then_inc(sg("ident_ready"), 1)
            ch.link(nc.gpsimd.memset(mhalf, -0.5))
            ch.link(nc.gpsimd.memset(mask0, 1.0))
            ch.link(nc.gpsimd.affine_select(out=mask0, in_=mask0, compare_op=ALU.is_ge, fill=0.0,
                                            base=-(CMP_BLOCK - 1), pattern=[[-CMP_STRIDE, NC0]],
                                            channel_multiplier=1))
            root_pool(pool, sg("ms_ready"), 1, ssum, rstd, NT, sg("rstd_ready"))

            pool.wait_ge(sg("prep_taken"), 1)
            src = distb[0:NH, :]
            pool.dma_start(bias_dram, bass.AP(tensor=src.tensor, offset=src.offset,
                                              ap=[src.ap[0], [0, P], src.ap[1]])).then_inc(sg("toep_stored"), 16)
            pool.wait_ge(sg("toep_stored"), 16)
            for a, b, off in ((0, P, 2 * P - 1), (P, SEG, P - 1)):
                src = bass.AP(tensor=bias_dram.tensor, offset=off, ap=[[384 - 1, P], [384 * P, NH], [1, b - a]])
                pool.dma_start(bm[:, :, a:b], src).then_inc(sg("toep_loaded"), 16)
            pool.wait_ge(sg("toep_loaded"), 32)
            nc.gpsimd.affine_select(out=bm[:, :, 0:P], in_=bm[:, :, 0:P], compare_op=ALU.is_ge, fill=NEG,
                                    base=0, pattern=[[0, NH], [-1, P]], channel_multiplier=1) \
                .then_inc(sg("bias_masked"), 1)
            nc.gpsimd.affine_select(out=bm[:, :, P:SEG], in_=bm[:, :, P:SEG], compare_op=ALU.is_ge, fill=NEG,
                                    base=P, pattern=[[0, NH], [-1, S]], channel_multiplier=1) \
                .then_inc(sg("bias_masked"), 1)
            pool.wait_ge(lt_lo_ready, B_OB)
            load(g_mask[:, :, :], c_masks[0:LEVELS + 3].rearrange("m p c -> p m c"), "mask_loaded")
            with fori(2) as g:
                root_pool(pool, sg("gss_ready"), Lin(1, [(2, g)]),
                          gss.rearrange("p a b -> p (a b)"), grs.rearrange("p a b -> p (a b)"), 16,
                          sg("grs_ready"))
                root_pool(pool, sg("gss_ready"), Lin(2, [(2, g)]),
                          gss.rearrange("p a b -> p (a b)")[:, 0:8],
                          grs.rearrange("p a b -> p (a b)")[:, 0:8], 8, sg("grs_ready"))
            pool.wait_ge(sg("y_ready"), 4)
            load(res[:, :, :], x.rearrange("(t p) d -> p t d", p=P), "x_again")
            load(w_row[:, 0, :], ln2_w.partition_broadcast(P), "row_loaded")
            root_pool(pool, sg("ms_ready"), 2, ssum, rstd, NT, sg("rstd_ready"))
            pool.wait_ge(sg("h_ready"), 2 * (D // NB))
            load(w_row[:, 0, :], ln_f_w.partition_broadcast(P), "row_loaded")
            load(f_causal, c_causal, "fox_loaded")
            load(tri, c_masks[LEVELS + 3], "fox_loaded")
            load(f_w, fox_w_in[:, 4 * D:4 * D + FOX_HEADS].rearrange("(k p) n -> p k n", p=P), "fox_loaded")
            root_pool(pool, sg("ms_ready"), 3, ssum, rstd, NT, sg("rstd_ready"))
            pool.wait_ge(sg("h_ready"), 3 * (D // NB))
            nc.gpsimd.memset(f_ones[:, :], 1.0).then_inc(sg("f_ones_ready"), 1)
            with fori(4) as g:
                for kind in range(2):
                    root_pool(pool, sg("f_ms_ready"), Lin(kind + 1, [(2, g)]), f_ss[:, kind, :], f_rs[:, kind, :],
                              8, sg("f_rs_ready"))
            pool.wait_ge(sg("fo_ready"), 4)
            for i in range(2):
                load(w_row[:, i, :], (ln_gain, ln_bias)[i][0, :].partition_broadcast(P), "ln_row_loaded")
            root_pool(pool, sg("ln_ms_ready"), 1, lnr, rstd, NT, sg("ln_rs_ready"))
            pool.wait_ge(sg("ln_done"), D // NB)
            load(r_cs[:, :, :, :], c_rope.rearrange("a (t p) n -> p a t n", p=P), "ret_loaded")
            load(r_dec, c_decay.rearrange("a p n -> p a n"), "ret_loaded")
            with fori(2) as h:
                with fori(2) as p:
                    pr = Lin(0, [(2, h), (1, p)])
                    wait(pool, acc_taken[1], Lin(J_RET, [(16, h), (6, p)]).half() + 1)
                    pool.dma_start(r_D[:, :, :], c_intra[:, bass.ds(h * 4 + p * 2, 2), :]) \
                        .then_inc(sg("r_D_loaded"), 16)
                    for hh in range(2):
                        root_pool(pool, sg("r_ms_ready"), pr * 2 + (hh + 1), r_rs, r_rs, NT,
                                  sg("r_rs_ready"))
            for i in range(2):
                if i == 0:
                    pool.wait_ge(lt_lo_ready, B_RO + 16)
                load(w_row[:, i, :], (ln_gain, ln_bias)[i][1, :].partition_broadcast(P), "ln_row_loaded")
            root_pool(pool, sg("ln_ms_ready"), 2, lnr, rstd, NT, sg("ln_rs_ready"))

        @block.scalar
        def _(act):
            A = nc.scalar.activation

            def fori(n):
                return act.Fori(0, n)

            loads = [(onehot[0:BUCKETS, :], c_onehot), (tabl[0:BUCKETS, :], rel_table),
                     (cw_nat[0:96, :], conv_w.rearrange("w (c p) -> (w c) p", p=P)),
                     (pe_nat[0:CMP_BLOCK, 0, :], pe_k), (pe_nat[0:CMP_BLOCK, 1, :], pe_v),
                     (wsmall[:, :, 0:24], w_in[:, C_GATE:C_GDN].rearrange("(k p) n -> p k n", p=P)),
                     (wsmall[:, :, 24:40], w_in[:, C_AB:C_MERGE].rearrange("(k p) n -> p k n", p=P)),
                     (w2[:, 0, :, :], w2_k.rearrange("(c p) n -> p c n", p=P)),
                     (w2[:, 1, :, :], w2_v.rearrange("(c p) n -> p c n", p=P)),
                     (a_row, a_log.partition_broadcast(P)), (dt_row, dt_bias.partition_broadcast(P)),
                     (bf_row, fox_b_f.partition_broadcast(P)), (gnorm[:, :], gdn_norm_w.partition_broadcast(P)),
                     (fgain[:, 0, :], fox_q_gain.partition_broadcast(P)),
                     (fgain[:, 1, :], fox_k_gain.partition_broadcast(P))]
            for dst, src in loads:
                act.dma_start(dst, src).then_inc(sg("const_loaded"), 16)
            assert N_CONST == len(loads)

            rms_act(act, 0)
            split_hi(act, 0, 0, 4)
            turn_hi(act, B_LN1, whole(lt_a), 8)
            act.wait_ge(sg("const_loaded"), 16 * N_CONST)
            few_hi(wsmall[:, :, :], 40)

            def copy_job(J, dst, func=ACT.Copy, scale=1.0, mix=None):
                split_job(split_hi, act, J, mix)
                take(act, J, lin(J).c % 2, lambda t: A(dst(t), acc[lin(J).c % 2][t][:, :], func, scale=scale))

            def nsa_turned(n):
                b = NSA_ORDER[n]
                act.wait_ge(sg("nsa_turned"), n + 1)
                A(T[:, 2 * b:2 * b + 2, :], mx[:, n % 4, :].rearrange("p (c s) -> p c s", s=S),
                  ACT.Copy).then_inc(sg("nsa_copied"), 1)

            def blocks_mix():
                yield
                nsa_turned(0)
                nsa_turned(1)
                yield
                for kv in range(2):
                    yield
                    act.wait_ge(sg("blocks_ready"), kv + 1)
                    A(cb[0][:, kv, :], blk, ACT.Copy).then_inc(sg("blocks_hi"), 1)
                    yield
                yield
                yield
                act.wait_ge(sg("softplus_arg"), 1)
                act.wait_ge(sg("const_loaded"), 16 * N_CONST)
                A(gt[0], gt[0], ACT.Exp).then_inc(sg("act_step"), 1)
                act.wait_ge(sg("act_step"), 1)
                A(gt[0], gt[0], ACT.Ln, bias=1.0)
                A(a_row, a_row, ACT.Exp).then_inc(sg("softplus_done"), 1)
                for n, slots in ((2, 1), (4, 8)):
                    for _ in range(slots):
                        yield
                    nsa_turned(n)
                    nsa_turned(n + 1)
                for _ in range(8):
                    yield
                nsa_turned(6)

            mix = None
            for J, blkno in enumerate(NSA_BLOCKS):
                copy_job(J, lambda t: nat[:, blkno, t, :], mix=mix)
                if J == 0:
                    few_copy(act, 40, 0)
                    act.wait_ge(sg("gates_ready"), 1)
                    A(gates[:, :, :], small_ps[:, :, 0:24], ACT.Sigmoid)
                    A(gt[1], small_ps[:, :, 24:32], ACT.Copy)
                    A(tok[:, G_BETA], small_ps[:, :, 32:40], ACT.Sigmoid).then_inc(sg("gates_done"), 1)
                    mix = blocks_mix()

            split_hi(act, J_CMP, 4, 12)
            split_hi(act, J_CMP + 1, 4, 12)
            for kv in range(2):
                par = (J_CMP + kv) % 2
                wait(act, granules_done, (J_CMP + kv + 1) * GPJ)
                A(cmp_hid[0:NKV * NCMP, kv, :], acc[par][0][0:NKV * NCMP, 0:CMP_HIDDEN],
                  ACT.Gelu_apprx_tanh).then_inc(acc_taken[par], 1)

            def nsa_mix():
                nsa_turned(7)
                yield
                act.wait_ge(sg("hid_turned"), 1)
                A(cmp_hT, mx[:, 0, 0:4 * NKV * NCMP].rearrange("p (a b) -> p a b", a=4), ACT.Copy) \
                    .then_inc(sg("hid_copied"), 1)
                yield
                act.wait_ge(sg("cmp_ready"), 1)
                A(kcT, mx[:, 1, 0:NKV * NCMP], ACT.Copy)
                A(vc[0:NCMP, :, :], mx[0:NCMP, 2, 0:NKV * HD].rearrange("p (g d) -> p g d", g=NKV), ACT.Copy) \
                    .then_inc(sg("cmp_copied"), 1)
                yield
                yield
                act.wait_ge(sg("cmp_rowmax"), 1)
                for j in range(NH):
                    for t, (a, b) in enumerate(((0, NC0), (NC0, NC0 + NCMP))):
                        last = A(scc[:, j, a:b], scc[:, j, a:b], ACT.Exp, bias=c_max[:, t, j:j + 1])
                last.then_inc(sg("cmp_exp"), 1)
                yield
                yield
                for g in range(NKV):
                    act.wait_ge(sg("cmp_turned"), g + 1)
                    A(pt[0:NC0, :, 0:P], mx[0:NC0, :, 0:P], ACT.Copy)
                    A(pt[0:NCMP, :, P:S], mx[0:NCMP, :, P:S], ACT.Copy).then_inc(sg("cmp_probs_copied"), 1)
                    yield
                    yield
                    for b in range(2):
                        yield from unit_act(act, 2 * g + b, sc, pt, 5)
                    turn_hi(act, B_OA + 2 * g, part(lt_b, 4 * g), 2)
                    yield

            def gdn_mix(g):
                for b in range(6):
                    wait(act, sg("gct_turned"), 6 * g + b + 1)
                    A(g_ct[:, 2 * b:2 * b + 2, 3:3 + S], mx[:, b % 4, :].rearrange("p (c s) -> p c s", s=S),
                      ACT.Copy).then_inc(sg("gct_copied"), 1)
                    if b % 2:
                        wait(act, sg("gct_copied"), 6 * g + b + 1)
                        wait(act, sg("taps_ready"), g + 1)
                        for i in range(2 * b - 2, 2 * b + 2):
                            last = A(g_cv[:, i, :], g_ct[:, i, 0:S], ACT.Copy, scale=cwg[:, i // 4, i % 4:i % 4 + 1])
                        last.then_inc(sg("tap_done"), 1)
                        yield
                for kind in range(3):
                    wait(act, sg("conv_done"), 3 * g + kind + 1)
                    A(g_cv[:, 4 * kind:4 * kind + 4, :], g_cv[:, 4 * kind:4 * kind + 4, :], ACT.Silu) \
                        .then_inc(sg("silu_done"), 1)
                    if kind == 2:
                        wait(act, acc_taken[0], (J_GDN + 4 * g + 3) // 2 + 1)
                        A(g_z[:, :, :], g_nat[:, 3], ACT.Silu)
                    yield
                    for t in range(NT):
                        b = 2 * kind + t
                        wait(act, sg("grn_turned"), 6 * g + b + 1)
                        A(g_rn[:, t, 4 * kind:4 * kind + 4, :], mx[:, b % 4, :].rearrange("p (c s) -> p c s", s=HD),
                          ACT.Copy).then_inc(sg("grn_copied"), 1)
                    if g == 0 and kind == 0:
                        act.wait_ge(sg("gcum_ready"), 1)
                        A(tok[:, G_E], tok[:, G_CUM], ACT.Exp)
                        A(tok[:, G_KD], tok[:, G_KD], ACT.Exp).then_inc(sg("gexp_done"), 1)
                    yield
                for _ in range(3):
                    yield
                for b in range(6):
                    wait(act, sg("gqk_turned"), 6 * g + b + 1)
                    A(g_cv[:, 2 * b:2 * b + 2, :], mx[:, b % 4, :].rearrange("p (c s) -> p c s", s=S),
                      ACT.Copy).then_inc(sg("gqk_copied"), 1)
                    if b % 3 == 2:
                        yield
                yield
                wait(act, sg("gdiff_ready"), g + 1)
                A(g_dec[:, :, :], g_dec[:, :, :], ACT.Exp, scale=-1.0)
                A(egl, egl, ACT.Exp)
                A(g_qkT[:, :, :], g_qkT[:, :, :], ACT.Exp).then_inc(sg("gdecay_ready"), 1)
                yield
                yield
                yield
                for lv in range(LEVELS * g, LEVELS * g + LEVELS):
                    for b in range(2):
                        wait(act, sg("inv_p"), 2 * lv + b + 1)
                        A(g_P1[:, 4 * b:4 * b + 4, :], mx[:, b, :].rearrange("p (c s) -> p c s", s=P),
                          ACT.Copy).then_inc(sg("inv_p_copied"), 1)
                    yield
                wait(act, sg("uw_ready"), g + 1)
                A(g_U[:, :, :], mx[:, 0:2, :].rearrange("p b (c s) -> p (b c) s", s=P), ACT.Copy)
                A(g_wT[:, :, :], mx[:, 2:4, :].rearrange("p b (c s) -> p (b c) s", s=P), ACT.Copy) \
                    .then_inc(sg("uw_copied"), 1)
                yield
                for n in range(4):
                    t, r = n // 2, slice(CHUNK * (n % 2), CHUNK * (n % 2) + CHUNK)
                    wait(act, sg("ws_ready"), 4 * g + n + 1)
                    A(g_o[r, t, :, :], mx[r, 1, :].rearrange("p (h d) -> p h d", d=HD), ACT.Copy) \
                        .then_inc(sg("oq_copied"), 1)
                    yield

            mix = nsa_mix()
            for kind in range(4):
                copy_job(J_GDN + kind, lambda t, kind=kind: g_nat[:, kind, t, :], mix=mix)
            mix = gdn_mix(0)
            for kind in range(4):
                copy_job(J_GDN + 4 + kind, lambda t, kind=kind: g_nat[:, kind, t, :], mix=mix)
            turn_hi(act, B_OB, part(lt_b, NH), 2)

            mix = gdn_mix(1)
            for c in range(4):
                copy_job(J_MERGE + c, lambda t, c=c: mg_a[:, c, t, :], ACT.Sigmoid, mix=mix)
            turn_hi(act, B_OB + 2, part(lt_b, NH + HG), 2)
            with fori(2) as i:
                for c in range(2):
                    copy_job(Lin(J_MERGE + 4 + c, [(2, i)]),
                             lambda t: mg_b[:, bass.ds(i * 2 + c, 1), t, :].rearrange("p a n -> p (a n)"),
                             ACT.Sigmoid)
            for n in range(4):
                split_hi(act, J_PAB + n, 4, 8)
                if n:
                    turn_hi(act, B_Y + 2 * (n - 1), part(lt_a, 4 * (n - 1)), 2)
                split_hi(act, J_PAB + n, 8, 12)
            turn_hi(act, B_Y + 6, part(lt_a, 12), 2)
            with fori(2) as i:
                for c in range(2):
                    split_hi(act, Lin(J_WO + c, [(2, i)]), 4, 12)
            act.wait_ge(sg("wo_done"), 4)
            rms_act(act, 1)
            turn_hi(act, B_LN2, whole(lt_a), 8)
            with fori(4) as g:
                for c in range(5):
                    J = Lin(J_MLP + c, [(8, g)])
                    split_hi(act, J, 4, 6)
                    if c:
                        turn_hi(act, Lin(B_U + 2 * (c - 1), [(8, g)]), part(lt_b, 4 * (c - 1)), 2)
                    split_hi(act, J, 6, 12)
                    if c < 4:
                        wait(act, granules_done, J * GPJ + GPJ)
                        for t in range(NT):
                            last = A(relu[:, t, :], acc[J.c % 2][t][:, :], ACT.Relu)
                        last.then_inc(acc_taken[J.c % 2], 1)
                for c in range(5, 8):
                    split_hi(act, Lin(J_MLP + c, [(8, g)]), 4, 12)
            act.wait_ge(sg("down_done"), 16)
            rms_act(act, 2)
            turn_hi(act, B_LNF, whole(lt_a), 8)
            act.wait_ge(sg("fox_loaded"), 48)
            few_hi(f_w[:, :, :], FOX_HEADS)
            few_copy(act, FOX_HEADS, 1)

            act.wait_ge(sg("f_arg_ready"), 1)
            A(f_t[1], f_t[1], ACT.Exp).then_inc(sg("act_step"), 1)
            act.wait_ge(sg("act_step"), 2)
            A(f_t[1], f_t[1], ACT.Ln, bias=1.0).then_inc(sg("f_ln_done"), 1)
            def fox_mix(g):
                for kind in range(2):
                    for _ in range(4):
                        yield
                    for b in range(2 * kind, 2 * kind + 2):
                        wait(act, sg("fqk_turned"), Lin(b + 1, [(4, g)]))
                        A(f_T[:, 2 * b:2 * b + 2, :], mx[:, b % 2, :].rearrange("p (c s) -> p c s", s=S),
                          ACT.Copy).then_inc(sg("fqk_copied"), 1)
                    yield
                    if kind == 0:
                        for _ in range(3):
                            yield
                yield from unit_act(act, Lin(4, [(1, g)]), f_sc, f_pt)

            with fori(4) as g:
                mix = None
                for kind in range(4):
                    if kind == 1:
                        mix = fox_mix(g)
                    copy_job(Lin(J_FOX + kind, [(4, g)]), lambda t, kind=kind: f_nat[:, kind, t, :],
                             ACT.Silu if kind == 3 else ACT.Copy, mix=mix)
                turn_hi(act, Lin(B_FO, [(2, g)]), part(lt_b, g * HG), 2)
            with fori(2) as i:
                for c in range(2):
                    split_hi(act, Lin(J_FOXO + c, [(2, i)]), 4, 12)
            turn_hi(act, B_LNG, whole(lt_a), 8)

            def ret_mix(h, p):
                pr = Lin(0, [(2, h), (1, p)])
                for _ in range(7):
                    yield
                for b in range(4):
                    wait(act, sg("rqk_turned"), pr * 5 + b + 1)
                    A(r_T[:, 2 * b:2 * b + 2, :], mx[:, b % 4, :].rearrange("p (c s) -> p c s", s=S),
                      ACT.Copy).then_inc(sg("rqk_copied"), 1)
                    if b % 2:
                        yield
                wait(act, sg("rqk_turned"), pr * 5 + 5)
                A(r_qdT[:, :, :], mx[:, 0, :].rearrange("p (c s) -> p c s", s=P), ACT.Copy) \
                    .then_inc(sg("rqk_copied"), 1)
                yield
                yield
                for hh in range(2):
                    wait(act, sg("r_R_ready"), pr * 2 + hh + 1)
                    A(r_R[:, 2 * hh:2 * hh + 2, :], mx[:, 2:4, :], ACT.Copy) \
                        .then_inc(sg("r_R_copied"), 1)
                    for _ in range(6 if hh == 0 else 8):
                        yield
                turn_hi(act, Lin(B_RO, [(8, h), (4, p)]), part(lt_b, p * 8), 2)
                yield

            with fori(2) as h:
                with fori(2) as p:
                    J = Lin(J_RET, [(16, h), (6, p)])
                    mix = None
                    for c in range(6):
                        if c == 2:
                            mix = ret_mix(h, p)
                        copy_job(J + c, lambda t, c=c: r_nat[:, c, t, :],
                                 ACT.Silu if c > 3 else ACT.Copy, RET_QK ** -0.5 if c == 1 else 1.0, mix=mix)
                    turn_hi(act, Lin(B_RO + 2, [(8, h), (4, p)]), part(lt_b, p * 8 + 4), 2)
                for c in range(4):
                    split_hi(act, Lin(J_RET + 12 + c, [(16, h)]), 4, 12)

        @block.tensor
        def _(pe):
            MM, TR = nc.tensor.matmul, nc.tensor.transpose

            def fori(n):
                return pe.Fori(0, n)

            def small_mm(n, k):
                pe.wait_ge(sg("small_lo"), k + 1)
                w_hi_, w_lo_ = few(n)
                for kt in range(KT):
                    a_hi, a_lo = (lt_a[p][:, kt, :] for p in range(2))
                    MM(few_ps[0:n, :], w_hi_[:, kt, :], a_hi, start=(kt == 0), stop=False)
                    MM(few_ps[0:n, :], w_lo_[:, kt, :], a_hi, start=False, stop=False)
                    last = MM(few_ps[0:n, :], w_hi_[:, kt, :], a_lo, start=False, stop=(kt == KT - 1))
                last.then_inc(sg("few_ready"), 1)
                pe.wait_ge(sg("few_copied"), k + 1)
                for t in range(NT):
                    last = TR(small_ps[:, t, 0:n], few_T[0:n, t * P:(t + 1) * P], ident[0:n, 0:n])
                return last

            pe.wait_ge(sg("ident_ready"), 1)
            turn(pe, B_LN1, lambda c, t: h_nat[:, t, c * P:(c + 1) * P], 8, ready=(sg("h_ready"), 0))
            multiply(pe, 0, lt_a, 0, fresh=B_LN1)
            pe.wait_ge(sg("const_loaded"), 16 * N_CONST)
            MM(mx[0:NH, 1, 0:384], tabl[0:BUCKETS, :], onehot[0:BUCKETS, :], start=True, stop=True)
            TR(mx[:, 2, 0:96], cw_nat[0:96, :], ident[0:96, 0:96])
            for kv in range(2):
                last = TR(mx[:, 3, 32 * kv:32 * kv + 32], pe_nat[0:CMP_BLOCK, kv, :],
                          ident[0:CMP_BLOCK, 0:CMP_BLOCK])
            last.then_inc(sg("prep_ready"), 1)
            small_mm(40, 0).then_inc(sg("gates_ready"), 1)

            def turn_nsa(n):
                if n >= 4:
                    pe.wait_ge(sg("nsa_copied"), n - 3)
                for c in range(2):
                    blkno, col = NSA_TILES[2 * NSA_ORDER[n] + c]
                    for t in range(NT):
                        last = TR(mx[:, n % 4, (2 * c + t) * P:(2 * c + t + 1) * P],
                                  nat[:, blkno, t, col * P:(col + 1) * P], ident[:, :])
                last.then_inc(sg("nsa_turned"), 1)

            def blocks_mix():
                yield
                pe.wait_ge(acc_taken[0], 1)
                pe.wait_ge(sg("prep_taken"), 1)
                pe.wait_ge(sg("gates_done"), 1)
                turn_nsa(0)
                turn_nsa(1)
                for _ in range(8):
                    yield
                pe.wait_ge(acc_taken[1], 1)
                turn_nsa(2)
                turn_nsa(3)
                for _ in range(8):
                    yield
                pe.wait_ge(acc_taken[0], 2)
                turn_nsa(4)
                turn_nsa(5)
                for _ in range(8):
                    yield
                pe.wait_ge(acc_taken[1], 2)
                turn_nsa(6)

            mix = blocks_mix()
            for J in range(1, 5):
                multiply(pe, J, lt_a, J % 2, mix=mix)
            for kv in range(2):
                J, par = J_CMP + kv, (J_CMP + kv) % 2
                pe.wait_ge(acc_taken[par], J // 2)
                pe.wait_ge(sg("blocks_lo"), kv + 1)
                for r in range(GPJ):
                    pe.wait_ge(lo_ready, J * GPJ + r + 1)
                    for k in range(4):
                        j = 4 * r + k
                        hi, lo = (w[:, r % 4].rearrange("p a b -> p (a b)")[:, k * 256:(k + 1) * 256]
                                  for w in (w_hi, w_lo))
                        b_hi, b_lo = (cb[p][:, kv, j * 30:(j + 1) * 30] for p in range(2))
                        o = acc[par][0][0:NKV * NCMP, 0:CMP_HIDDEN]
                        MM(o, b_hi, hi, start=(j == 0), stop=False)
                        MM(o, b_hi, lo, start=False, stop=False)
                        last = MM(o, b_lo, hi, start=False, stop=(j == CMP_BLOCK - 1))
                    last.then_inc(granules_done, 1)

            def nsa_mix():
                pe.wait_ge(acc_taken[0], 3)
                turn_nsa(7)
                yield
                n = NKV * NCMP
                pe.wait_ge(acc_taken[J_CMP % 2], J_CMP // 2 + 1)
                pe.wait_ge(acc_taken[(J_CMP + 1) % 2], (J_CMP + 1) // 2 + 1)
                pe.wait_ge(sg("nsa_copied"), 7)
                for kv in range(2):
                    for c in range(2):
                        last = TR(mx[:, 0, (2 * kv + c) * n:(2 * kv + c + 1) * n],
                                  cmp_hid[0:n, kv, c * P:(c + 1) * P], ident[0:n, 0:n])
                last.then_inc(sg("hid_turned"), 1)
                yield
                pe.wait_ge(sg("hid_copied"), 1)
                for c in range(2):
                    MM(mx[:, 1, 0:n], w2[:, 0, c, :], cmp_hT[:, c, :], start=(c == 0), stop=(c == 1))
                for g in range(NKV):
                    for c in range(2):
                        last = MM(mx[0:NCMP, 2, g * HD:(g + 1) * HD], cmp_hT[:, 2 + c, g * NCMP:(g + 1) * NCMP],
                                  w2[:, 1, c, :], start=(c == 0), stop=(c == 1))
                last.then_inc(sg("cmp_ready"), 1)
                yield
                pe.wait_ge(sg("cmp_copied"), 1)
                pe.wait_ge(sg("nsa_copied"), 8)
                for g in range(NKV):
                    kc, o = kcT[:, g * NCMP:(g + 1) * NCMP], g * (NC0 + NCMP)
                    for j in range(HG):
                        MM(mx[:, j, o:o + NC0], T[:, HG * g + j, 0:P], kc[:, 0:NC0], start=True, stop=True)
                        last = MM(mx[:, j, o + NC0:o + NC0 + NCMP], T[:, HG * g + j, P:S], kc,
                                  start=True, stop=True)
                last.then_inc(sg("cmp_scores"), 1)
                yield
                yield
                yield
                for g in range(NKV):
                    pe.wait_ge(sg("cmp_probs"), 1)
                    for j in range(HG):
                        TR(mx[0:NC0, j, 0:P], scc[:, HG * g + j, 0:NC0], ident[:, :])
                        last = TR(mx[0:NCMP, j, P:S], scc[:, HG * g + j, NC0:NC0 + NCMP], ident[:, :])
                    last.then_inc(sg("cmp_turned"), 1)
                    yield
                    pe.wait_ge(sg("cmp_probs_copied"), g + 1)
                    for j in range(HG):
                        MM(mx[:, 0, j * HD:(j + 1) * HD], pt[0:NC0, j, 0:P], vc[0:NC0, g, :],
                           start=True, stop=True)
                        last = MM(mx[:, 1, j * HD:(j + 1) * HD], pt[0:NCMP, j, P:S], vc[0:NCMP, g, :],
                                  start=True, stop=True)
                    last.then_inc(sg("cmp_out_ready"), 1)
                    yield
                    pe.wait_ge(sg("cmp_out_taken"), g + 1)
                    for b in range(2):
                        yield from unit_pe(pe, 2 * g + b, sc, pt, lambda j: T[:, HG * g + j, :],
                                           lambda j: T[:, 12 + 2 * b + g, :],
                                           lambda j, t: nat[:, 3 + b, t, (2 + g) * HD:(3 + g) * HD], 5)
                    pe.wait_ge(att["att_out_taken"], 2 * g + 2)
                    turn(pe, B_OA + 2 * g, lambda c, t: o_nat[:, t, c, :], 2)
                    yield
                    pe.wait_ge(lt_lo_ready, B_OA + 2 * g + 2)

            def gdn_mix(g):
                for b in range(6):
                    if b >= 4:
                        wait(pe, sg("gct_copied"), 6 * g + b - 3)
                    for c in range(2):
                        i = 2 * b + c
                        for t in range(NT):
                            last = TR(mx[:, b % 4, (2 * c + t) * P:(2 * c + t + 1) * P],
                                      g_nat[:, i // 4, t, (i % 4) * P:(i % 4 + 1) * P], ident[:, :])
                    last.then_inc(sg("gct_turned"), 1)
                    if b % 2:
                        yield
                if g == 0:
                    pe.wait_ge(sg("mask_loaded"), 16)
                    pe.wait_ge(sg("gct_copied"), 3)
                    for t in range(NT):
                        MM(mx[:, 2, t * NH:(t + 1) * NH], g_mask[:, M_TRI, :], tok[:, G_G, t, :],
                           start=True, stop=True)
                        last = MM(mx[:, 2, (2 + t) * NH:(3 + t) * NH], g_mask[:, M_ONES, :], tok[:, G_G, t, :],
                                  start=True, stop=True)
                    last.then_inc(sg("gsum_ready"), 1)
                yield
                for kind in range(3):
                    wait(pe, sg("silu_done"), 3 * g + kind + 1)
                    if kind == 0:
                        wait(pe, sg("gct_copied"), 6 * g + 6)
                    if kind == 1:
                        pe.wait_ge(sg("gcum_ready"), 1)
                    if kind == 2:
                        wait(pe, sg("grn_copied"), 6 * g + 2)
                    for t in range(NT):
                        b = 2 * kind + t
                        for c in range(4):
                            last = TR(mx[:, b % 4, c * P:(c + 1) * P],
                                      g_cv[:, 4 * kind + c, t * P:(t + 1) * P], ident[:, :])
                        last.then_inc(sg("grn_turned"), 1)
                    yield
                    yield
                yield
                yield
                wait(pe, sg("g_normed"), g + 1)
                for b in range(6):
                    if b >= 4:
                        wait(pe, sg("gqk_copied"), 6 * g + b - 3)
                    for c in range(2):
                        i = 2 * b + c
                        for t in range(NT):
                            src = g_rn[:, t, i, :] if i < 8 else g_qg[:, t, i - 8, :]
                            last = TR(mx[:, b % 4, (2 * c + t) * P:(2 * c + t + 1) * P], src, ident[:, :])
                    last.then_inc(sg("gqk_turned"), 1)
                    if b % 3 == 2:
                        yield
                wait(pe, sg("gqk_copied"), 6 * g + 6)
                for i in range(HG * NT):
                    last = MM(mx[:, i // 4, (i % 4) * P:(i % 4 + 1) * P],
                              tg[:, G_G, i % NT, i // NT:i // NT + 1].to_broadcast([P, P]), g_mask[:, M_TRI, :],
                              start=True, stop=True)
                last.then_inc(sg("gb_ready"), 1)
                for i in range(HG * NT):
                    k = g_kT[:, i // NT, (i % NT) * P:(i % NT + 1) * P]
                    last = MM(mx[:, 2 + i // 4, (i % 4) * P:(i % 4 + 1) * P], k, k, start=True, stop=True)
                last.then_inc(sg("kk_ready"), 1)
                yield
                yield
                wait(pe, sg("gdiff_ready"), g + 1)
                for i in range(HG * NT):
                    ts = slice((i % NT) * P, (i % NT + 1) * P)
                    last = MM(mx[:, i // 4, (i % 4) * P:(i % 4 + 1) * P], g_kT[:, i // NT, ts],
                              g_qT[:, i // NT, ts], start=True, stop=True)
                last.then_inc(sg("qk_ready"), 1)
                yield
                yield
                for l in range(LEVELS):
                    for b in range(2):
                        wait(pe, sg("inv_c"), 2 * ((LEVELS + 1) * g + l) + b + 1)
                        for i in range(4 * b, 4 * b + 4):
                            last = MM(mx[:, b, (i % 4) * P:(i % 4 + 1) * P], g_dec[:, i, :], g_Y[:, i, :],
                                      start=True, stop=True)
                        last.then_inc(sg("inv_p"), 1)
                    for b in range(2):
                        wait(pe, sg("inv_p_copied"), 2 * (LEVELS * g + l) + b + 1)
                        for i in range(4 * b, 4 * b + 4):
                            MM(mx[:, 2 + b, (i % 4) * P:(i % 4 + 1) * P], g_X[:, i, :], g_P1[:, i, :],
                               start=True, stop=True)
                        for i in range(4 * b, 4 * b + 4):
                            last = MM(mx[:, b, (i % 4) * P:(i % 4 + 1) * P], g_P1[:, i, :], g_X[:, i, :],
                                      start=True, stop=True)
                        last.then_inc(sg("inv_q"), 1)
                    yield
                wait(pe, sg("inv_c"), 2 * (LEVELS + 1) * (g + 1))
                for i in range(HG * NT):
                    t, h = i % NT, i // NT
                    MM(mx[:, i // 4, (i % 4) * P:(i % 4 + 1) * P], g_Y[:, i, :], g_vb[:, t, h, :],
                       start=True, stop=True)
                    last = MM(mx[:, 2 + i // 4, (i % 4) * P:(i % 4 + 1) * P], g_kbeg[:, t, h, :],
                              g_Y[:, i, :], start=True, stop=True)
                last.then_inc(sg("uw_ready"), 1)
                yield
                wait(pe, sg("uw_copied"), g + 1)
                for n in range(4):
                    t, r = n // 2, slice(CHUNK * (n % 2), CHUNK * (n % 2) + CHUNK)
                    wait(pe, sg("s_ready"), 5 * g + n + 1)
                    if n:
                        wait(pe, sg("oq_copied"), 4 * g + n)
                    for h in range(HG):
                        MM(mx[:, 0, h * HD:(h + 1) * HD], g_wT[:, h * NT + t, :], g_S[:, h, :],
                           start=True, stop=True)
                    for h in range(HG):
                        last = MM(mx[r, 1, h * HD:(h + 1) * HD], g_qgT[:, h, t * P + r.start:t * P + r.stop],
                                  g_S[:, h, :], start=True, stop=True)
                    last.then_inc(sg("ws_ready"), 1)
                    wait(pe, sg("v_ready"), 4 * g + n + 1)
                    for h in range(HG):
                        last = MM(mx[:, 2, h * HD:(h + 1) * HD], g_kdec[r, t, h, :], g_V[r, h, :],
                                  start=True, stop=True)
                    last.then_inc(sg("su_ready"), 1)
                    if n % 2:
                        for h in range(HG):
                            last = MM(mx[:, 3, h * HD:(h + 1) * HD], g_qkT[:, h * NT + t, :], g_V[:, h, :],
                                      start=True, stop=True)
                        last.then_inc(sg("in_ready"), 1)
                    yield

            mix = nsa_mix()
            for kind in range(4):
                multiply(pe, J_GDN + kind, lt_a, (J_GDN + kind) % 2, mix=mix)
            assert next(mix, "over") == "over"
            for g in range(2):
                mix = gdn_mix(g)
                for kind in range(4):
                    J = (J_GDN + 4 if g == 0 else J_MERGE) + kind
                    multiply(pe, J, lt_a, J % 2, mix=mix)
                wait(pe, sg("go_ready"), g + 1)
                turn(pe, B_OB + 2 * g, lambda c, t: g_o[:, t, c, :], 2)
                if g == 0:
                    wait(pe, lt_lo_ready, B_OB + 2)

            with fori(2) as i:
                for c in range(2):
                    J = Lin(J_MERGE + 4 + c, [(2, i)])
                    multiply(pe, J, lt_a, J.c % 2)
            def turn_y_block(n):
                turn(pe, B_Y + 2 * n, lambda c, t: y_nat[:, t, n * NB + c * P:n * NB + (c + 1) * P], 2,
                     ready=(sg("y_ready"), n))

            for n in range(4):
                J = J_PAB + n
                for r in range(GPJ):
                    if n == 0 and r == 0:
                        pe.wait_ge(lt_lo_ready, B_OB + 4)
                        wait(pe, acc_taken[0], (J + 1) // 2)
                        wait(pe, acc_taken[1], J // 2)
                    if n and r == 0:
                        pe.wait_ge(sg("pab_taken"), n)
                    if n and r == 3:
                        turn_y_block(n - 1)
                    if n and r == 4:
                        wait(pe, acc_taken[(J - 1) % 2], (J - 1) // 2 + 1)
                    wait(pe, lo_ready, J * GPJ + r + 1)
                    for k in range(2):
                        kt = 2 * r + k
                        for t in range(NT):
                            a_hi, a_lo = (lt_b[p][:, kt, t * P:(t + 1) * P] for p in range(2))
                            o = acc[kt // 8][t][:, :]
                            MM(o, a_hi, w_hi[:, r % 4, k, :], start=(kt % 8 == 0), stop=False)
                            MM(o, a_hi, w_lo[:, r % 4, k, :], start=False, stop=False)
                            last = MM(o, a_lo, w_hi[:, r % 4, k, :], start=False, stop=(kt % 8 == 7))
                    last.then_inc(granules_done, 1)
            turn_y_block(3)
            pe.wait_ge(acc_taken[0], (J_WO + 1) // 2)
            with fori(2) as i:
                for c in range(2):
                    J = Lin(J_WO + c, [(2, i)])
                    multiply(pe, J, lt_a, J.c % 2, fresh=B_Y if c == 0 else None)
            turn(pe, B_LN2, lambda c, t: h_nat[:, t, c * P:(c + 1) * P], 8, ready=(sg("h_ready"), D // NB))
            with fori(4) as g:
                for c in range(8):
                    J = Lin(J_MLP + c, [(8, g)])

                    def hook(r, c=c):
                        if r == 3 and 1 <= c <= 4:
                            wait(pe, sg("u_ready"), Lin(c, [(4, g)]))
                            turn(pe, Lin(B_U + 2 * (c - 1), [(8, g)]),
                                 lambda k, t: u_nat[:, (c - 1) % 2, t, k * P:(k + 1) * P], 2)
                        if r == 6 and c == 4:
                            wait(pe, lt_lo_ready, Lin(B_U + 8, [(8, g)]))
                    if c == 4:
                        wait(pe, lt_lo_ready, Lin(B_U + 6, [(8, g)]))
                    multiply(pe, J, lt_a if c < 4 else lt_b, J.c % 2, hook, fresh=B_LN2 if c == 0 else None)
            turn(pe, B_LNF, lambda c, t: res[:, t, c * P:(c + 1) * P], 8, ready=(sg("h_ready"), 2 * (D // NB)))
            pe.wait_ge(lt_lo_ready, B_LNF + 8)

            pe.wait_ge(sg("fox_loaded"), 48)
            small_mm(FOX_HEADS, 1).then_inc(sg("f_logit_ready"), 1)
            pe.wait_ge(sg("f_ones_ready"), 1)
            def fox_mix(g):
                one, two = Lin(1, [(1, g)]), Lin(0, [(2, g)])
                for kind in range(2):
                    for _ in range(4):
                        yield
                    wait(pe, sg("fq_ready"), two + kind + 1)
                    for b in range(2):
                        for c in range(2):
                            for t in range(NT):
                                i = 2 * b + c
                                last = TR(mx[:, b, (2 * c + t) * P:(2 * c + t + 1) * P],
                                          f_nat[:, kind, t, i * P:(i + 1) * P], ident[:, :])
                        last.then_inc(sg("fqk_turned"), 1)
                    yield
                    wait(pe, sg("fqk_copied"), Lin(2 * kind + 2, [(4, g)]))
                    if kind == 0:
                        for h in range(HG):
                            MM(mx[:, h, 0:P], f_lg[:, 0, h:h + 1].to_broadcast([P, P]), tri[:, :],
                               start=True, stop=True)
                            MM(mx[:, h, P:S], f_lg[:, 0, h:h + 1].to_broadcast([P, P]), f_ones[:, :],
                               start=True, stop=False)
                            last = MM(mx[:, h, P:S], f_lg[:, 1, h:h + 1].to_broadcast([P, P]), tri[:, :],
                                      start=False, stop=True)
                        last.then_inc(sg("f_cum_ready"), 1)
                        for _ in range(3):
                            yield
                        wait(pe, sg("f_bias_ready"), one)
                yield from unit_pe(pe, Lin(4, [(1, g)]), f_sc, f_pt, lambda j: f_T[:, j, :],
                                   lambda j: f_T[:, 4 + j, :],
                                   lambda j, t: f_nat[:, 2, t, j * HD:(j + 1) * HD])

            with fori(4) as g:
                mix = None
                for kind in range(4):
                    J = Lin(J_FOX + kind, [(4, g)])
                    if kind == 1:
                        mix = fox_mix(g)
                    multiply(pe, J, lt_a, J.c % 2, mix=mix)
                assert next(mix, "over") == "over"
                wait(pe, sg("fo_ready"), Lin(1, [(1, g)]))
                turn(pe, Lin(B_FO, [(2, g)]), lambda c, t: f_o[:, t, c, :], 2)
            with fori(2) as i:
                for c in range(2):
                    J = Lin(J_FOXO + c, [(2, i)])
                    multiply(pe, J, lt_b, J.c % 2, fresh=B_FO if c == 0 else None)
            turn(pe, B_LNG, lambda c, t: res[:, t, c * P:(c + 1) * P], 8, ready=(sg("ln_done"), 0))

            def turn_y(h, p, hh):
                wait(pe, sg("r_y_ready"), Lin(hh + 1, [(4, h), (2, p)]))
                turn(pe, Lin(B_RO + 2 * hh, [(8, h), (4, p)]),
                     lambda c, t: r_nat[:, 4 + hh, t, c * P:(c + 1) * P], 2)

            def ret_mix(h, p):
                pr = Lin(0, [(2, h), (1, p)])
                J = Lin(J_RET, [(16, h), (6, p)])
                for _ in range(7):
                    yield
                wait(pe, sg("rot_ready"), pr + 1)
                for b in range(4):
                    for c in range(2):
                        i = 2 * b + c
                        for t in range(NT):
                            last = TR(mx[:, b, (2 * c + t) * P:(2 * c + t + 1) * P],
                                      r_nat[:, i // 4, t, (i % 4) * P:(i % 4 + 1) * P], ident[:, :])
                    last.then_inc(sg("rqk_turned"), 1)
                    if b % 2:
                        yield
                wait(pe, sg("rqk_copied"), pr * 5 + 1)
                for c in range(4):
                    last = TR(mx[:, 0, c * P:(c + 1) * P], r_tmp[:, 0, c * P:(c + 1) * P], ident[:, :])
                last.then_inc(sg("rqk_turned"), 1)
                yield
                wait(pe, sg("rqk_copied"), pr * 5 + 5)
                for hh in range(2):
                    for t in range(NT):
                        for k in range(2):
                            i = 2 * hh + t
                            last = MM(mx[:, 1, i * P:(i + 1) * P], r_T[:, 4 + 2 * hh + k, t * P:(t + 1) * P],
                                      r_T[:, 2 * hh + k, t * P:(t + 1) * P], start=(k == 0), stop=(k == 1))
                last.then_inc(sg("r_inner"), 1)
                yield
                for hh in range(2):
                    wait(pe, acc_taken[1 - hh], (J + 2 + hh).half() + 1)
                    for k in range(2):
                        last = MM(mx[:, 2 + k, :], r_kd[:, hh, k * P:(k + 1) * P], r_nat[:, 2 + hh, 0, :],
                                  start=True, stop=True)
                    last.then_inc(sg("r_R_ready"), 1)
                    yield
                    if hh == 0:
                        wait(pe, sg("r_in_ready"), pr + 1)
                    else:
                        wait(pe, sg("r_o_taken"), pr * 2 + hh)
                    MM(mx[:, 0, :], r_in[:, 2 * hh, :], r_nat[:, 2 + hh, 0, :], start=True, stop=True)
                    MM(mx[:, 1, :], r_in[:, 2 * hh + 1, :], r_nat[:, 2 + hh, 1, :], start=True, stop=False)
                    wait(pe, sg("r_R_copied"), pr * 2 + hh + 1)
                    for k in range(2):
                        last = MM(mx[:, 1, :], r_qdT[:, 2 * hh + k, :], r_R[:, 2 * hh + k, :],
                                  start=False, stop=(k == 1))
                    last.then_inc(sg("r_o_ready"), 1)
                    for _ in range(5 if hh == 0 else 7):
                        yield
                turn_y(h, p, 0)
                yield

            with fori(2) as h:
                with fori(2) as p:
                    J = Lin(J_RET, [(16, h), (6, p)])
                    mix = None
                    for c in range(6):
                        if c == 2:
                            mix = ret_mix(h, p)
                        multiply(pe, J + c, lt_a, (J + c).c % 2, mix=mix, fresh=B_LNG if c == 0 else None)
                    turn_y(h, p, 1)
                for c in range(4):
                    J = Lin(J_RET + 12 + c, [(16, h)])
                    multiply(pe, J, lt_b, J.c % 2, fresh=Lin(B_RO, [(8, h)]) if c == 0 else None)

        @block.vector
        def _(dve):
            TT, TS, STT = nc.vector.tensor_tensor, nc.vector.tensor_scalar, nc.vector.scalar_tensor_tensor
            copy = nc.vector.tensor_copy

            def fori(n):
                return dve.Fori(0, n)

            def splits(J, mix=None):
                split_job(split_lo, dve, J, mix)

            rms_dve(dve, 0, h_nat)
            turn_lo(dve, B_LN1, whole(lt_a), 8)
            split_lo(dve, 0, 0, 4)
            splits(0)
            few_lo(dve, wsmall[:, :, :], 40, 0)
            dve.wait_ge(sg("prep_ready"), 1)
            copy(distb[0:NH, :], mx[0:NH, 1, 0:384])
            copy(cwt[:, :], mx[:, 2, 0:96])
            copy(pet[:, :, :], mx[:, 3, 0:64].rearrange("p (a b) -> p a b", a=2)).then_inc(sg("prep_taken"), 1)
            ch = Chain(dve, sg("dve_step"))

            def blocks_mix():
                yield
                yield
                dve.wait_ge(sg("prep_taken"), 1)
                for kv in range(2):
                    dve.wait_ge(sg("nsa_copied"), 2)
                    v = T[:, 8 + 2 * kv, :]
                    win = bass.AP(tensor=v.tensor, offset=v.offset,
                                  ap=[v.ap[0], [1, CMP_BLOCK], [S, NKV], [CMP_STRIDE, NCMP]])
                    pos = pet[:, kv, :]
                    pos = bass.AP(tensor=pos.tensor, offset=pos.offset, ap=[*pos.ap, [0, NKV], [0, NCMP]])
                    TT(blk.rearrange("p (j g n) -> p j g n", g=NKV, n=NCMP), win, pos, ALU.add) \
                        .then_inc(sg("blocks_ready"), 1)
                    yield
                    yield
                    dve.wait_ge(sg("blocks_hi"), kv + 1)
                    TT(cb[1][:, kv, :], blk, cb[0][:, kv, :].bitcast(F32), ALU.subtract) \
                        .then_inc(sg("blocks_lo"), 1)
                    dve.wait_ge(sg("blocks_lo"), kv + 1)
                yield
                dve.wait_ge(sg("gates_done"), 1)
                dve.wait_ge(sg("const_loaded"), 16 * N_CONST)
                ch.link(TT(gt[1], gt[1], heads_bcast(dt_row, NT), ALU.add))
                STT(gt[0], gt[1], -1.0, gt[1], ALU.mult, ALU.min).then_inc(sg("softplus_arg"), 1)
                yield
                yield
                dve.wait_ge(sg("softplus_done"), 1)
                ch.link(STT(gt[2], gt[1], 0.0, gt[0], ALU.max, ALU.add))
                ch.link(STT(tok[:, G_G], gt[2], -1.0, heads_bcast(a_row, NT), ALU.mult, ALU.mult))

            mix = blocks_mix()
            for J in range(1, 5):
                splits(J, mix)
            splits(J_CMP)
            splits(J_CMP + 1)

            def nsa_mix():
                dve.wait_ge(sg("bias_masked"), 2)
                last0 = CMP_BLOCK - 1
                copy(bm[:, :, SEG:SEG + NC0], bm[:, :, last0:last0 + CMP_STRIDE * (NC0 - 1) + 1:CMP_STRIDE])
                ch.link(copy(bm[:, :, SEG + NC0:SEGC],
                             bm[:, :, P + last0:P + last0 + CMP_STRIDE * (NCMP - 1) + 1:CMP_STRIDE]))
                for _ in range(3):
                    yield
                gate4 = gates[:, :, :].rearrange("p t (h b) -> p t h b", b=3)
                dve.wait_ge(sg("cmp_scores"), 1)
                n = NC0 + NCMP
                for g in range(NKV):
                    hs = slice(HG * g, HG * g + HG)
                    last = STT(scc[:, hs, :], mx[:, :, g * n:(g + 1) * n], ATT_SCALE, bm[:, hs, SEG:SEGC],
                               ALU.mult, ALU.add)
                ch.link(last)
                nc.vector.tensor_reduce(c_max[:, 0, :], scc[:, :, 0:NC0], AX.X, ALU.max, negate=True)
                nc.vector.tensor_reduce(c_max[:, 1, :], scc[:, :, NC0:NC0 + NCMP], AX.X, ALU.max,
                                        negate=True).then_inc(sg("cmp_rowmax"), 1)
                yield
                yield
                dve.wait_ge(sg("cmp_exp"), 1)
                TT(scc[:, :, 0:NC0], scc[:, :, 0:NC0], heads_bcast(mask0, NH), ALU.mult) \
                    .then_inc(sg("cmp_probs"), 1)
                dve.wait_ge(sg("cmp_probs"), 1)
                nc.vector.tensor_reduce(c_sum[:, 0, :], scc[:, :, 0:NC0], AX.X, ALU.add)
                ch.link(nc.vector.tensor_reduce(c_sum[:, 1, :], scc[:, :, NC0:NC0 + NCMP], AX.X, ALU.add))
                ch.link(TS(c_coef[:, 0], c_sum, 1e-30, None, ALU.max))
                ch.link(nc.vector.reciprocal(c_coef[:, 1], c_coef[:, 0]))
                ch.link(TT(c_coef[:, 2], c_coef[:, 1], gate4[:, :, :, 0], ALU.mult))
                yield
                for g in range(NKV):
                    hs = slice(HG * g, HG * g + HG)
                    yield
                    dve.wait_ge(sg("cmp_out_ready"), g + 1)
                    for t in range(NT):
                        for j in range(HG):
                            last = TS(o_nat[:, t, j, :], mx[:, t, j * HD:(j + 1) * HD],
                                      c_coef[:, 2, t, HG * g + j:HG * g + j + 1], None, ALU.mult)
                    last.then_inc(sg("cmp_out_taken"), 1)
                    dve.wait_ge(sg("cmp_out_taken"), g + 1)
                    yield
                    for b in range(2):
                        yield from unit_dve(dve, 2 * g + b, ch, sc, o_nat, bm[:, hs, 0:SEG],
                                            gate4[:, :, hs, 1 + b], False, 5)
                    turn_lo(dve, B_OA + 2 * g, part(lt_b, 4 * g), 2)
                    yield

            def gdn_mix(g):
                copy(cwg[:, :, :], cwt[:, :].rearrange("p (c h) -> p c h", h=NH)[:, :, g * HG:(g + 1) * HG])
                nc.vector.memset(g_ct[:, :, 0:3], 0.0).then_inc(sg("taps_ready"), 1)
                yield
                for kind in range(3):
                    wait(dve, sg("tap_done"), 3 * g + kind + 1)
                    for w in range(1, 4):
                        for i in range(4 * kind, 4 * kind + 4):
                            s = cwg[:, 3 * w + i // 4, i % 4:i % 4 + 1]
                            last = STT(g_cv[:, i, :], g_ct[:, i, w:w + S], s, g_cv[:, i, :], ALU.mult, ALU.add)
                        if w < 3:
                            ch.link(last)
                        if w == 2:
                            continue
                        if w == 3:
                            last.then_inc(sg("conv_done"), 1)
                        if g == 0 and kind == 1 and w == 1:
                            dve.wait_ge(sg("gsum_ready"), 1)
                            sums = mx[:, 2, 0:4 * NH].rearrange("p (a h) -> p a h", h=NH)
                            ch.link(copy(tok[:, G_CUM], sums[:, 0:2, :]))
                            TT(tok[:, G_KD], sums[:, 2:4, :], tok[:, G_CUM], ALU.subtract) \
                                .then_inc(sg("gcum_ready"), 1)
                        yield
                if g == 0:
                    dve.wait_ge(sg("gexp_done"), 1)
                    ch.link(TT(tok[:, G_BEG], tok[:, G_BETA], tok[:, G_E], ALU.mult))
                copy(tg[:, :, :, :].rearrange("p a t h -> p (a t) h"),
                     tok[:, :, :, :].rearrange("p a t h -> p (a t) h")[:, :, g * HG:(g + 1) * HG])
                wait(dve, sg("grn_copied"), 6 * g + 4)
                qk = g_rn[:, :, 0:8, :]
                ch.link(TT(g_sq[:, :, :, :], qk, qk, ALU.mult))
                yield
                ch.link(nc.vector.tensor_reduce(gss, g_sq[:, :, :, :], AX.X, ALU.add))
                TS(gss, gss, NORM_EPS, None, ALU.add).then_inc(sg("gss_ready"), 1)
                yield
                wait(dve, sg("grs_ready"), 2 * g + 1)
                ch.link(TS(grs[:, :, 0:4], grs[:, :, 0:4], HD ** -0.5, None, ALU.mult))
                ch.link(TT(qk, qk, bcast(grs, HD), ALU.mult))
                yield
                wait(dve, sg("grn_copied"), 6 * g + 6)
                qn, kn, vn = (g_rn[:, :, 4 * i:4 * i + 4, :] for i in range(3))
                TT(g_vb[:, :, :, :], vn, bcast(tg[:, G_BETA], HD), ALU.mult)
                TT(g_kbeg[:, :, :, :], kn, bcast(tg[:, G_BEG], HD), ALU.mult)
                yield
                TT(g_kdec[:, :, :, :], kn, bcast(tg[:, G_KD], HD), ALU.mult)
                TT(g_qg[:, :, :, :], qn, bcast(tg[:, G_E], HD), ALU.mult).then_inc(sg("g_normed"), 1)
                yield
                copy(g_X[:, :, :], heads_bcast(ident[:, :], HG * NT))
                yield
                copy(g_Y[:, :, :], heads_bcast(ident[:, :], HG * NT))
                yield
                wait(dve, sg("gb_ready"), g + 1)
                wait(dve, sg("gqk_turned"), 6 * g + 6)
                for i in range(HG * NT):
                    gb, s = mx[:, i // 4, (i % 4) * P:(i % 4 + 1) * P], tg[:, G_CUM, i % NT, i // NT:i // NT + 1]
                    TS(g_dec[:, i, :], gb, s, 0.0, ALU.subtract, ALU.max)
                    TS(g_qkT[:, i, :], gb, s, 0.0, ALU.subtract, ALU.min)
                    if i == 4:
                        yield
                copy(egl, mx[:, 0:2, CHUNK - 1::CHUNK].rearrange("p b (i n) -> p (b i) n", n=2)) \
                    .then_inc(sg("gdiff_ready"), 1)
                yield
                wait(dve, sg("gdecay_ready"), g + 1)
                TT(g_dec[:, :, :], g_dec[:, :, :], heads_bcast(g_mask[:, M_STRICT, :], HG * NT), ALU.mult)
                ch.link(TT(g_qkT[:, :, :], g_qkT[:, :, :], heads_bcast(g_mask[:, M_TRI, :], HG * NT), ALU.mult))
                yield
                wait(dve, sg("kk_ready"), g + 1)
                for i in range(HG * NT):
                    STT(g_A[:, i, :], mx[:, 2 + i // 4, (i % 4) * P:(i % 4 + 1) * P],
                        tg[:, G_BETA, i % NT, i // NT:i // NT + 1], g_dec[:, i, :], ALU.mult, ALU.mult)
                wait(dve, sg("qk_ready"), g + 1)
                ch.link(TT(g_qkT[:, :, :], mx[:, 0:2, :].rearrange("p b (c s) -> p (b c) s", s=P), g_qkT[:, :, :],
                           ALU.mult))
                for b in range(2):
                    TT(g_dec[:, 4 * b:4 * b + 4, :], g_A[:, 4 * b:4 * b + 4, :],
                       heads_bcast(g_mask[:, 0, :], 4), ALU.mult).then_inc(sg("inv_c"), 1)
                yield
                for l in range(LEVELS):
                    for b in range(2):
                        wait(dve, sg("inv_q"), 2 * (LEVELS * g + l) + b + 1)
                        hs = slice(4 * b, 4 * b + 4)
                        TT(g_Y[:, hs, :], g_Y[:, hs, :], mx[:, 2 + b, :].rearrange("p (c s) -> p c s", s=P),
                           ALU.subtract)
                        last = TT(g_X[:, hs, :], g_X[:, hs, :], mx[:, b, :].rearrange("p (c s) -> p c s", s=P),
                                  ALU.subtract)
                        if l + 1 < LEVELS:
                            last = TT(g_dec[:, hs, :], g_A[:, hs, :], heads_bcast(g_mask[:, l + 1, :], 4), ALU.mult)
                        last.then_inc(sg("inv_c"), 1)
                    yield
                yield
                wait(dve, sg("uw_copied"), g + 1)
                nc.vector.memset(g_S[:, :, :], 0.0).then_inc(sg("s_ready"), 1)
                U4 = g_U[:, :, :].rearrange("p (h t) d -> p h t d", t=NT)
                for n in range(4):
                    t, r = n // 2, slice(CHUNK * (n % 2), CHUNK * (n % 2) + CHUNK)
                    wait(dve, sg("ws_ready"), 4 * g + n + 1)
                    TT(g_V[r, :, :], U4[r, :, t, :], mx[r, 0, :].rearrange("p (h d) -> p h d", d=HD),
                       ALU.subtract).then_inc(sg("v_ready"), 1)
                    wait(dve, sg("su_ready"), 4 * g + n + 1)
                    wait(dve, sg("s_ready"), 5 * g + n + 1)
                    for h in range(HG):
                        last = STT(g_S[:, h, :], g_S[:, h, :], egl[:, h * NT + t, n % 2:n % 2 + 1],
                                   mx[:, 2, h * HD:(h + 1) * HD], ALU.mult, ALU.add)
                    last.then_inc(sg("s_ready"), 1)
                    if n % 2:
                        wait(dve, sg("in_ready"), 2 * g + n // 2 + 1)
                        wait(dve, sg("oq_copied"), 4 * g + n + 1)
                        ch.link(TT(g_o[:, t, :, :], mx[:, 3, :].rearrange("p (h d) -> p h d", d=HD),
                                   g_o[:, t, :, :], ALU.add))
                    yield
                sq = g_Y[:, :, :]
                o8 = g_o[:, :, :, :].rearrange("p t h d -> p (t h) d")
                s8 = gss.rearrange("p a b -> p (a b)")[:, 0:8]
                ch.link(TT(sq, o8, o8, ALU.mult))
                ch.link(nc.vector.tensor_reduce(s8, sq, AX.X, ALU.add))
                TS(s8, s8, 1.0 / HD, NORM_EPS, ALU.mult, ALU.add).then_inc(sg("gss_ready"), 1)
                yield
                wait(dve, sg("grs_ready"), 2 * g + 2)
                ch.link(TT(o8, o8, bcast(grs.rearrange("p a b -> p (a b)")[:, 0:8], HD), ALU.mult))
                yield
                ch.link(TT(o8, o8, heads_bcast(gnorm[:, :], 8), ALU.mult))
                TT(g_o[:, :, :, :].rearrange("p t h d -> p t (h d)"),
                   g_o[:, :, :, :].rearrange("p t h d -> p t (h d)"), g_z[:, :, :], ALU.mult) \
                    .then_inc(sg("go_ready"), 1)
                yield

            mix = nsa_mix()
            for kind in range(4):
                splits(J_GDN + kind, mix)
            assert next(mix, "over") == "over"
            for g in range(2):
                mix = gdn_mix(g)
                for kind in range(4):
                    splits((J_GDN + 4 if g == 0 else J_MERGE) + kind, mix)
                assert next(mix, "over") == "over"
                turn_lo(dve, B_OB + 2 * g, part(lt_b, NH + g * HG), 2)

            with fori(2) as i:
                for c in range(2):
                    splits(Lin(J_MERGE + 4 + c, [(2, i)]))
            dve.wait_ge(acc_taken[0], (J_PAB + 1) // 2)
            dve.wait_ge(acc_taken[1], J_PAB // 2)

            def merge_a(n):
                wait(dve, granules_done, (J_PAB + n) * GPJ + 4)
                for t in range(NT):
                    last = TT(y_nat[:, t, n * NB:(n + 1) * NB], acc[0][t][:, :], mg_a[:, n, t, :], ALU.mult)
                last.then_inc(sg("pab_taken"), 1)

            def merge_b(n):
                J = J_PAB + n
                wait(dve, granules_done, J * GPJ + GPJ)
                for t in range(NT):
                    last = TT(y_tmp[:, t, :], acc[1][t][:, :], mg_b[:, n, t, :], ALU.mult)
                last.then_inc(acc_taken[J % 2], 1)
                wait(dve, acc_taken[J % 2], J // 2 + 1)
                dve.wait_ge(sg("pab_taken"), n + 1)
                yy = y_nat[:, :, n * NB:(n + 1) * NB]
                TT(yy, yy, y_tmp[:, :, :], ALU.add).then_inc(sg("y_ready"), 1)

            for n in range(4):
                split_lo(dve, J_PAB + n, 4, 5)
                if n:
                    merge_b(n - 1)
                split_lo(dve, J_PAB + n, 5, 8)
                if n:
                    turn_lo(dve, B_Y + 2 * (n - 1), part(lt_a, 4 * (n - 1)), 2)
                split_lo(dve, J_PAB + n, 8, 9)
                merge_a(n)
                split_lo(dve, J_PAB + n, 9, 12)
            merge_b(3)
            dve.wait_ge(sg("y_ready"), 4)
            turn_lo(dve, B_Y + 6, part(lt_a, 12), 2)

            def add_job(J, col, done=None):
                J = lin(J)
                par = J.c % 2
                wait(dve, granules_done, J * GPJ + GPJ)
                cs = slice(col, col + NB) if isinstance(col, int) else bass.ds(col, NB)
                for t in range(NT):
                    last = TT(res[:, t, cs], res[:, t, cs], acc[par][t][:, :], ALU.add)
                last.then_inc(acc_taken[par], 1)
                if done:
                    wait(dve, acc_taken[par], J.half() + 1)
                    nc.vector.memset(y_tmp[:, 0, 0:1], 0.0).then_inc(sg(done), 1)

            dve.wait_ge(sg("x_again"), 16)
            with fori(2) as i:
                for c in range(2):
                    J = Lin(J_WO + c, [(2, i)])
                    splits(J)
                    add_job(J, i * (2 * NB) + c * NB, "wo_done")
            rms_dve(dve, 1, h_nat)
            turn_lo(dve, B_LN2, whole(lt_a), 8)
            with fori(4) as g:
                for c in range(5):
                    J = Lin(J_MLP + c, [(8, g)])
                    split_lo(dve, J, 4, 6)
                    if c:
                        turn_lo(dve, Lin(B_U + 2 * (c - 1), [(8, g)]), part(lt_b, 4 * (c - 1)), 2)
                    split_lo(dve, J, 6, 12)
                    if c < 4:
                        wait(dve, acc_taken[J.c % 2], J.half() + 1)
                        TT(u_nat[:, c % 2], relu[:, :, :], relu[:, :, :], ALU.mult).then_inc(sg("u_ready"), 1)
                    else:
                        add_job(J, 0, "down_done")
                for c in range(5, 8):
                    J = Lin(J_MLP + c, [(8, g)])
                    splits(J)
                    add_job(J, (c - 4) * NB, "down_done")
            rms_dve(dve, 2, res)
            turn_lo(dve, B_LNF, whole(lt_a), 8)
            few_lo(dve, f_w[:, :, :], FOX_HEADS, 1)

            dve.wait_ge(sg("f_logit_ready"), 1)
            ch.link(TT(f_t[0], small_ps[:, :, 0:FOX_HEADS], heads_bcast(bf_row, NT), ALU.add))
            STT(f_t[1], f_t[0], -1.0, f_t[0], ALU.mult, ALU.min).then_inc(sg("f_arg_ready"), 1)
            dve.wait_ge(sg("f_ln_done"), 1)
            ch.link(STT(f_logf, f_t[0], 0.0, f_t[1], ALU.min, ALU.subtract))
            def fox_mix(g, fc):
                one = Lin(1, [(1, g)])
                for kind in range(2):
                    J = Lin(J_FOX + kind, [(4, g)])
                    wait(dve, acc_taken[J.c % 2], J.half() + 1)
                    v = f_nat[:, kind].rearrange("p t (h d) -> p (t h) d", d=HD)
                    sq = f_sc[:, :, :].rearrange("p h k -> p (h k)")[:, 0:8 * HD].rearrange(
                        "p (h d) -> p h d", d=HD)
                    ss, rs = f_ss[:, kind, :], f_rs[:, kind, :]
                    fc.link(TT(sq, v, v, ALU.mult))
                    yield
                    if kind == 0:
                        copy(f_lg[:, :, :], f_logf[:, :, bass.ds(g * HG, HG)])
                    fc.link(nc.vector.tensor_reduce(ss, sq, AX.X, ALU.add))
                    TS(ss, ss, 1.0 / HD, NORM_EPS, ALU.mult, ALU.add).then_inc(sg("f_ms_ready"), 1)
                    yield
                    wait(dve, sg("f_rs_ready"), Lin(kind + 1, [(2, g)]))
                    fc.link(TT(v, v, bcast(rs, HD), ALU.mult))
                    yield
                    TT(v, v, heads_bcast(fgain[:, kind, :], 8), ALU.mult).then_inc(sg("fq_ready"), 1)
                    yield
                    yield
                    if kind == 0:
                        wait(dve, sg("f_cum_ready"), one)
                        STT(f_bias[:, :, 0:P], mx[:, :, 0:P], -1.0, heads_bcast(f_causal[:, 0:P], HG),
                            ALU.mult, ALU.add)
                        yield
                        STT(f_bias[:, :, P:SEG], mx[:, :, 0:S], -1.0, heads_bcast(f_causal[:, P:SEG], HG),
                            ALU.mult, ALU.add).then_inc(sg("f_bias_ready"), 1)
                        yield
                        yield
                yield from unit_dve(dve, Lin(4, [(1, g)]), fc, f_sc, f_o, f_bias[:, :, :], None, True)

            with fori(4) as g:
                fc = Chain(dve, sg("fox_dve_step"), Lin(0, [(K_FOX_DVE, g)]))
                mix = None
                for kind in range(4):
                    if kind == 1:
                        mix = fox_mix(g, fc)
                    splits(Lin(J_FOX + kind, [(4, g)]), mix)
                wait(dve, acc_taken[0], Lin((J_FOX + 3) // 2 + 1, [(2, g)]))
                fo = f_o[:, :, :, :].rearrange("p t h d -> p t (h d)")
                TT(fo, fo, f_nat[:, 3], ALU.mult).then_inc(sg("fo_ready"), 1)
                turn_lo(dve, Lin(B_FO, [(2, g)]), part(lt_b, g * HG), 2)
                fc.end(K_FOX_DVE)

            def block_stats(c):
                for t in range(NT):
                    last = nc.vector.bn_stats(lnst[:, t, c, :], res[:, t, c * NB:(c + 1) * NB])
                return last

            def layer_norm(k):
                for t in range(NT):
                    last = nc.vector.bn_aggr(lnmv[:, t, :], lnst[:, t, :, :].rearrange("p a b -> p (a b)"))
                ch.link(last)
                TS(lnr, lnmv[:, :, 1], LN_EPS, None, ALU.add).then_inc(sg("ln_ms_ready"), 1)
                dve.wait_ge(sg("ln_row_loaded"), 32 * (k + 1))
                for c in range(D // NB):
                    cs = slice(c * NB, c * NB + NB)
                    for t in range(NT):
                        last = STT(res[:, t, cs], res[:, t, cs], lnmv[:, t, 0:1], w_row[:, 0, cs],
                                   ALU.subtract, ALU.mult)
                    ch.link(last)
                    if c == 0:
                        dve.wait_ge(sg("ln_rs_ready"), k + 1)
                    for t in range(NT):
                        last = STT(res[:, t, cs], res[:, t, cs], rstd[:, t:t + 1], w_row[:, 1, cs],
                                   ALU.mult, ALU.add)
                    last.then_inc(sg("ln_done"), 1)

            for c in range(4):
                J = J_FOXO + c
                splits(J)
                wait(dve, granules_done, J * GPJ + GPJ)
                cs = slice(c * NB, c * NB + NB)
                for t in range(NT):
                    last = STT(res[:, t, cs], res[:, t, cs], ALPHA, acc[J % 2][t][:, :], ALU.mult, ALU.add)
                last.then_inc(acc_taken[J % 2], 1)
                dve.wait_ge(acc_taken[J % 2], J // 2 + 1)
                last = block_stats(c)
            ch.link(last)
            layer_norm(0)
            turn_lo(dve, B_LNG, whole(lt_a), 8)

            dve.wait_ge(sg("ln_done"), D // NB)
            ch.link(TS(res[:, :, :], res[:, :, :], ALPHA, None, ALU.mult))
            dve.wait_ge(sg("ret_loaded"), 32)
            def gate_y(J, pr, hh):
                wait(dve, acc_taken[1 - hh], (J + 4 + hh).half() + 1)
                wait(dve, sg("r_o_taken"), pr * 2 + hh + 1)
                TT(r_nat[:, 4 + hh], r_nat[:, 2 + hh], r_nat[:, 4 + hh], ALU.mult) \
                    .then_inc(sg("r_y_ready"), 1)

            def ret_mix(h, p, rc):
                pr = Lin(0, [(2, h), (1, p)])
                J = Lin(J_RET, [(16, h), (6, p)])
                for kind in range(2):
                    wait(dve, acc_taken[1 - kind], (J + kind).half() + 1)
                    v = r_nat[:, kind].rearrange("p t (h d) -> p t h d", h=2)
                    x1, x2 = v[:, :, :, 0:P], v[:, :, :, P:2 * P]
                    tmp = [r_tmp[:, i, :].rearrange("p (t h d) -> p t h d", t=NT, h=2) for i in range(4)]

                    def rope(i):
                        a = r_cs[:, i]
                        return bass.AP(tensor=a.tensor, offset=a.offset, ap=[a.ap[0], a.ap[1], [0, 2], a.ap[2]])
                    TT(tmp[0], x1, rope(0), ALU.mult)
                    TT(tmp[1], x2, rope(1), ALU.mult)
                    yield
                    TT(tmp[2], x1, rope(1), ALU.mult)
                    rc.link(TT(tmp[3], x2, rope(0), ALU.mult))
                    yield
                    TT(x1, tmp[0], tmp[1], ALU.subtract)
                    rc.link(TT(x2, tmp[2], tmp[3], ALU.add))
                    yield
                for hh in range(2):
                    cs = slice(hh * RET_QK, (hh + 1) * RET_QK)
                    hd = h * 4 + p * 2 + hh
                    TS(r_tmp[:, 0, cs], r_nat[:, 0, 1, cs], r_dec[:, 0, bass.ds(hd, 1)], None, ALU.mult)
                    last = TS(r_kd[:, hh, :], r_nat[:, 1, 0, cs], r_dec[:, 1, bass.ds(hd, 1)], None, ALU.mult)
                last.then_inc(sg("rot_ready"), 1)
                for _ in range(4):
                    yield
                wait(dve, sg("r_inner"), pr + 1)
                wait(dve, sg("r_D_loaded"), pr * 16 + 16)
                for hh in range(2):
                    last = TT(r_in[:, 2 * hh:2 * hh + 2, :],
                              mx[:, 1, 2 * hh * P:(2 * hh + 2) * P].rearrange("p (t c) -> p t c", c=P),
                              heads_bcast(r_D[:, hh, :], NT), ALU.mult)
                last.then_inc(sg("r_in_ready"), 1)
                yield
                yield
                for hh in range(2):
                    wait(dve, sg("r_o_ready"), pr * 2 + hh + 1)
                    for t in range(NT):
                        last = nc.vector.bn_stats(r_st[:, t, :], mx[:, t, :])
                    rc.link(last)
                    yield
                    nc.vector.memset(r_tmp[:, 1, 0:1], 0.0)
                    for t in range(NT):
                        last = nc.vector.bn_aggr(r_mv[:, t, :], r_st[:, t, :])
                    rc.link(last)
                    TS(r_rs, r_mv[:, :, 1], NORM_EPS, None, ALU.add).then_inc(sg("r_ms_ready"), 1)
                    yield
                    wait(dve, sg("r_rs_ready"), pr * 2 + hh + 1)
                    for t in range(NT):
                        last = TS(r_nat[:, 2 + hh, t, :], mx[:, t, :], r_mv[:, t, 0:1], r_rs[:, t:t + 1],
                                  ALU.subtract, ALU.mult)
                    last.then_inc(sg("r_o_taken"), 1)
                    for _ in range(4):
                        yield
                gate_y(J, pr, 0)
                yield
                turn_lo(dve, Lin(B_RO, [(8, h), (4, p)]), part(lt_b, p * 8), 2)
                yield

            with fori(2) as h:
                with fori(2) as p:
                    pr = Lin(0, [(2, h), (1, p)])
                    J = Lin(J_RET, [(16, h), (6, p)])
                    rc = Chain(dve, sg("ret_dve_step"), pr * K_RET_DVE)
                    mix = None
                    for c in range(6):
                        if c == 2:
                            mix = ret_mix(h, p, rc)
                        splits(J + c, mix)
                    gate_y(J, pr, 1)
                    turn_lo(dve, Lin(B_RO + 2, [(8, h), (4, p)]), part(lt_b, p * 8 + 4), 2)
                    rc.end(K_RET_DVE)
                for c in range(4):
                    J = Lin(J_RET + 12 + c, [(16, h)])
                    splits(J)
                    add_job(J, c * NB)
                    wait(dve, acc_taken[J.c % 2], J.half() + 1)
                    block_stats(c).then_inc(sg("stats_ready"), 1)
                    wait(dve, sg("stats_ready"), Lin(c + 1, [(4, h)]))
            dve.wait_ge(sg("stats_ready"), 8)
            layer_norm(1)


def t5_bucket(dist):
    n = np.maximum(dist, 0)
    exact = BUCKETS // 2
    nf = np.maximum(n, 1).astype(np.float32)
    large = exact + (np.log(nf / np.float32(exact)) / np.float32(math.log(MAX_DIST / exact))
                     * np.float32(BUCKETS - exact)).astype(np.int32)
    return np.where(n < exact, n, np.minimum(large, BUCKETS - 1))


def constants():
    f = np.float32
    dist = 2 * P - 1 - np.arange(384)
    onehot = (t5_bucket(dist)[None, :] == np.arange(BUCKETS)[:, None]).astype(f)
    c, s = np.arange(P)[:, None], np.arange(P)[None, :]
    masks = []
    for lv in range(LEVELS):
        b = 2 ** lv
        masks.append((c // (2 * b) == s // (2 * b)) & (c // b == s // b + 1))
    same = c // CHUNK == s // CHUNK
    masks += [same & (c > s), same & (c <= s), same, c <= s]
    masks = np.stack(masks).astype(f)
    key = np.concatenate([np.arange(P), np.arange(S) - P])[None, :]
    causal = np.where(key <= np.arange(P)[:, None], 0.0, NEG).astype(f)
    inv = f(10000.0) ** (-np.arange(0, RET_QK, 2, dtype=f) / f(RET_QK))
    ang = np.arange(S, dtype=f)[:, None] * inv[None, :]
    rope = np.stack([np.cos(ang), np.sin(ang)]).astype(f)
    lg = np.log1p(-np.exp2(-5.0 - np.arange(RET_HEADS, dtype=f)).astype(f)).astype(f)
    pos = np.arange(P, dtype=f)
    diff = pos[None, :] - pos[:, None]
    intra = np.where(diff[:, None, :] >= 0, np.exp(np.maximum(diff, 0)[:, None, :] * lg[None, :, None]), 0.0)
    decay = np.stack([np.exp((pos[:, None] + 1) * lg[None, :]), np.exp((P - 1 - pos[:, None]) * lg[None, :])])
    return {"c_onehot": onehot, "c_masks": masks, "c_causal": causal, "c_rope": rope,
            "c_intra": intra.astype(f), "c_decay": decay.astype(f)}


_INS = ["x", "rel_table", "ln1_w", "w_in", "cmp_pe_k", "cmp_pe_v", "cmp_w1_k", "cmp_w2_k", "cmp_w1_v",
        "cmp_w2_v", "conv_w", "a_log", "dt_bias", "gdn_norm_w", "w_pa", "w_pb", "w_o", "ln2_w", "w_up",
        "w_down", "ln_f_w", "fox_w_in_2", "fox_b_f_2", "fox_q_gain_2", "fox_k_gain_2", "fox_w_out_2",
        "ret_w_in_2", "ret_w_out_2", "ln_gain_2", "ln_bias_2"]


def kernel(**inputs):
    import concourse.bacc as bacc
    from concourse.bass_utils import run_bass_kernel_spmd

    nc = bacc.Bacc("TRN2", target_bir_lowering=False, num_devices=1)
    arrays, args = {}, []

    def add(name, a):
        arrays[name] = a
        args.append(nc.dram_tensor(name, a.shape, mybir.dt.from_np(a.dtype), kind="ExternalInput").ap())

    for name in _INS:
        a = np.ascontiguousarray(inputs[name])
        if a.ndim > 1 and a.shape[0] == 1:
            a = a[0]
        add("in_" + name, a)
    for name, a in constants().items():
        add(name, np.ascontiguousarray(a))
    args.append(nc.dram_tensor("out_x", (S, D), F32, kind="ExternalOutput").ap())
    build(nc, *args)
    r = run_bass_kernel_spmd(nc, [arrays], core_ids=[0])
    return r.results[0]["out_x"].reshape(1, S, D)
```
